# Optimizing a Trainium2 kernel written in Bass

```python
import jax, jax.numpy as jnp
from jax import lax
import numpy as np

D_MODEL = 1024
BATCH = 1
SEQ = 512
DEPTH = 2

MIX_WIDTH = D_MODEL
ATTN_WIDTH = MIX_WIDTH // 2
POOL_WIDTH = MIX_WIDTH - ATTN_WIDTH
HEAD_DIM = 64
N_HEADS = ATTN_WIDTH // HEAD_DIM
N_KV_HEADS = 2
GROUP = N_HEADS // N_KV_HEADS
KV_WIDTH = N_KV_HEADS * HEAD_DIM
WINDOW = 128
BLOCK = 128
ROT_DIM = HEAD_DIM // 4
ROPE_THETA = 500000.0
POOL_WINDOWS = (2, 4, 8, 16)
N_POOL_GROUPS = len(POOL_WINDOWS)
POOL_GROUP_WIDTH = POOL_WIDTH // N_POOL_GROUPS
IN_WIDTH = ATTN_WIDTH + 2 * KV_WIDTH + POOL_WIDTH
D_FF = ((int(np.ceil(8 * D_MODEL / 3)) + 255) // 256) * 256
N_MOD = 6
EPS = 1e-6
NEG_INF = -1e30


def rms_norm(x, g):
    xf = x.astype(jnp.float32)
    y = xf * lax.rsqrt(jnp.mean(xf * xf, axis=-1, keepdims=True) + EPS)
    return (y * g.astype(jnp.float32)).astype(x.dtype)

def partial_rotary(t, positions):
    inv_freq = ROPE_THETA ** (-jnp.arange(0, ROT_DIM, 2, dtype=jnp.float32) / ROT_DIM)
    ang = positions.astype(jnp.float32)[:, :, None] * inv_freq
    cos = jnp.cos(ang)[:, :, None, :]
    sin = jnp.sin(ang)[:, :, None, :]
    tf = t.astype(jnp.float32)
    half = ROT_DIM // 2
    t1, t2, rest = tf[..., :half], tf[..., half:ROT_DIM], tf[..., ROT_DIM:]
    rot = jnp.concatenate([t1 * cos - t2 * sin, t2 * cos + t1 * sin, rest], axis=-1)
    return rot.astype(t.dtype)

def sliding_window_attention_with_sinks(q, k, v, sinks):
    B, S = q.shape[0], q.shape[1]
    nb = S // BLOCK
    qb = q.reshape(B, nb, BLOCK, N_KV_HEADS, GROUP, HEAD_DIM)
    kb = k.reshape(B, nb, BLOCK, N_KV_HEADS, HEAD_DIM)
    vb = v.reshape(B, nb, BLOCK, N_KV_HEADS, HEAD_DIM)
    pad = ((0, 0), (1, 0), (0, 0), (0, 0), (0, 0))
    k_cat = jnp.concatenate([jnp.pad(kb, pad)[:, :-1], kb], axis=2)
    v_cat = jnp.concatenate([jnp.pad(vb, pad)[:, :-1], vb], axis=2)
    scores = jnp.einsum("bnqkgd,bnskd->bnkgqs", qb, k_cat).astype(jnp.float32)
    scores = scores * (HEAD_DIM ** -0.5)
    qi = jnp.arange(BLOCK)[:, None]
    kj = jnp.arange(2 * BLOCK)[None, :]
    diff = qi + BLOCK - kj
    blk = jnp.arange(nb)[:, None, None]
    key_abs = blk * BLOCK + kj[None] - BLOCK
    valid = (diff[None] >= 0) & (diff[None] < WINDOW) & (key_abs >= 0)
    scores = jnp.where(valid[None, :, None, None], scores, NEG_INF)
    sink = jnp.broadcast_to(
        sinks.astype(jnp.float32).reshape(1, 1, N_KV_HEADS, GROUP, 1, 1),
        scores.shape[:-1] + (1,))
    probs = jax.nn.softmax(jnp.concatenate([scores, sink], axis=-1), axis=-1)[..., :-1]
    out = jnp.einsum("bnkgqs,bnskd->bnqkgd", probs.astype(v.dtype), v_cat)
    return out.reshape(B, S, N_HEADS * HEAD_DIM)

def causal_pool_mixer(u, pool_w, pool_scale):
    S = u.shape[1]
    t = jnp.arange(S, dtype=jnp.float32)[None, :, None]
    outs = []
    for gi, w in enumerate(POOL_WINDOWS):
        ug = u[..., gi * POOL_GROUP_WIDTH:(gi + 1) * POOL_GROUP_WIDTH].astype(jnp.float32)
        cs = jnp.pad(jnp.cumsum(ug, axis=1), ((0, 0), (1, 0), (0, 0)))
        upper = cs[:, 1:]
        lower = jnp.pad(cs, ((0, 0), (w - 1, 0), (0, 0)))[:, :S]
        count = jnp.minimum(t + 1.0, float(w))
        pooled = (upper - lower) / count - ug
        outs.append(jnp.einsum("bsc,cd->bsd", pooled.astype(u.dtype), pool_w[gi]))
    return jnp.concatenate(outs, axis=-1) * pool_scale

def first_inputs(seed: int = 0) -> dict:
    key = jax.random.key(seed)
    ks = jax.random.split(key, 20)
    f32 = jnp.float32
    def nrm(k, shape, scale):
        return jax.random.normal(k, shape, f32) * scale
    x = jax.random.normal(ks[0], (BATCH, SEQ, D_MODEL), f32)
    c = jax.random.normal(ks[1], (BATCH, D_MODEL), f32)
    offsets = jax.random.randint(ks[2], (BATCH, 1), 0, 4096, dtype=jnp.int32)
    positions = (offsets + jnp.arange(SEQ, dtype=jnp.int32)[None, :]).astype(jnp.int32)
    return {
        "x": x,
        "c": c,
        "positions": positions,
        "ada_w": nrm(ks[3], (DEPTH, D_MODEL, N_MOD * D_MODEL), D_MODEL ** -0.5),
        "ada_b": nrm(ks[4], (DEPTH, N_MOD * D_MODEL), 0.02),
        "w_in": nrm(ks[5], (DEPTH, D_MODEL, IN_WIDTH), D_MODEL ** -0.5),
        "b_in": nrm(ks[6], (DEPTH, IN_WIDTH), 0.02),
        "sinks": nrm(ks[7], (DEPTH, N_HEADS), 1.0),
        "pool_w": nrm(ks[8], (DEPTH, N_POOL_GROUPS, POOL_GROUP_WIDTH, POOL_GROUP_WIDTH), POOL_GROUP_WIDTH ** -0.5),
        "pool_scale": 1.0 + nrm(ks[9], (DEPTH, POOL_WIDTH), 0.1),
        "w_out": nrm(ks[10], (DEPTH, MIX_WIDTH, D_MODEL), MIX_WIDTH ** -0.5),
        "w_gate": nrm(ks[11], (DEPTH, D_MODEL, D_FF), D_MODEL ** -0.5),
        "w_up": nrm(ks[12], (DEPTH, D_MODEL, D_FF), D_MODEL ** -0.5),
        "w_down": nrm(ks[13], (DEPTH, D_FF, D_MODEL), D_FF ** -0.5),
        "g_pre_mix": 1.0 + nrm(ks[14], (DEPTH, D_MODEL), 0.02),
        "g_post_mix": 1.0 + nrm(ks[15], (DEPTH, D_MODEL), 0.02),
        "g_pre_ffn": 1.0 + nrm(ks[16], (DEPTH, D_MODEL), 0.02),
        "g_post_ffn": 1.0 + nrm(ks[17], (DEPTH, D_MODEL), 0.02),
    }

def first_block(x, c, positions, ada_w, ada_b, w_in, b_in, sinks, pool_w, pool_scale,
              w_out, w_gate, w_up, w_down, g_pre_mix, g_post_mix, g_pre_ffn, g_post_ffn):
    B, S = x.shape[0], x.shape[1]
    c_act = jax.nn.silu(c)
    for l in range(DEPTH):
        mod = c_act @ ada_w[l] + ada_b[l]
        shift_m, scale_m, gate_m, shift_f, scale_f, gate_f = [
            m[:, None, :] for m in jnp.split(mod, N_MOD, axis=-1)]

        h = rms_norm(x, g_pre_mix[l]) * (1.0 + scale_m) + shift_m
        proj = h @ w_in[l] + b_in[l]
        q, k, v, u = jnp.split(
            proj, [ATTN_WIDTH, ATTN_WIDTH + KV_WIDTH, ATTN_WIDTH + 2 * KV_WIDTH], axis=-1)
        q = partial_rotary(q.reshape(B, S, N_HEADS, HEAD_DIM), positions)
        k = partial_rotary(k.reshape(B, S, N_KV_HEADS, HEAD_DIM), positions)
        v = v.reshape(B, S, N_KV_HEADS, HEAD_DIM)
        attn_out = sliding_window_attention_with_sinks(q, k, v, sinks[l])
        pool_out = causal_pool_mixer(u, pool_w[l], pool_scale[l])
        mix = jnp.concatenate([attn_out, pool_out], axis=-1) @ w_out[l]
        x = x + gate_m * rms_norm(mix, g_post_mix[l])

        h = rms_norm(x, g_pre_ffn[l]) * (1.0 + scale_f) + shift_f
        f = (jax.nn.silu(h @ w_gate[l]) * (h @ w_up[l])) @ w_down[l]
        x = x + gate_f * rms_norm(f, g_post_ffn[l])
    return x


DEPTH_2 = 1

HG_HEADS = 8
HG_DK = 128
HG_DV = D_MODEL // HG_HEADS
HG_DIM_K = HG_HEADS * HG_DK
HG_DIM_V = HG_HEADS * HG_DV
RET_HEADS = 4
RET_DK = 256
RET_DV = 256
RET_DIM_K = RET_HEADS * RET_DK
RET_DIM_V = RET_HEADS * RET_DV
ROPE_BASE = 10000.0
MAX_POS_OFFSET = 4096
CHUNK = 64
PROJ_WIDTHS = (HG_DIM_K, HG_DIM_K, HG_DIM_K, HG_DIM_V, HG_DIM_V, RET_DIM_K, RET_DIM_K, RET_DIM_V, RET_DIM_V, D_MODEL, D_MODEL)
PROJ_DIM = HG_DIM_K * 3 + HG_DIM_V * 2 + RET_DIM_K * 2 + RET_DIM_V * 2 + D_MODEL * 2
N_GROUPS = 4
EXPERTS_PER_GROUP = 8
N_EXPERTS = N_GROUPS * EXPERTS_PER_GROUP
TOP_K = 2
D_EXPERT = 512
MOE_BLOCK = 128
DEEPNORM_ALPHA = (2 * DEPTH_2) ** 0.25
DEEPNORM_BETA = (8 * DEPTH_2) ** -0.25
LN_EPS = 1e-5
RMS_EPS = 1e-6


def _layer_norm(x, g, b):
    xf = x.astype(jnp.float32)
    mu = jnp.mean(xf, -1, keepdims=True)
    var = jnp.mean(jnp.square(xf - mu), -1, keepdims=True)
    return ((xf - mu) * lax.rsqrt(var + LN_EPS) * g + b).astype(x.dtype)

def _rms_norm_heads(o, g):
    of = o.astype(jnp.float32)
    of = of * lax.rsqrt(jnp.mean(of * of, -1, keepdims=True) + RMS_EPS)
    return of.reshape(*o.shape[:-2], -1) * g

def _to_chunks(t):
    b, l, h, d = t.shape
    return t.reshape(b, l // CHUNK, CHUNK, h, d).transpose(1, 0, 3, 2, 4)

def _from_chunks(t):
    n, b, h, c, d = t.shape
    return t.transpose(1, 0, 3, 2, 4).reshape(b, n * c, h, d)

def _hgrn2_scan(q, k, v, log_f):
    dt = v.dtype
    qc, kc, vc, lfc = (_to_chunks(t.astype(jnp.float32)) for t in (q, k, v, log_f))
    b, h, dk, dv = qc.shape[1], qc.shape[2], qc.shape[-1], vc.shape[-1]
    causal = jnp.tril(jnp.ones((CHUNK, CHUNK), bool))[:, :, None]

    def step(S, inp):
        qb, kb, vb, lf = inp
        G = jnp.cumsum(lf, axis=2)
        g_last = G[:, :, -1:, :]
        decay = jnp.exp(jnp.where(causal, G[:, :, :, None, :] - G[:, :, None, :, :], -jnp.inf))
        attn = jnp.einsum('bhtd,bhsd,bhtsd->bhts', qb, kb, decay)
        o = jnp.einsum('bhts,bhsv->bhtv', attn, vb) + jnp.einsum('bhtd,bhdv->bhtv', qb * jnp.exp(G), S)
        S = jnp.exp(g_last[:, :, 0, :, None]) * S + jnp.einsum('bhsd,bhsv->bhdv', kb * jnp.exp(g_last - G), vb)
        return S, o

    S0 = jnp.zeros((b, h, dk, dv), jnp.float32)
    _, o = lax.scan(step, S0, (qc, kc, vc, lfc))
    return _from_chunks(o).astype(dt)

def _retention_scan(q, k, v, log_gamma):
    dt = v.dtype
    qc, kc, vc = (_to_chunks(t.astype(jnp.float32)) for t in (q, k, v))
    b, h, dk, dv = qc.shape[1], qc.shape[2], qc.shape[-1], vc.shape[-1]
    idx = jnp.arange(CHUNK, dtype=jnp.float32)
    rel = idx[:, None] - idx[None, :]
    lg = log_gamma[:, None]
    decay = jnp.where(rel >= 0, jnp.exp(jnp.maximum(rel, 0.0) * log_gamma[:, None, None]), 0.0)
    cross = jnp.exp((idx + 1.0) * lg)[:, :, None]
    k_dec = jnp.exp((CHUNK - 1.0 - idx) * lg)[:, :, None]
    chunk_dec = jnp.exp(CHUNK * log_gamma)[:, None, None]

    def step(R, inp):
        qb, kb, vb = inp
        inner = jnp.einsum('bhtd,bhsd->bhts', qb, kb) * decay
        o = jnp.einsum('bhts,bhsv->bhtv', inner, vb) + cross * jnp.einsum('bhtd,bhdv->bhtv', qb, R)
        R = chunk_dec * R + jnp.einsum('bhsd,bhsv->bhdv', kb * k_dec, vb)
        return R, o

    R0 = jnp.zeros((b, h, dk, dv), jnp.float32)
    _, o = lax.scan(step, R0, (qc, kc, vc))
    return _from_chunks(o).astype(dt)

def _rotary(t, positions):
    d = t.shape[-1]
    inv = 1.0 / (ROPE_BASE ** jnp.linspace(0.0, 1.0, d // 2, dtype=jnp.float32))
    ang = positions.astype(jnp.float32)[..., None] * inv
    sin, cos = jnp.sin(ang)[:, :, None, :], jnp.cos(ang)[:, :, None, :]
    tf = t.astype(jnp.float32)
    t1, t2 = tf[..., 0::2], tf[..., 1::2]
    out = jnp.stack([t1 * cos - t2 * sin, t1 * sin + t2 * cos], axis=-1).reshape(t.shape)
    return out.astype(t.dtype)

def _token_mixer(x, positions, w_in, lb, hg_norm_g, ret_norm_g, w_branch_hg, w_branch_ret, w_out):
    b, l, _ = x.shape
    proj = x @ w_in
    hq, hf_fwd, hf_bwd, hi, hgate, rq, rk, rv, rgate, ga, gb = jnp.split(proj, np.cumsum(PROJ_WIDTHS)[:-1].tolist(), axis=-1)
    heads = lambda t, n: t.reshape(b, l, n, -1)
    flip = lambda t: jnp.flip(t, axis=1)

    q_h = heads(jax.nn.silu(hq), HG_HEADS)
    v_h = heads(hi, HG_HEADS)

    def hgrn_direction(f_logits, qd, vd):
        f = lb + (1.0 - lb) * jax.nn.sigmoid(f_logits.astype(jnp.float32))
        return _hgrn2_scan(qd, heads(1.0 - f, HG_HEADS), vd, heads(jnp.log(f), HG_HEADS))

    o_hg = hgrn_direction(hf_fwd, q_h, v_h) + flip(hgrn_direction(flip(hf_bwd), flip(q_h), flip(v_h)))
    o_hg = _rms_norm_heads(o_hg, hg_norm_g) * jax.nn.silu(hgate.astype(jnp.float32))
    y_hg = o_hg.astype(x.dtype) @ w_branch_hg

    rq_h = _rotary(heads(rq, RET_HEADS), positions)
    rk_h = _rotary(heads(rk, RET_HEADS), positions) * RET_DK ** -0.5
    rv_h = heads(rv, RET_HEADS)
    log_gamma = jnp.log(1.0 - 2.0 ** (-5.0 - jnp.arange(RET_HEADS, dtype=jnp.float32)))
    o_ret = _retention_scan(rq_h, rk_h, rv_h, log_gamma) + flip(_retention_scan(flip(rq_h), flip(rk_h), flip(rv_h), log_gamma))
    o_ret = _rms_norm_heads(o_ret, ret_norm_g) * jax.nn.silu(rgate.astype(jnp.float32))
    y_ret = o_ret.astype(x.dtype) @ w_branch_ret

    merged = jax.nn.sigmoid(ga) * y_hg + jax.nn.sigmoid(gb) * y_ret
    return merged @ w_out

def _hier_moe(x, w_group, b_group, w_router, b_router, w1, w3, w2):
    t, d = x.shape
    g_logits = (x @ w_group).astype(jnp.float32) + b_group
    grp = jnp.argmax(g_logits, -1)
    p_grp = jnp.take_along_axis(jax.nn.softmax(g_logits, -1), grp[:, None], -1)
    e_logits = ((x @ w_router).astype(jnp.float32) + b_router).reshape(t, N_GROUPS, EXPERTS_PER_GROUP)
    e_logits = jnp.take_along_axis(e_logits, grp[:, None, None], 1)[:, 0]
    top_p, top_i = lax.top_k(jax.nn.softmax(e_logits, -1), TOP_K)
    top_p = top_p / jnp.sum(top_p, -1, keepdims=True)
    wts = (p_grp * top_p).reshape(-1)
    eid = (grp[:, None] * EXPERTS_PER_GROUP + top_i).reshape(-1)
    n_assign = t * TOP_K
    tok = jnp.arange(n_assign, dtype=jnp.int32) // TOP_K

    order = jnp.argsort(eid)
    e_sorted = eid[order]
    counts = jnp.zeros((N_EXPERTS,), jnp.int32).at[eid].add(1)
    start = jnp.cumsum(counts) - counts
    padded = (counts + MOE_BLOCK - 1) // MOE_BLOCK * MOE_BLOCK
    pend = jnp.cumsum(padded)
    pstart = pend - padded
    dest = pstart[e_sorted] + (jnp.arange(n_assign, dtype=jnp.int32) - start[e_sorted])
    n_blocks = -(-n_assign // MOE_BLOCK) + N_EXPERTS
    rows = jnp.full((n_blocks * MOE_BLOCK,), t, jnp.int32).at[dest].set(tok[order])
    row_w = jnp.zeros((n_blocks * MOE_BLOCK,), jnp.float32).at[dest].set(wts[order])
    block_expert = jnp.clip(jnp.searchsorted(pend, jnp.arange(n_blocks, dtype=jnp.int32) * MOE_BLOCK, side='right'), 0, N_EXPERTS - 1)
    x_pad = jnp.concatenate([x, jnp.zeros((1, d), x.dtype)], 0)
    xb = x_pad[rows].reshape(n_blocks, MOE_BLOCK, d)

    def expert_block(args):
        xs, e = args
        return (jax.nn.silu(xs @ w1[e]) * (xs @ w3[e])) @ w2[e]

    yb = lax.map(expert_block, (xb, block_expert))
    y = yb.reshape(-1, d) * row_w[:, None].astype(x.dtype)
    return jax.ops.segment_sum(y, rows, num_segments=t + 1)[:t]

def second_inputs(seed: int = 0) -> dict:
    key = jax.random.key(seed)
    ks = jax.random.split(key, 20)
    nrm = lambda k, shape, s: jax.random.normal(k, shape, jnp.float32) * s
    beta = DEEPNORM_BETA
    x = nrm(ks[0], (BATCH, SEQ, D_MODEL), 1.0)
    positions = jax.random.randint(ks[1], (BATCH, 1), 0, MAX_POS_OFFSET, jnp.int32) + jnp.arange(SEQ, dtype=jnp.int32)[None, :]
    col_scales = (1.0, 1.0, 1.0, beta, 1.0, 1.0, 1.0, beta, 1.0, 1.0, 1.0)
    col_scale = jnp.concatenate([jnp.full((w,), s, jnp.float32) for w, s in zip(PROJ_WIDTHS, col_scales)])
    w_in = nrm(ks[2], (DEPTH_2, D_MODEL, PROJ_DIM), D_MODEL ** -0.5) * col_scale
    hg_lb_logits = nrm(ks[3], (DEPTH_2 + 1, HG_DIM_K), 0.5)
    hg_norm_g = 1.0 + nrm(ks[4], (DEPTH_2, HG_DIM_V), 0.02)
    ret_norm_g = 1.0 + nrm(ks[5], (DEPTH_2, RET_DIM_V), 0.02)
    w_branch_hg = nrm(ks[6], (DEPTH_2, HG_DIM_V, D_MODEL), HG_DIM_V ** -0.5 * beta)
    w_branch_ret = nrm(ks[7], (DEPTH_2, RET_DIM_V, D_MODEL), RET_DIM_V ** -0.5 * beta)
    w_out = nrm(ks[8], (DEPTH_2, D_MODEL, D_MODEL), D_MODEL ** -0.5 * beta)
    ln1_g = 1.0 + nrm(ks[9], (DEPTH_2, D_MODEL), 0.02)
    ln1_b = nrm(ks[10], (DEPTH_2, D_MODEL), 0.02)
    w_group = nrm(ks[11], (DEPTH_2, D_MODEL, N_GROUPS), D_MODEL ** -0.5)
    b_group = nrm(ks[12], (DEPTH_2, N_GROUPS), 0.01)
    w_router = nrm(ks[13], (DEPTH_2, D_MODEL, N_EXPERTS), D_MODEL ** -0.5)
    b_router = nrm(ks[14], (DEPTH_2, N_EXPERTS), 0.01)
    w1 = nrm(ks[15], (DEPTH_2, N_EXPERTS, D_MODEL, D_EXPERT), D_MODEL ** -0.5)
    w3 = nrm(ks[16], (DEPTH_2, N_EXPERTS, D_MODEL, D_EXPERT), D_MODEL ** -0.5)
    w2 = nrm(ks[17], (DEPTH_2, N_EXPERTS, D_EXPERT, D_MODEL), D_EXPERT ** -0.5 * beta)
    ln2_g = 1.0 + nrm(ks[18], (DEPTH_2, D_MODEL), 0.02)
    ln2_b = nrm(ks[19], (DEPTH_2, D_MODEL), 0.02)
    return {'x': x, 'positions': positions, 'w_in': w_in, 'hg_lb_logits': hg_lb_logits,
            'hg_norm_g': hg_norm_g, 'ret_norm_g': ret_norm_g, 'w_branch_hg': w_branch_hg,
            'w_branch_ret': w_branch_ret, 'w_out': w_out, 'ln1_g': ln1_g, 'ln1_b': ln1_b,
            'w_group': w_group, 'b_group': b_group, 'w_router': w_router, 'b_router': b_router,
            'w1': w1, 'w3': w3, 'w2': w2, 'ln2_g': ln2_g, 'ln2_b': ln2_b}

def second_block(x, positions, w_in, hg_lb_logits, hg_norm_g, ret_norm_g, w_branch_hg, w_branch_ret,
              w_out, ln1_g, ln1_b, w_group, b_group, w_router, b_router, w1, w3, w2, ln2_g, ln2_b):
    lb_cum = jnp.cumsum(jax.nn.softmax(hg_lb_logits.astype(jnp.float32), axis=0), axis=0)
    for layer in range(DEPTH_2):
        lb = lb_cum[layer + 1] - lb_cum[0]
        mix = _token_mixer(x, positions, w_in[layer], lb, hg_norm_g[layer], ret_norm_g[layer],
                           w_branch_hg[layer], w_branch_ret[layer], w_out[layer])
        x = _layer_norm(DEEPNORM_ALPHA * x + mix, ln1_g[layer], ln1_b[layer])
        moe = _hier_moe(x.reshape(-1, D_MODEL), w_group[layer], b_group[layer], w_router[layer],
                        b_router[layer], w1[layer], w3[layer], w2[layer]).reshape(x.shape)
        x = _layer_norm(DEEPNORM_ALPHA * x + moe, ln2_g[layer], ln2_b[layer])
    return x


_first_inputs = second_inputs


def second_inputs(seed=0):
    import zlib

    import numpy as np

    out = dict(_first_inputs(seed))
    spreads = {}
    factors = {'hg_lb_logits': 7.239,
     'hg_norm_g': 8.0,
     'ret_norm_g': 8.0,
     'b_group': 8.0,
     'b_router': 8.0,
     'ln2_g': 2.912,
     'ln2_b': 2.842}
    for name, (base, spread) in spreads.items():
        noise = np.random.default_rng([zlib.crc32(name.encode()), seed]).standard_normal(out[name].shape)
        drawn = base * np.exp(spread * noise) if base else spread * noise
        out[name] = __import__('jax').numpy.asarray(drawn.astype(out[name].dtype))
    for name, factor in factors.items():
        out[name] = (out[name] * factor).astype(out[name].dtype)
    return out


_narrow_inputs = second_inputs


def second_inputs(seed=0):

    out = dict(_narrow_inputs(seed))
    wider = {'hg_norm_g': 4.96, 'ret_norm_g': 3.95, 'ln2_g': 3.27, 'ln2_b': 3.28}
    for name, times in wider.items():
        mean = out[name].mean()
        out[name] = (mean + times * (out[name] - mean)).astype(out[name].dtype)
    return out


def setup_inputs(seed=0):
    out = dict(first_inputs(seed))
    for name, value in second_inputs(seed + 1).items():
        if name != "x":
            out[name + "_2"] = value
    return out


def reference(
    x, c, positions, ada_w, ada_b, w_in, b_in, sinks, pool_w, pool_scale, w_out, w_gate, w_up,
    w_down, g_pre_mix, g_post_mix, g_pre_ffn, g_post_ffn, positions_2, w_in_2, hg_lb_logits_2,
    hg_norm_g_2, ret_norm_g_2, w_branch_hg_2, w_branch_ret_2, w_out_2, ln1_g_2, ln1_b_2,
    w_group_2, b_group_2, w_router_2, b_router_2, w1_2, w3_2, w2_2, ln2_g_2, ln2_b_2,
):
    x = first_block(
        x, c, positions, ada_w, ada_b, w_in, b_in, sinks, pool_w, pool_scale, w_out, w_gate,
        w_up, w_down, g_pre_mix, g_post_mix, g_pre_ffn, g_post_ffn,
    )
    return second_block(
        x, positions_2, w_in_2, hg_lb_logits_2, hg_norm_g_2, ret_norm_g_2, w_branch_hg_2,
        w_branch_ret_2, w_out_2, ln1_g_2, ln1_b_2, w_group_2, b_group_2, w_router_2, b_router_2,
        w1_2, w3_2, w2_2, ln2_g_2, ln2_b_2,
    )


_drawn_inputs = setup_inputs


def setup_inputs(seed=0):
    import zlib

    import numpy as np

    out = dict(_drawn_inputs(seed))
    spreads = {}
    factors = {'sinks': 2.987, 'b_group_2': 4.411, 'b_router_2': 2.768}
    for name, (base, spread) in spreads.items():
        noise = np.random.default_rng([zlib.crc32(name.encode()), seed]).standard_normal(out[name].shape)
        drawn = base * np.exp(spread * noise) if base else spread * noise
        out[name] = __import__('jax').numpy.asarray(drawn.astype(out[name].dtype))
    for name, factor in factors.items():
        out[name] = (out[name] * factor).astype(out[name].dtype)
    return out
```

```python
from contextlib import ExitStack

import concourse.bass as bass
import concourse.mybir as mybir
import numpy as np
from concourse.alu_op_type import AluOpType as ALU

F32 = mybir.dt.float32
I32 = mybir.dt.int32
ACT = mybir.ActivationFunctionType
AXX = mybir.AxisListType.X

P = 128
D = 1024
KD = D // P
S = 512
T = S // P
LAYERS = 2
HEADS, HD, KVH, GROUP = 8, 64, 2, 4
QKV = HEADS * HD + 2 * KVH * HD
POOL_G = 4
IN_W = QKV + 512
FF = 2816
KF = FF // P
ROT_HALF = 8
EPS = 1e-6
NEG = -1e30
POOL_WINDOWS = (2, 4, 8, 16)

RING = 4
SLOT = 4096
MOD_UNITS = 12
IN_UNITS = 4
IN_COLS = IN_W // IN_UNITS
OUT_UNITS = 2
GU_UNITS = 11
DOWN_UNITS = ((0, 3), (3, 3), (6, 3), (9, 3), (12, 3), (15, 3), (18, 4))
LAYER_UNITS = MOD_UNITS + IN_UNITS + OUT_UNITS + GU_UNITS + len(DOWN_UNITS)
U_MOD_M, U_IN = 0, 6
U_MOD_F = U_IN + IN_UNITS
U_OUT = U_MOD_F + 6
U_GU = U_OUT + OUT_UNITS
U_DOWN = U_GU + GU_UNITS

HG = 8
RH, RDK = 4, 256
LEVELS = 7
ALPHA = 2.0 ** 0.25
RMS_EPS, LN_EPS = 1e-6, 1e-5
COL_Q, COL_F, COL_FB, COL_V, COL_G = 0, 1024, 2048, 3072, 4096
COL_RQ, COL_RK, COL_RV, COL_RG, COL_GA, COL_GB = 5120, 6144, 7168, 8192, 9216, 10240
GROUPS, PER_GROUP, EXPERTS, DE = 4, 8, 32, 512
NL = GROUPS + EXPERTS
TOKENS_PER_BLOCK = P
MAX_BLOCKS = 40
XT_TURN = 2 * LAYERS

TURN = {"dve_layer": 94, "act_layer": 68, "dve_hg": 104, "act_hg": 18, "dve_moe": 18}

TWO_PI = 2.0 * np.pi
C1 = 6.28125
C2 = float(np.float32(np.round((TWO_PI - C1) * 2.0**20) / 2.0**20))
C3 = float(np.float32(TWO_PI - C1 - C2))
ROUND = 1.5 * 2.0**23


DOWN_CREDIT, POST_CREDIT = len(DOWN_UNITS) - 1, 16


def unit_done(u):
    if u < 0:
        name, per_layer, count = unit_done(u + LAYER_UNITS)
        return name, per_layer, count - per_layer
    if U_MOD_M <= u < U_IN:
        return "mod_mm", MOD_UNITS, u + 1
    if U_IN <= u < U_MOD_F:
        return "proj_mm", 16, 4 * (u - U_IN + 1)
    if U_MOD_F <= u < U_OUT:
        return "mod_mm", MOD_UNITS, 6 + u - U_MOD_F + 1
    if U_OUT <= u < U_GU:
        return "post_mm", 16, POST_CREDIT + 4 * (u - U_OUT + 1)
    if U_GU <= u < U_DOWN:
        return "gu_mm", GU_UNITS, u - U_GU + 1
    if u < LAYER_UNITS - 1:
        return "down_mm", len(DOWN_UNITS) - 1, DOWN_CREDIT + u - U_DOWN + 1
    return "post_mm", 16, POST_CREDIT + 16


class Chain:

    def __init__(self, eng, sem):
        self.eng, self.sem, self.base, self.n, self.turn = eng, sem, 0, 0, 0

    def link(self, ins):
        ins.then_inc(self.sem, 1)
        self.n += 1
        return ins

    def settle(self):
        self.eng.wait_ge(self.sem, self.turn + (self.base + self.n))

    def enter(self, i, name):
        self.base += self.n
        self.n, self.turn, self.name = 0, i * TURN[name], name

    def leave(self, turns):
        assert self.n == TURN[self.name], f"TURN[{self.name!r}] is {self.n}"
        self.base += turns * self.n
        self.n, self.turn = 0, 0


def shape_constants():
    c = {}
    c["ident"] = np.eye(P, dtype=np.float32)
    q, k = np.arange(P)[:, None], np.arange(P)[None, :]
    prev = np.where(k > q, 0.0, NEG)
    cur = np.where(k <= q, 0.0, NEG)
    c["window"] = np.concatenate([prev, cur], 1).astype(np.float32)
    pool = np.zeros((P, POOL_G, 3, P), np.float32)
    s, t = np.arange(P)[:, None], np.arange(P)[None, :]
    for g, w in enumerate(POOL_WINDOWS):
        here = (s <= t) & (s > t - w)
        pool[:, g, 0] = here / np.float32(w) - (s == t)
        pool[:, g, 1] = (s - P > t - w) / np.float32(w)
        pool[:, g, 2] = here / np.minimum(t + 1.0, w).astype(np.float32) - (s == t)
    c["pool"] = pool.reshape(P, -1)
    inv = (np.float32(500000.0) ** (-np.arange(0, 16, 2, dtype=np.float32) / 16)).astype(np.float32)
    c["inv1"] = np.broadcast_to(inv, (P, ROT_HALF)).copy()
    a, b = np.arange(P)[:, None], np.arange(P)[None, :]
    masks = [a == b] + [(a >> l == b >> l) & (a >> (l - 1) != b >> (l - 1)) for l in range(1, LEVELS)]
    c["masks"] = np.stack(masks, 1).astype(np.float32).reshape(P, -1)
    c["restart"] = np.tile((np.arange(S) % P != 0).astype(np.float32), (P, 1))
    half = RDK // 2
    inv = 1.0 / (np.float32(10000.0) ** np.linspace(0.0, 1.0, half, dtype=np.float32))
    c["inv2"] = inv.astype(np.float32).reshape(P, 1)
    gamma = 1.0 - 2.0 ** (-5.0 - np.arange(RH, dtype=np.float64))
    dist = np.abs(np.arange(S + 3 * P)[None, :] - 3 * P - np.arange(P)[:, None])
    strip = gamma[:, None, None] ** dist[None] * np.where(dist == 0, 2.0, 1.0) * RDK ** -0.5
    c["iota"] = np.tile(np.arange(P, dtype=np.float32), (P, 1))
    c["before"] = (np.arange(P)[:, None] < np.arange(P)[None, :]).astype(np.float32)
    c["decay"] = strip.astype(np.float32)
    return c


def build(nc, A, K, out, stop=None):
    with ExitStack() as ctx:
        sems = {}

        def sem(name):
            if name not in sems:
                sems[name] = ctx.enter_context(nc.semaphore(name))
            return sems[name]

        arena_size = 53000
        arena = ctx.enter_context(nc.sbuf_tensor("arena", [P, arena_size], F32))
        top = [0]

        def take(*shape):
            n = int(np.prod(shape))
            a = arena[:, top[0]:top[0] + n]
            top[0] += n
            assert top[0] <= arena_size, top[0]
            if len(shape) > 1:
                names = "abcd"[:len(shape)]
                a = a.rearrange(f"p ({' '.join(names)}) -> p {' '.join(names)}",
                                **{n_: s_ for n_, s_ in zip(names[1:], shape[1:])})
            return a

        psum = ctx.enter_context(nc.psum_tensor("psum", [P, 8, 512], F32))

        def bank(b):
            return psum[:, b, :]

        ring = [take(SLOT) for _ in range(RING)]
        x = take(T, D)
        hT = take(KD, S)
        mixT = hT
        ident = take(P)
        eps = take(1)
        ln_eps = take(1)
        lnv, rstd = take(T), take(T)
        mx = take(2, HEADS)
        small_top = top[0]
        shift, scale, gate_m, gate_f = take(D), take(D), take(D), take(D)
        region = top[0]
        proj = take(T, IN_W)
        qkT = take(6, S)
        kdup = take(T, 2, 2, HD)
        probs = take(2, HEADS, 2 * P)
        probsT = take(HEADS, 2, P)
        pooled = take(2, S)
        mixer_top = top[0]
        top[0] = region
        actT = take(KF, S)
        sig = take(2, 2, 512)
        hrow = take(2, D)
        tmp_row = take(2, 512)
        sq_junk = hrow[:, 0]
        top[0] = mixer_top
        window = take(2 * P)
        poolm = take(POOL_G, 3, P)
        inv1 = take(ROT_HALF)
        pos_i = take(T)
        pos_f = take(T)
        cos1, sin1 = take(T, ROT_HALF), take(T, ROT_HALF)
        rt = [take(T, ROT_HALF) for _ in range(3)]
        rope_flat = probs.rearrange("p a b c -> p (a b c)")

        def rope_tile(a, i):
            n = 10 * ROT_HALF
            return rope_flat[:, (T * a + i) * n:(T * a + i + 1) * n].rearrange("p (h d) -> p h d", h=10)

        ang_tmp = take(T, ROT_HALF)
        aux = take(2, 2, 512)
        b_in = take(IN_W)
        sink = take(HEADS)
        pscale = take(POOL_G)
        poolw = take(POOL_G, P)
        crep = take(KD, P)
        ccol = take(KD)
        csil = take(KD)
        ssq = take(8)
        negm, den, esink, rsum = (take(2, HEADS) for _ in range(4))

        top[0] = small_top
        o_hgT = take(HG, S)
        masks = take(LEVELS, P)
        restart = take(S)
        ones = take(P)
        inv2 = take(1)
        lb, one_lb = take(HG), take(HG)
        hg_g, ret_g = take(HG), take(2 * RH)
        cos2, sin2 = take(S), take(S)
        heads_top = top[0]
        sigs = take(4, S)
        q_h = take(S)
        k_h = take(2, S)
        lf = take(2, S)
        cum_f, cum_b, cumx_b = take(S), take(S), take(S)
        gate_h = take(2, S)
        v_h = take(T, P)
        lev_e = take(2, 2, S)
        lev_qk = take(2, 2, S)
        xf_q, xf_k, xb_q, xb_k = (take(4, P) for _ in range(4))
        et_b = take(T)
        scoresT = take(T, S)
        osq, rs_h = take(S), take(S)
        diag = bass.AP(scoresT.tensor, scoresT.offset, [[arena_size, P], [S + P, T], [1, P]])
        hg_top = top[0]
        top[0] = heads_top
        o_retT = take(2 * RH, S)
        rq, rk = take(2, S), take(2, S)
        rv = take(T, RDK)
        rgate = take(2, 2, S)
        rsig = take(2, S)
        rope_a, rope_b = take(2, S), take(2, S)
        rscT = take(T, S)
        o_c, o_sq = take(2, S), take(2, S)
        rrs = take(S)
        strip = take(2, S + 3 * P)
        ret_top = top[0]
        top[0] = heads_top + 8 * S
        mergedT = take(KD, S)
        gsig = take(2, S)
        ytmp = take(2, S)
        ln_g, ln_b = take(2, D), take(2, D)
        bn = take(T, 2, 6)
        mv = take(T, 2)
        x_of_top = top[0]
        wr = take(KD, NL)
        bias_r = take(NL)
        logits = take(T, NL)
        iota = take(P)
        iota_b = take(P)
        before = take(P)
        oh_g, gexp = take(T, GROUPS), take(T, GROUPS)
        picked = take(T, GROUPS, PER_GROUP)
        es, t8 = take(T, PER_GROUP), take(T, PER_GROUP)
        oh_e = take(2, T, PER_GROUP)
        m_k = take(2, T, EXPERTS)
        m_sum = take(T, EXPERTS)
        rank = take(T, EXPERTS)
        ge = take(T, EXPERTS)
        cnt, extra, ends, base_e, over_d = (take(EXPERTS) for _ in range(5))
        r4 = [take(T) for _ in range(6)]
        wts = take(2, T)
        slot_f, slot_i = take(2, T), take(2, T)
        cmp8 = take(8, EXPERTS)
        table_f, table_i = take(MAX_BLOCKS + 1), take(MAX_BLOCKS + 1)
        xsT = take(2, KD, P)
        assert top[0] <= arena_size
        top[0] = heads_top + 8 * S
        msig, mg = take(S), take(S)
        mgT = take(T, P)
        ysb = take(2, D)
        sel = take(2, T, P)
        assert top[0] <= heads_top + 8 * S + 12 * S
        moe_slots = ring + [arena[:, small_top:small_top + SLOT], arena[:, heads_top:heads_top + SLOT]]
        yg = [[ring[k][:, i * D:(i + 1) * D] for i in range(T)] for k in range(2)]
        y_dram = nc.dram_tensor("y_blocks", (MAX_BLOCKS * P, D), F32).ap()
        ang2, sin_arg, cos_arg, ang2_tmp, pos2_f, pos2_i = (o_hgT[:, a] for a in range(6))

        wslot = lambda u: ring[u % RING]
        ready = [sem(f"slot{i}_loaded") for i in range(RING)]

        def x_of(l):
            return 1 + 8 * l

        aux_total = [0, 0]
        aux_at = []
        for j in range(MOD_UNITS):
            aux_total[j % 2] += 16 if (j % 6) < 2 else 32
            aux_at.append(aux_total[j % 2])

        block = ctx.enter_context(nc.Block())

        @block.sync
        def _(sp):
            sp.dma_start(x, A["x"].rearrange("b (t p) d -> p (b t) d", p=P)).then_inc(sem("x_in"), 16)

            sp.sem_inc(sem("down_mm"), DOWN_CREDIT)
            sp.sem_inc(sem("post_mm"), POST_CREDIT)

            def wait_slot(l, u):
                name, per_layer, count = unit_done(u - RING)
                sp.wait_ge(sem(name), l * per_layer + count)

            def unit(l, u, dst, src):
                wait_slot(l, u)
                sp.dma_start(dst, src).then_inc(ready[u % RING], 16)

            with sp.Fori(0, LAYERS) as l:
                def cols(name, u, c0, n):
                    w = A[name][l].rearrange("(k p) n -> p k n", p=P)
                    unit(l, u, wslot(u)[:, 0:KD * n].rearrange("p (k n) -> p k n", k=KD), w[:, :, c0:c0 + n])

                for j in range(6):
                    cols("ada_w", U_MOD_M + j, 512 * j, 512)
                for j in range(IN_UNITS):
                    cols("w_in", U_IN + j, IN_COLS * j, IN_COLS)
                for j in range(6):
                    cols("ada_w", U_MOD_F + j, 512 * (6 + j), 512)
                for j in range(OUT_UNITS):
                    cols("w_out", U_OUT + j, 512 * j, 512)
                wg = A["w_gate"][l].rearrange("(k p) n -> p k n", p=P)
                wu = A["w_up"][l].rearrange("(k p) n -> p k n", p=P)
                for j in range(GU_UNITS):
                    u = U_GU + j
                    dst = wslot(u).rearrange("p (h k n) -> p h k n", h=2, k=KD)
                    wait_slot(l, u)
                    sp.dma_start(dst[:, 0], wg[:, :, 256 * j:256 * j + 256]).then_inc(ready[u % RING], 16)
                    sp.dma_start(dst[:, 1], wu[:, :, 256 * j:256 * j + 256]).then_inc(ready[u % RING], 16)
                wd = A["w_down"][l].rearrange("(k p) n -> p k n", p=P)
                for j, (k0, n) in enumerate(DOWN_UNITS):
                    unit(l, U_DOWN + j, wslot(U_DOWN + j)[:, 0:n * D].rearrange("p (k n) -> p k n", k=n),
                         wd[:, k0:k0 + n, :])

            w2 = A["w_in_2"][0].rearrange("(k p) n -> p k n", p=P)

            def pieces(n, width, srcs, wait):
                sp.wait_ge(*wait)
                dst = ring[n % RING][:, 0:KD * width * len(srcs)].rearrange("p (s k n) -> p s k n", k=KD, n=width)
                for a, src in enumerate(srcs):
                    sp.dma_start(dst[:, a], src).then_inc(ready[n % RING], 16)

            def hg_units(h, b, waits):
                def src(col):
                    return w2[:, :, bass.ds(h * P + col, P)]
                pieces(2 * b, P, [src(COL_Q), src(COL_F), src(COL_FB)], waits[0])
                pieces(2 * b + 1, P, [src(COL_G), src(COL_V)], waits[1])

            def layer_end(u):
                name, per_layer, count = unit_done(u)
                return sem(name), (LAYERS - 1) * per_layer + count

            hg_units(0, 0, (layer_end(LAYER_UNITS - 4), layer_end(LAYER_UNITS - 3)))
            hg_units(1, 1, (layer_end(LAYER_UNITS - 2), layer_end(LAYER_UNITS - 1)))

            with sp.Fori(0, HG // 2 - 1) as i:
                for b in range(2):
                    h = i * 2 + (2 + b)
                    hg_units(h, b, ((sem("hgp_mm"), i * 10 + (3 + 5 * b)), (sem("hgp_mm"), i * 10 + (5 + 5 * b))))

            def ret_units(r):
                b, c = r % 2, r * RDK
                if r < 2:
                    f = 5 * (HG - 2 + r)
                    waits = (sem("hgp_mm"), f + 3), (sem("hgp_mm"), f + 5)
                else:
                    waits = (sem("retp_mm"), 8 * (r - 2) + 4), (sem("retp_mm"), 8 * (r - 2) + 8)
                pieces(2 * b, RDK, [w2[:, :, COL_RQ + c:COL_RQ + c + RDK], w2[:, :, COL_RK + c:COL_RK + c + RDK]], waits[0])
                pieces(2 * b + 1, RDK, [w2[:, :, COL_RG + c:COL_RG + c + RDK], w2[:, :, COL_RV + c:COL_RV + c + RDK]], waits[1])

            for r in range(RH):
                ret_units(r)
            wh = A["w_branch_hg_2"][0].rearrange("(k p) n -> p k n", p=P)
            wr = A["w_branch_ret_2"][0].rearrange("(k p) n -> p k n", p=P)
            wo = A["w_out_2"][0].rearrange("(k p) n -> p k n", p=P)
            merge_srcs = []
            for c in range(2):
                for g, w in ((COL_GA, wh), (COL_GB, wr)):
                    merge_srcs += [w2[:, :, g + 512 * c:g + 512 * c + 512], w[:, :, 512 * c:512 * c + 512]]
            for n, src in enumerate(merge_srcs):
                if n < 4:
                    wait = sem("retp_mm"), 8 * (2 + n // 2) + (4, 8)[n % 2]
                else:
                    wait = sem("merge_mm"), 4 * ((n - 4) // 2 + 1)
                pieces(n, 512, [src], wait)
            for n in range(4):
                pieces(n, 256, [wo[:, :, 256 * n:256 * n + 256]], (sem("merge_mm"), 4 * (n // 2 + 3)))
            def expert_units(b, e, waits):
                for a, name in enumerate(("w1_2", "w3_2", "w2_2")):
                    dst = moe_slots[3 * b + a]
                    src = A[name][0, e].rearrange("(k p) n -> p k n", p=P)
                    for w_ in waits[a]:
                        sp.wait_ge(*w_)
                    sp.dma_start(dst.rearrange("p (k n) -> p k n", n=src.shape[2]), src
                                 ).then_inc(sem(f"expert_w{3 * b + a}"), 16)

            mixed = lambda n: [(sem("mix2_mm"), 4 * (n + 1))]
            expert_units(0, 0, (mixed(0), mixed(1), mixed(2)))
            expert_units(1, 1, (mixed(3), [(sem("merge_mm"), 16)], [(sem("merge_mm"), 16)]))
            sp.wait_ge(sem("table_ready"), 1)
            turns = sp.value_load(table_i[0:1, MAX_BLOCKS:MAX_BLOCKS + 1].bitcast(I32), min_val=16, max_val=20)
            with sp.Fori(1, turns) as i:
                for b in range(2):
                    e = sp.value_load(table_i[0:1, bass.ds(2 * i + b, 1)].bitcast(I32), min_val=0, max_val=EXPERTS - 1)
                    h_done = [(sem("h_mm"), 2 * i + (b - 1))]
                    expert_units(b, e, (h_done, h_done, [(sem("y_mm"), 2 * i + (b - 1))]))
            sp.wait_ge(sem("x2_ready"), 4)
            sp.dma_start(out.rearrange("b (t p) d -> p (b t) d", p=P), x).then_inc(sem("out_done"), 16)
            sp.wait_ge(sem("out_done"), 16)

        arrivals = [0] * RING
        arrive_at = []
        for u in range(LAYER_UNITS):
            arrivals[u % RING] += 32 if U_GU <= u < U_DOWN else 16
            arrive_at.append(arrivals[u % RING])

        @block.gpsimd
        def _(pool):
            for dst, src in ((ident, K["ident"]), (window, K["window"]),
                             (poolm.rearrange("p a b c -> p (a b c)"), K["pool"]), (inv1, K["inv1"]),
                             (ccol, A["c"].rearrange("b (k p) -> p (b k)", p=P)),
                             (pos_i.bitcast(I32), A["positions"].rearrange("b (t p) -> p (b t)", p=P))):
                with nc.allow_non_contiguous_dma("small loads, once"):
                    pool.dma_start(dst, src).then_inc(sem("const_in"), 16)
            nc.gpsimd.memset(pooled, 0.0).then_inc(sem("zeros_ready"), 1)
            pool.wait_ge(sem("zeros_ready"), 1)
            for b in range(EXPERTS, MAX_BLOCKS):
                pool.dma_start(y_dram[b * P:(b + 1) * P, :], pooled.rearrange("p a n -> p (a n)")
                               ).then_inc(sem("zeros_out"), 16)
            with pool.Fori(0, LAYERS) as l:
                pool.wait_ge(sem("x_ready"), x_of(l))
                with nc.allow_non_contiguous_dma("small loads"):
                    pool.dma_start(b_in, A["b_in"][l].partition_broadcast(P)).then_inc(sem("layer_in"), 16)
                    pool.dma_start(sink, A["sinks"][l].partition_broadcast(P)).then_inc(sem("layer_in"), 16)
                    pool.dma_start(pscale, A["pool_scale"][l].rearrange("(g p) -> p g", p=P)
                                   ).then_inc(sem("layer_in"), 16)
                    pool.dma_start(poolw, A["pool_w"][l].rearrange("g c d -> c g d")).then_inc(sem("layer_in"), 16)
                for j in range(MOD_UNITS):
                    what, c = (j % 6) // 2, 512 * (j % 2)
                    pool.wait_ge(sem("mod_free"), l * MOD_UNITS + (j + 1))
                    pool.dma_start(aux[:, j % 2, 0], A["ada_b"][l, 512 * j:512 * j + 512].partition_broadcast(P)
                                   ).then_inc(sem(f"aux{j % 2}_in"), 16)
                    if what:
                        g = A[(("g_pre_mix", "g_post_mix"), ("g_pre_ffn", "g_post_ffn"))[j // 6][what - 1]]
                        pool.dma_start(aux[:, j % 2, 1], g[l, c:c + 512].partition_broadcast(P)
                                       ).then_inc(sem(f"aux{j % 2}_in"), 16)

            pool.wait_ge(sem("x_ready"), x_of(LAYERS))
            with nc.allow_non_contiguous_dma("small loads"):
                for dst, src in (
                        (pos2_i.bitcast(I32), A["positions_2"][0].partition_broadcast(P)),
                        (inv2, K["inv2"]), (restart, K["restart"]),
                        (masks.rearrange("p a b -> p (a b)"), K["masks"]),
                        (lb, A["hg_lb_logits_2"][0].rearrange("(h p) -> p h", p=P)),
                        (one_lb, A["hg_lb_logits_2"][1].rearrange("(h p) -> p h", p=P)),
                        (hg_g, A["hg_norm_g_2"][0].rearrange("(h p) -> p h", p=P)),
                        (ret_g, A["ret_norm_g_2"][0].rearrange("(h p) -> p h", p=P))):
                    pool.dma_start(dst, src).then_inc(sem("const2_in"), 16)
            pool.wait_ge(sem("hg_out"), HG + 1)
            for r in range(RH):
                if r >= 2:
                    pool.wait_ge(sem("rsc_ready"), 4 * (r - 1))
                pool.dma_start(strip[:, r % 2], K["decay"][r]).then_inc(sem(f"strip{r % 2}_in"), 16)
            pool.wait_ge(sem("ret_out"), RH)
            for dst, name in ((ln_g[:, 0], "ln1_g_2"), (ln_b[:, 0], "ln1_b_2")):
                pool.dma_start(dst, A[name][0].partition_broadcast(P)).then_inc(sem("ln0_in"), 16)

            for dst, src in ((wr[:, :, 0:GROUPS], A["w_group_2"][0].rearrange("(k p) n -> p k n", p=P)),
                             (wr[:, :, GROUPS:NL], A["w_router_2"][0].rearrange("(k p) n -> p k n", p=P)),
                             (bias_r[:, 0:GROUPS], A["b_group_2"][0].partition_broadcast(P)),
                             (bias_r[:, GROUPS:NL], A["b_router_2"][0].partition_broadcast(P)),
                             (iota, K["iota"]), (before, K["before"])):
                with nc.allow_non_contiguous_dma("small loads"):
                    pool.dma_start(dst, src).then_inc(sem("route_in"), 16)
            for dst, name in ((ln_g[:, 1], "ln2_g_2"), (ln_b[:, 1], "ln2_b_2")):
                pool.dma_start(dst, A[name][0].partition_broadcast(P)).then_inc(sem("ln1_in"), 16)
            pool.wait_ge(sem("table_ready"), 1)
            pool.sem_inc(sem("ysb_free"), 2)
            turns = pool.value_load(table_i[0:1, MAX_BLOCKS:MAX_BLOCKS + 1].bitcast(I32), min_val=16, max_val=20)
            with pool.Fori(0, turns) as i:
                for b in range(2):
                    pool.wait_ge(sem("y_taken"), 2 * i + (b + 1))
                    pool.sem_inc(sem("store_order"), 1)
                    pool.dma_start(y_dram[bass.ds((2 * i + b) * P, P), :], ysb[:, b]).then_inc(sem("y_stored"), 16)
                    pool.wait_ge(sem("y_stored"), 32 * i + (16 * b + 16))
                    pool.sem_inc(sem("ysb_free"), 1)
            pool.wait_ge(sem("zeros_out"), 16 * (MAX_BLOCKS - EXPERTS))
            for i in range(T):
                for k in range(2):
                    pool.indirect_dma_start(
                        out=yg[k][i], out_offset=None, in_=y_dram,
                        in_offset=bass.IndirectOffsetOnAxis(ap=slot_i[:, k, i:i + 1].bitcast(I32), axis=0),
                        bounds_check=MAX_BLOCKS * P - 1, oob_is_err=False).then_inc(sem(f"rows{i}_in"), 16)

        @block.tensor
        def _(pe):

            def need(l, u):
                pe.wait_ge(ready[u % RING], l * arrivals[u % RING] + arrive_at[u])
                return wslot(u)

            def modulation(l, j, u):
                w = need(l, u).rearrange("p (k n) -> p k n", k=KD)
                pe.wait_ge(sem("mod_free"), l * MOD_UNITS + (j + 1))
                for k in range(KD):
                    m = nc.tensor.matmul(bank(j % 2), crep[:, k], w[:, k], start=k == 0, stop=k == KD - 1)
                m.then_inc(sem("mod_mm"), 1)

            def to_features(n):
                for i in range(T):
                    pe.wait_ge(sem("h_row"), 4 * n + (i + 1))
                    if i >= 2:
                        pe.wait_ge(sem("hT_ready"), 4 * n + (i - 1))
                    for k in range(KD):
                        m = nc.tensor.transpose(psum[:, 2 + 2 * (i % 2) + k // 4, (k % 4) * P:(k % 4 + 1) * P],
                                                hrow[:, i % 2, k * P:(k + 1) * P], ident)
                    m.then_inc(sem("tr_mm"), 1)
                pe.wait_ge(sem("hT_ready"), 4 * n + 4)

            pe.wait_ge(sem("crep_ready"), 1)
            with pe.Fori(0, LAYERS) as l:
                pe.wait_ge(sem("x_ready"), x_of(l))
                for j in range(6):
                    modulation(l, j, U_MOD_M + j)
                to_features(2 * l)
                for c in range(IN_UNITS):
                    w = need(l, U_IN + c)[:, 0:KD * IN_COLS].rearrange("p (k n) -> p k n", k=KD)
                    for i in range(T):
                        pe.wait_ge(sem("proj_free"), 16 * l + (4 * c + i + 1))
                        for k in range(KD):
                            m = nc.tensor.matmul(psum[:, 2 + i, 0:IN_COLS], hT[:, k, i * P:(i + 1) * P], w[:, k],
                                                 start=k == 0, stop=k == KD - 1)
                        m.then_inc(sem("proj_mm"), 1)
                for j in range(6, 12):
                    modulation(l, j, U_MOD_F + j - 6)
                pe.wait_ge(sem("proj_free"), 16 * l + 20)
                pe.wait_ge(sem("layer_in"), 64 * l + 64)

                def pool_window(g):
                    for i in range(T):
                        u_i = [proj[:, j, QKV + g * P:QKV + (g + 1) * P] for j in (i, max(i - 1, 0))]
                        o = psum[:, 2 + g % 2, i * P:(i + 1) * P]
                        m = nc.tensor.matmul(o, u_i[0], poolm[:, g, 0 if i else 2], start=True, stop=i == 0)
                        if i:
                            m = nc.tensor.matmul(o, u_i[1], poolm[:, g, 1], start=False, stop=True)
                    m.then_inc(sem("pool_mm"), 1)

                def pool_weights(g):
                    pe.wait_ge(sem("pooled_ready"), 4 * l + (g + 1))
                    if g >= 2:
                        pe.wait_ge(sem("poolT_ready"), 4 * l + (g - 1))
                    nc.tensor.matmul(bank(6 + g % 2), poolw[:, g], pooled[:, g % 2], start=True, stop=True
                                     ).then_inc(sem("poolw_mm"), 1)

                pool_window(0)
                pool_window(1)
                for g in range(POOL_G):
                    pool_weights(g)
                    if g + 2 < POOL_G:
                        pool_window(g + 2)
                pe.wait_ge(sem("rope_done"), l + 1)
                for c in range(6):
                    if c >= 4:
                        pe.wait_ge(sem("qkT_ready"), 6 * l + (c - 3))
                    for i in range(T):
                        src = proj[:, i, c * P:(c + 1) * P] if c < 4 else \
                            kdup[:, i, c - 4].rearrange("p a d -> p (a d)")
                        m = nc.tensor.transpose(psum[:, 2 + c % 4, i * P:(i + 1) * P], src, ident)
                    m.then_inc(sem("qkT_mm"), 1)
                pe.wait_ge(sem("qkT_ready"), 6 * l + 6)
                pe.wait_ge(sem("poolT_ready"), 4 * l + 4)

                def scores(n):
                    k0, nk = (n - 1, 2 * P) if n else (0, P)
                    for jj in range(KVH):
                        if n:
                            pe.wait_ge(sem("score_free"), 16 * l + (4 * (n - 1) + 2 * jj + 2))
                        for j in (2 * jj, 2 * jj + 1):
                            for a in range(2):
                                half = slice(64 * a, 64 * a + 64)
                                m = nc.tensor.matmul(psum[:, 4 + 2 * jj + a, (j % 2) * nk:(j % 2 + 1) * nk],
                                                     qkT[half, j, n * P:(n + 1) * P],
                                                     qkT[half, 4 + jj, k0 * P:k0 * P + nk], start=True, stop=True)
                                if j % 2:
                                    m.then_inc(sem("score_mm"), 1)

                def attend(n):
                    nk = 2 if n else 1
                    pe.wait_ge(sem("probs_ready"), 4 * l + (n + 1))
                    for g in range(4):
                        if 4 * n + g >= 2:
                            pe.wait_ge(sem("probsT_ready"), 16 * l + (4 * n + g - 1))
                        for a in range(2):
                            for b in range(nk):
                                m = nc.tensor.transpose(psum[:, 2 + g % 2, (a * nk + b) * P:(a * nk + b + 1) * P],
                                                        probs[:, n % 2, 2 * g + a, b * P:(b + 1) * P], ident)
                        m.then_inc(sem("probsT_mm"), 1)
                    pe.wait_ge(sem("probsT_ready"), 16 * l + (4 * n + 4))
                    if n >= 2:
                        pe.wait_ge(sem("attnT_ready"), 4 * l + (n - 1))
                    else:
                        pe.wait_ge(sem("mod_free"), l * MOD_UNITS + 14)
                    for h in range(HEADS):
                        v0 = HEADS * HD + KVH * HD + (h // GROUP) * HD
                        o = psum[64 * (h % 2):64 * (h % 2) + 64, n % 2, (h // 2) * P:(h // 2 + 1) * P]
                        for b in range(nk):
                            m = nc.tensor.matmul(o, proj[:, n - nk + 1 + b, v0:v0 + HD], probsT[:, h, b],
                                                 start=b == 0, stop=b == nk - 1)
                    m.then_inc(sem("attn_mm"), 1)

                scores(0)
                for n in range(T):
                    if n + 1 < T:
                        scores(n + 1)
                    attend(n)
                pe.wait_ge(sem("attnT_ready"), 4 * l + 4)
                for c in range(OUT_UNITS):
                    w = need(l, U_OUT + c).rearrange("p (k n) -> p k n", k=KD)
                    for i in range(T):
                        for k in range(KD):
                            m = nc.tensor.matmul(bank(4 * c + i), mixT[:, k, i * P:(i + 1) * P], w[:, k],
                                                 start=k == 0, stop=k == KD - 1)
                        m.then_inc(sem("post_mm"), 1)
                to_features(2 * l + 1)
                for u in range(GU_UNITS):
                    w = need(l, U_GU + u).rearrange("p (h k n) -> p h k n", h=2, k=KD)
                    if u >= 2:
                        pe.wait_ge(sem("actT_ready"), GU_UNITS * l + (u - 1))
                    for a in range(2):
                        for c in range(2):
                            for k in range(KD):
                                m = nc.tensor.matmul(bank(4 * (u % 2) + 2 * a + c), w[:, a, k, c * P:(c + 1) * P],
                                                     hT[:, k], start=k == 0, stop=k == KD - 1)
                    m.then_inc(sem("gu_mm"), 1)
                for j, (k0, nk) in enumerate(DOWN_UNITS):
                    w = need(l, U_DOWN + j)[:, 0:nk * D].rearrange("p (k n) -> p k n", k=nk)
                    if j == 0:
                        pe.wait_ge(sem("actT_ready"), GU_UNITS * l + GU_UNITS)
                    for k in range(nk):
                        for i in range(T):
                            for c in range(2):
                                m = nc.tensor.matmul(bank(4 * c + i), actT[:, k0 + k, i * P:(i + 1) * P],
                                                     w[:, k, c * 512:(c + 1) * 512],
                                                     start=k0 + k == 0, stop=k0 + k == KF - 1)
                                if k0 + k == KF - 1:
                                    m.then_inc(sem("post_mm"), 1)
                    if k0 + nk < KF:
                        m.then_inc(sem("down_mm"), 1)


            def x_to_features(n, sem_name):
                for i in range(T):
                    pe.wait_ge(sem(sem_name), {"x_ready": 1 + 4 * XT_TURN - 3 + i, "x1_ready": i + 1}[sem_name])
                    if i >= 2:
                        pe.wait_ge(sem("hT_ready"), 4 * n + i - 1)
                    for k in range(KD):
                        m = nc.tensor.transpose(psum[:, 2 + 2 * (i % 2) + k // 4, (k % 4) * P:(k % 4 + 1) * P],
                                                x[:, i, k * P:(k + 1) * P], ident)
                    m.then_inc(sem("tr_mm"), 1)
                pe.wait_ge(sem("hT_ready"), 4 * n + 4)

            pe.wait_ge(sem("x_ready"), x_of(LAYERS))
            x_to_features(XT_TURN, "x_ready")
            xT = hT
            seen = [LAYERS * a for a in arrivals]

            def hg_chunk(h, b, what):
                if what in (0, 3):
                    slot = 2 * b + what // 3
                    n = 48 if what == 0 else 32
                    pe.wait_ge(ready[slot], (h - b) * (n // 2) + (seen[slot] + n))
                w = ring[2 * b + what // 3][:, 0:KD * P * (3 if what < 3 else 2)].rearrange(
                    "p (s k n) -> p s k n", k=KD, n=P)[:, what % 3]
                if what < 4:
                    for k in range(KD):
                        m = nc.tensor.matmul(bank(what), w[:, k], xT[:, k], start=k == 0, stop=k == KD - 1)
                else:
                    for i in range(T):
                        for k in range(KD):
                            m = nc.tensor.matmul(psum[:, 4, i * P:(i + 1) * P], xT[:, k, i * P:(i + 1) * P], w[:, k],
                                                 start=k == 0, stop=k == KD - 1)
                m.then_inc(sem("hgp_mm"), 1)

            def hg_free(h, what):
                if what == 0:
                    pe.wait_ge(sem("hgp_taken"), 2 * h - 1)
                elif what in (1, 2):
                    pe.wait_ge(sem("hg_sig"), 4 * h - 2 + (what - 1))
                elif what == 3:
                    pe.wait_ge(sem("hgp_taken"), 2 * h)
                else:
                    pe.wait_ge(sem("v_ready"), h)

            def next_chunk(h, b, what, last):
                if last:
                    if what < 4:
                        ret_qk(0, what)
                    return
                hg_free(h + 1, what)
                hg_chunk(h + 1, 1 - b, what)

            def ret_w(r, side, width=RDK):
                return ring[2 * (r % 2) + side][:, 0:2 * KD * width].rearrange("p (s k n) -> p s k n", k=KD, n=width)

            def ret_qk(r, what):
                if what == 0:
                    pe.wait_ge(ready[2 * (r % 2)], seen[2 * (r % 2)] + 48 * (HG // 2) + 32 * (r // 2 + 1))
                if r == 0:
                    hg_free(HG, what)
                else:
                    pe.wait_ge(sem("rsc_ready"), 4 * (r - 1) + what + 1)
                w = ret_w(r, 0)[:, what // 2]
                for k in range(KD):
                    m = nc.tensor.matmul(bank(what), w[:, k, what % 2:RDK:2], xT[:, k], start=k == 0, stop=k == KD - 1)
                m.then_inc(sem("retp_mm"), 1)

            def hg_norm_sum(h):
                pe.wait_ge(sem("osq_ready"), h + 1)
                nc.tensor.matmul(bank(6), ones, osq, start=True, stop=True).then_inc(sem("hgs_mm"), 1)

            def hg_level(h, l):
                pe.wait_ge(sem("kq_ready"), 8 * h + (LEVELS - l + 1))
                if l >= LEVELS - 2:
                    pe.wait_ge(sem("row_ready"), 4 * h + (LEVELS - 1 - l + 3))
                else:
                    pe.wait_ge(sem("level_taken"), 7 * h + (LEVELS - 2 - l))
                for i in range(T):
                    ts = slice(i * P, (i + 1) * P)
                    rhs = lev_qk[:, l % 2, 0, ts] if l else q_h[:, ts]
                    m = nc.tensor.matmul(psum[:, 5 + (LEVELS - 1 - l) % 2, ts], lev_qk[:, l % 2, 1, ts], rhs,
                                         start=True, stop=True)
                m.then_inc(sem("hgs_mm"), 1)

            def hg_rows(h):
                pe.wait_ge(sem("kq_ready"), 8 * h + 1)
                for s in range(T):
                    if s == 1:
                        pe.wait_ge(sem("sum_taken"), h + 1)
                    elif s >= 2:
                        pe.wait_ge(sem("row_ready"), 4 * h + (s - 1))
                    far_f, far_b = xf_q[:, 2:4].rearrange("p a t -> p (a t)"), xb_q[:, 2:4].rearrange("p a t -> p (a t)")
                    own = (s, 1, lev_qk[:, 1, 1, s * P:(s + 1) * P], lev_qk[:, 1, 0, s * P:(s + 1) * P])
                    products = {
                        0: [own, (1, 1, xf_k[:, 0], xf_q[:, 0]), (2, 2, xf_k[:, 2], far_f)],
                        1: [(0, 1, xb_k[:, 0], xb_q[:, 0]), own, (2, 2, xf_k[:, 3], far_f)],
                        2: [(0, 2, xb_k[:, 2], far_b), own, (3, 1, xf_k[:, 1], xf_q[:, 1])],
                        3: [(0, 2, xb_k[:, 3], far_b), (2, 1, xb_k[:, 1], xb_q[:, 1]), own],
                    }[s]
                    for t, n, lhs, rhs in products:
                        m = nc.tensor.matmul(psum[:, 5 + s % 2, t * P:(t + n) * P], lhs, rhs, start=True, stop=True)
                    m.then_inc(sem("hgs_mm"), 1)

            def hg_out(h):
                pe.wait_ge(sem("level_taken"), 7 * h + 7)
                pe.wait_ge(sem("v_ready"), h + 1)
                pe.wait_ge(sem("hg_out"), h + 1)
                for i in range(T):
                    m = nc.tensor.matmul(bank(7), v_h[:, i], scoresT[:, i], start=i == 0, stop=i == T - 1)
                m.then_inc(sem("o_mm"), 1)

            def hg_head(h, b, first=False, last=False):
                next_chunk(h, b, 0, last)
                if not first:
                    hg_norm_sum(h - 1)
                hg_rows(h)
                for what, pair in ((1, (6, 5)), (2, (4, 3)), (3, (2, 1)), (4, (0,))):
                    next_chunk(h, b, what, last)
                    for l in pair:
                        hg_level(h, l)
                hg_out(h)

            pe.wait_ge(sem("ones_ready"), 1)
            for what in range(5):
                hg_chunk(0, 0, what)
            hg_head(0, 0, first=True)
            with pe.Fori(0, HG // 2 - 1) as i:
                hg_head(2 * i + 1, 1)
                hg_head(2 * i + 2, 0)
            hg_head(HG - 1, 1, last=True)
            hg_norm_sum(HG - 1)

            def ret_gate(r):
                pe.wait_ge(ready[2 * (r % 2) + 1], seen[2 * (r % 2) + 1] + 32 * (HG // 2) + 32 * (r // 2 + 1))
                if r == 0:
                    pe.wait_ge(sem("hg_out"), HG + 1)
                else:
                    pe.wait_ge(sem("rgate_ready"), r)
                if r >= 2:
                    pe.wait_ge(sem("rsum_taken"), r - 1)
                w = ret_w(r, 1)[:, 0]
                for a in range(2):
                    for k in range(KD):
                        m = nc.tensor.matmul(bank(6 + a), w[:, k, a * P:(a + 1) * P], xT[:, k],
                                             start=k == 0, stop=k == KD - 1)
                    m.then_inc(sem("retp_mm"), 1)

            def ret_v(r):
                w = ret_w(r, 1)[:, 1]
                if r:
                    pe.wait_ge(sem("o_copied"), 2 * r)
                for i in range(T):
                    for k in range(KD):
                        m = nc.tensor.matmul(psum[:, 4 + i // 2, (i % 2) * RDK:(i % 2 + 1) * RDK],
                                             xT[:, k, i * P:(i + 1) * P], w[:, k], start=k == 0, stop=k == KD - 1)
                    if i % 2:
                        m.then_inc(sem("retp_mm"), 1)

            def ret_scores(r):
                pe.wait_ge(sem("rope2_done"), 2 * r + 2)
                for s in range(T):
                    for a in range(2):
                        m = nc.tensor.matmul(bank(s), rk[:, a, s * P:(s + 1) * P], rq[:, a],
                                             start=a == 0, stop=a == 1)
                    m.then_inc(sem("rs_mm"), 1)

            def ret_out(r):
                pe.wait_ge(sem("rsc_ready"), 4 * r + 4)
                pe.wait_ge(sem("rv_ready"), 2 * r + 2)
                for a in range(2):
                    for s in range(T):
                        m = nc.tensor.matmul(bank(4 + a), rv[:, s, a * P:(a + 1) * P], rscT[:, s],
                                             start=s == 0, stop=s == T - 1)
                    m.then_inc(sem("ro_mm"), 1)

            def ret_norm_sum(r):
                pe.wait_ge(sem("rosq_ready"), r + 1)
                pe.wait_ge(sem("rgate_ready"), min(r + 2, RH))
                for a in range(2):
                    m = nc.tensor.matmul(bank(6), ones, o_sq[:, a], start=a == 0, stop=a == 1)
                m.then_inc(sem("rsum_mm"), 1)

            ret_gate(0)
            pe.wait_ge(sem("v_ready"), HG)
            ret_v(0)
            for r in range(RH):
                ret_scores(r)
                if r + 1 < RH:
                    for what in range(4):
                        ret_qk(r + 1, what)
                ret_out(r)
                if r + 1 < RH:
                    ret_gate(r + 1)
                    ret_v(r + 1)
                ret_norm_sum(r)

            base = [seen[n] + (48, 32, 48, 32)[n] * (HG // 2) + 32 * (RH // 2) for n in range(RING)]
            pe.wait_ge(sem("ret_out"), RH)
            for n in range(0, 8, 2):
                src = o_hgT if n % 4 == 0 else o_retT
                for a in range(2):
                    pe.wait_ge(ready[(n + a) % RING], base[(n + a) % RING] + 16 * ((n + a) // RING + 1))
                wg_, wb = (ring[(n + a) % RING].rearrange("p (k n) -> p k n", k=KD) for a in range(2))
                for j in range(4):
                    s = 2 * n + j
                    if s >= 4:
                        pe.wait_ge(sem("merge_taken"), s - 3)
                    b = 2 * (s % 4)
                    for k in range(KD):
                        m = nc.tensor.matmul(bank(b), wg_[:, k, j * P:(j + 1) * P], xT[:, k],
                                             start=k == 0, stop=k == KD - 1)
                    for k in range(KD):
                        m = nc.tensor.matmul(bank(b + 1), wb[:, k, j * P:(j + 1) * P], src[:, k],
                                             start=k == 0, stop=k == KD - 1)
                    m.then_inc(sem("merge_mm"), 1)
            pe.wait_ge(sem("merge_taken"), 16)
            for n in range(4):
                pe.wait_ge(ready[n], base[n] + 16 * 3)
                w = ring[n][:, 0:KD * 256].rearrange("p (k n) -> p k n", k=KD)
                for i in range(T):
                    for k in range(KD):
                        m = nc.tensor.matmul(psum[:, 2 * i + n // 2, (n % 2) * 256:(n % 2 + 1) * 256],
                                             mergedT[:, k, i * P:(i + 1) * P], w[:, k],
                                             start=k == 0, stop=k == KD - 1)
                    m.then_inc(sem("mix2_mm"), 1)


            x_to_features(XT_TURN + 1, "x1_ready")
            pe.wait_ge(sem("route_in"), 96)
            for i in range(T):
                for k in range(KD):
                    m = nc.tensor.matmul(psum[:, 0, i * NL:(i + 1) * NL], hT[:, k, i * P:(i + 1) * P], wr[:, k],
                                         start=k == 0, stop=k == KD - 1)
            m.then_inc(sem("logits_mm"), 1)
            pe.wait_ge(sem("onehots_ready"), 1)
            for i in range(T + 1):
                o = psum[:, 1, i * EXPERTS:(i + 1) * EXPERTS]
                for j in range(i):
                    m = nc.tensor.matmul(o, ones, m_sum[:, j], start=j == 0, stop=j == T - 1)
                if i < T:
                    m = nc.tensor.matmul(o, before, m_sum[:, i], start=i == 0, stop=True)
            m.then_inc(sem("ranks_mm"), 1)

            def gather(j, b):
                pe.wait_ge(sem("sel_ready"), j + 1)
                if not isinstance(j, int):
                    pe.wait_ge(sem("xs_ready"), j)
                for k in range(KD):
                    for i in range(T):
                        m = nc.tensor.matmul(psum[:, k // 4, (k % 4) * P:(k % 4 + 1) * P], x[:, i, k * P:(k + 1) * P],
                                             sel[:, b, i], start=i == 0, stop=i == T - 1)
                m.then_inc(sem("gather_mm"), 1)

            def expert(i, b):
                j = 2 * i + b
                w1, w3 = (moe_slots[3 * b + a].rearrange("p (k n) -> p k n", k=KD) for a in range(2))
                w2_ = moe_slots[3 * b + 2].rearrange("p (k n) -> p k n", k=DE // P)
                pe.wait_ge(sem("xs_ready"), j + 1)
                for a, w in enumerate((w1, w3)):
                    pe.wait_ge(sem(f"expert_w{3 * b + a}"), 16 * i + 16)
                    for k in range(KD):
                        m = nc.tensor.matmul(bank(2 + a), xsT[:, b, k], w[:, k], start=k == 0, stop=k == KD - 1)
                m.then_inc(sem("h_mm"), 1)
                gather(j + 1, 1 - b)
                pe.wait_ge(sem("mg_ready"), j + 1)
                for k in range(DE // P):
                    m = nc.tensor.transpose(psum[:, 4, k * P:(k + 1) * P], mg[:, k * P:(k + 1) * P], ident)
                m.then_inc(sem("mgT_mm"), 1)
                pe.wait_ge(sem("mgT_ready"), j + 1)
                pe.wait_ge(sem("y_free"), j + 1)
                pe.wait_ge(sem(f"expert_w{3 * b + 2}"), 16 * i + 16)
                for c in range(2):
                    for k in range(DE // P):
                        m = nc.tensor.matmul(bank(5 + c), mgT[:, k], w2_[:, k, 512 * c:512 * c + 512],
                                             start=k == 0, stop=k == DE // P - 1)
                m.then_inc(sem("y_mm"), 1)

            pe.wait_ge(sem("table_ready"), 1)
            turns = pe.value_load(table_i[0:1, MAX_BLOCKS:MAX_BLOCKS + 1].bitcast(I32), min_val=16, max_val=20)
            gather(0, 0)
            with pe.Fori(0, turns) as i:
                for b in range(2):
                    expert(i, b)

        @block.scalar
        def _(act):
            C = Chain(act, sem("act_order"))

            def rsqrt_mean(src, dst, n):
                C.settle()
                C.link(nc.scalar.activation(lnv[:, 0:n], src, ACT.Ln, bias=eps, scale=1.0 / D))
                C.settle()
                return nc.scalar.activation(dst, lnv[:, 0:n], ACT.Exp, scale=-0.5)

            act.wait_ge(sem("const_in"), 96)
            C.link(nc.scalar.activation(csil, ccol, ACT.Silu))
            C.settle()
            for k in range(KD):
                m = nc.scalar.activation(crep[:, k], csil[:, k:k + 1].to_broadcast([P, P]), ACT.Copy)
                m.then_inc(sem("crep_ready"), 1) if k == KD - 1 else C.link(m)
            act.wait_ge(sem("angles_ready"), 1)
            C.link(nc.scalar.activation(sin1, rt[1], ACT.Sin))
            nc.scalar.activation(cos1, rt[2], ACT.Sin).then_inc(sem("rope_tables"), 1)

            def pre_norm(l, which):
                n = 2 * l + which
                act.wait_ge(sem("x_ready"), 8 * l + (1 + 4 * which))
                for i in range(T):
                    C.link(nc.scalar.activation(sq_junk, x[:, i], ACT.Square, accum_out=ssq[:, i:i + 1]))
                    C.settle()
                rsqrt_mean(ssq[:, 0:T], rstd, T).then_inc(sem("pre_rstd"), 1)
                for i in range(T):
                    act.wait_ge(sem("tr_mm"), 4 * n + (i + 1))
                    for q in range(2):
                        m = nc.scalar.activation(hT[:, 4 * q:4 * q + 4, i * P:(i + 1) * P],
                                                 bank(2 + 2 * (i % 2) + q).rearrange("p (k t) -> p k t", k=4), ACT.Copy)
                        m.then_inc(sem("hT_ready"), 1) if q else C.link(m)

            def post_norm(l, which):
                n = 2 * l + which
                act.wait_ge(sem("post_mm"), 8 * n + (8 + POST_CREDIT))
                for i in range(T):
                    for c in range(2):
                        C.link(nc.scalar.activation(sq_junk[:, 0:512], bank(4 * c + i), ACT.Square,
                                                    accum_out=ssq[:, 4 * c + i:4 * c + i + 1]))
                        C.settle()
                m = nc.scalar.activation(lnv, ssq[:, 0:T], ACT.Identity, bias=0.0)
                m.then_inc(sem("post_sq"), 1)
                act.wait_ge(sem("post_sum"), n + 1)
                rsqrt_mean(ssq[:, 0:T], rstd, T).then_inc(sem("post_rstd"), 1)

            with act.Fori(0, LAYERS) as l:
                C.enter(l, "act_layer")
                pre_norm(l, 0)
                act.wait_ge(sem("layer_in"), 64 * l + 64)
                for g in range(POOL_G):
                    act.wait_ge(sem("poolw_mm"), 4 * l + (g + 1))
                    nc.scalar.activation(mixT[:, 4 + g], bank(6 + g % 2), ACT.Copy, scale=pscale[:, g:g + 1]
                                         ).then_inc(sem("poolT_ready"), 1)
                for c in range(6):
                    act.wait_ge(sem("qkT_mm"), 6 * l + (c + 1))
                    nc.scalar.activation(qkT[:, c], bank(2 + c % 4), ACT.Copy).then_inc(sem("qkT_ready"), 1)

                def soft(n):
                    nk = 2 * P if n else P
                    b = n % 2
                    act.wait_ge(sem("max_ready"), 4 * l + (n + 1))
                    for h in range(HEADS):
                        C.link(nc.scalar.activation(probs[:, b, h, 0:nk], probs[:, b, h, 0:nk], ACT.Exp,
                                                    bias=negm[:, b, h:h + 1], accum_out=rsum[:, b, h:h + 1]))
                    nc.scalar.activation(esink[:, b], den[:, b], ACT.Exp).then_inc(sem("exp_done"), 1)

                def take_probsT(n):
                    nk = 2 if n else 1
                    for g in range(4):
                        act.wait_ge(sem("probsT_mm"), 16 * l + (4 * n + g + 1))
                        nc.scalar.activation(probsT[:, 2 * g:2 * g + 2, 0:nk],
                                             bank(2 + g % 2)[:, 0:2 * nk * P].rearrange("p (h b t) -> p h b t", h=2, b=nk),
                                             ACT.Copy).then_inc(sem("probsT_ready"), 1)
                    act.wait_ge(sem("attn_mm"), 4 * l + (n + 1))
                    nc.scalar.activation(mixT[:, 0:4, n * P:(n + 1) * P],
                                         bank(n % 2).rearrange("p (k t) -> p k t", k=4), ACT.Copy
                                         ).then_inc(sem("attnT_ready"), 1)

                soft(0)
                for n in range(T):
                    if n + 1 < T:
                        soft(n + 1)
                    take_probsT(n)
                post_norm(l, 0)
                pre_norm(l, 1)
                for u in range(GU_UNITS):
                    act.wait_ge(sem("gu_mm"), GU_UNITS * l + (u + 1))
                    if u >= 2:
                        act.wait_ge(sem("actT_ready"), GU_UNITS * l + (u - 1))
                    b = 4 * (u % 2)
                    nc.scalar.activation(sig[:, u % 2], psum[:, b:b + 2], ACT.Sigmoid).then_inc(sem("sig_ready"), 1)
                post_norm(l, 1)
                C.leave(LAYERS)


            n = XT_TURN
            for i in range(T):
                act.wait_ge(sem("tr_mm"), 4 * n + i + 1)
                for q in range(2):
                    m = nc.scalar.activation(hT[:, 4 * q:4 * q + 4, i * P:(i + 1) * P],
                                             bank(2 + 2 * (i % 2) + q).rearrange("p (k t) -> p k t", k=4), ACT.Copy)
                    m.then_inc(sem("hT_ready"), 1) if q else C.link(m)
            act.wait_ge(sem("lb_shifted"), 1)
            C.link(nc.scalar.activation(lb, lb, ACT.Exp))
            nc.scalar.activation(one_lb, one_lb, ACT.Exp).then_inc(sem("lb_exp"), 1)
            act.wait_ge(sem("angles2_ready"), 1)
            C.link(nc.scalar.activation(sin2, sin_arg, ACT.Sin))
            nc.scalar.activation(cos2, cos_arg, ACT.Sin).then_inc(sem("rope2_tables"), 1)

            cross_f, cross_kf, cross_kb, cross_qb = (sigs[:, a] for a in range(4))

            def hg_gates(h, b):
                act.wait_ge(sem("kq_ready"), 8 * h - 7) if not isinstance(h, int) or h else None
                for a in range(4):
                    act.wait_ge(sem("hgp_mm"), 5 * h + (a + 1))
                    nc.scalar.activation(sigs[:, a], bank(a), ACT.Sigmoid).then_inc(sem("hg_sig"), 1)
                act.wait_ge(sem("f_ready"), h + 1)
                nc.scalar.activation(lf, sigs[:, 1:3], ACT.Ln).then_inc(sem("lf_ready"), 1)

            def hg_v(h):
                act.wait_ge(sem("hgp_mm"), 5 * h + 5)
                nc.scalar.activation(v_h, bank(4).rearrange("p (i d) -> p i d", i=T), ACT.Copy
                                     ).then_inc(sem("v_ready"), 1)

            def level_exp(h, l):
                act.wait_ge(sem("sub_ready"), 7 * h + (LEVELS - l + 1))
                nc.scalar.activation(lev_e[:, l % 2], lev_e[:, l % 2], ACT.Exp).then_inc(sem("exp_ready"), 1)

            def cross_exp(h):
                C.link(nc.scalar.activation(cross_f, cum_f, ACT.Exp))
                C.link(nc.scalar.activation(cross_kb, cumx_b, ACT.Exp))
                for i in range(T - 1):
                    ts = slice(i * P, (i + 1) * P)
                    edge = slice((i + 1) * P - 1, (i + 1) * P)
                    C.link(nc.scalar.activation(cross_kf[:, ts], cum_f[:, ts], ACT.Exp, scale=-1.0, bias=cum_f[:, edge]))
                    C.link(nc.scalar.activation(cross_qb[:, ts], cumx_b[:, ts], ACT.Exp, scale=-1.0, bias=cum_b[:, edge]))
                nc.scalar.activation(et_b, cum_b[:, P - 1:S:P], ACT.Exp).then_inc(sem("cross_ready"), 1)

            def hg_norm(h):
                act.wait_ge(sem("hgs_mm"), 12 * h + 12)
                C.link(nc.scalar.activation(rs_h, bank(6), ACT.Ln, bias=eps, scale=1.0 / P))
                C.settle()
                nc.scalar.activation(rs_h, rs_h, ACT.Exp, scale=-0.5).then_inc(sem("sum_taken"), 1)

            def hg_head(h, b, last=False):
                level_exp(h, 7)
                cross_exp(h)
                level_exp(h, 6)
                for s in range(T):
                    act.wait_ge(sem("hgs_mm"), 12 * h + (s + 1))
                    nc.scalar.activation(scoresT[:, s], bank(5 + s % 2), ACT.Copy).then_inc(sem("row_ready"), 1)
                for l in range(5, 0, -1):
                    level_exp(h, l)
                if not last:
                    hg_gates(h + 1, 1 - b)
                act.wait_ge(sem("o_mm"), h + 1)
                nc.scalar.activation(osq, bank(7), ACT.Square).then_inc(sem("osq_ready"), 1)
                if not last:
                    hg_v(h + 1)
                hg_norm(h)

            hg_gates(0, 0)
            hg_v(0)
            hg_head(0, 0)
            with act.Fori(0, HG // 2 - 1) as i:
                C.enter(i, "act_hg")
                hg_head(2 * i + 1, 1)
                hg_head(2 * i + 2, 0)
                C.leave(HG // 2 - 1)
            hg_head(HG - 1, 1, last=True)

            def ret_gates(r):
                for a in range(2):
                    act.wait_ge(sem("retp_mm"), 8 * r + 5 + a)
                    m = nc.scalar.activation(rsig[:, a], bank(6 + a), ACT.Sigmoid)
                    m.then_inc(sem("rsig_ready"), 1)

            def ret_v(r):
                for a in range(2):
                    act.wait_ge(sem("retp_mm"), 8 * r + 7 + a)
                    nc.scalar.activation(rv[:, 2 * a:2 * a + 2], bank(4 + a).rearrange("p (i d) -> p i d", i=2), ACT.Copy
                                         ).then_inc(sem("rv_ready"), 1)

            def ret_o(r):
                for a in range(2):
                    act.wait_ge(sem("ro_mm"), 2 * r + a + 1)
                    nc.scalar.activation(o_c[:, a], bank(4 + a), ACT.Copy).then_inc(sem("o_copied"), 1)
                act.wait_ge(sem("o_copied"), 2 * r + 2)
                nc.scalar.activation(o_sq, o_c, ACT.Square).then_inc(sem("rosq_ready"), 1)

            def ret_norm(r):
                act.wait_ge(sem("rsum_mm"), r + 1)
                C.link(nc.scalar.activation(rrs, bank(6), ACT.Ln, bias=eps, scale=1.0 / RDK))
                C.settle()
                nc.scalar.activation(rrs, rrs, ACT.Exp, scale=-0.5).then_inc(sem("rsum_taken"), 1)

            act.wait_ge(sem("hg_out"), HG + 1)
            ret_gates(0)
            ret_v(0)
            for r in range(RH):
                if r:
                    act.wait_ge(sem("ret_out"), r)
                ret_o(r)
                if r + 1 < RH:
                    act.wait_ge(sem("rgate_ready"), r + 1)
                    ret_gates(r + 1)
                    ret_v(r + 1)
                ret_norm(r)

            act.wait_ge(sem("ret_out"), RH)
            for s in range(16):
                act.wait_ge(sem("merge_mm"), s + 1)
                if s >= 2:
                    act.wait_ge(sem("merge_taken"), s - 1)
                nc.scalar.activation(gsig[:, s % 2], bank(2 * (s % 4)), ACT.Sigmoid).then_inc(sem("gsig_ready"), 1)

            def ln_scale(n):
                act.wait_ge(sem("ln_stats"), n + 1)
                C.link(nc.scalar.activation(lnv, mv[:, :, 1], ACT.Ln, bias=ln_eps))
                C.settle()
                nc.scalar.activation(rstd, lnv, ACT.Exp, scale=-0.5).then_inc(sem("ln_rstd"), 1)

            ln_scale(0)

            n = XT_TURN + 1
            for i in range(T):
                act.wait_ge(sem("tr_mm"), 4 * n + i + 1)
                for q in range(2):
                    m = nc.scalar.activation(hT[:, 4 * q:4 * q + 4, i * P:(i + 1) * P],
                                             bank(2 + 2 * (i % 2) + q).rearrange("p (k t) -> p k t", k=4), ACT.Copy)
                    m.then_inc(sem("hT_ready"), 1) if q else C.link(m)
            act.wait_ge(sem("gshift_ready"), 1)
            nc.scalar.activation(gexp, gexp, ACT.Exp).then_inc(sem("gexp_ready"), 1)
            act.wait_ge(sem("eshift_ready"), 1)
            nc.scalar.activation(r4[3], r4[2], ACT.Exp).then_inc(sem("eexp_ready"), 1)

            def take_gather(j, b):
                act.wait_ge(sem("gather_mm"), j + 1)
                nc.scalar.activation(xsT[:, b], psum[:, 0:2].rearrange("p a (k t) -> p (a k) t", k=4), ACT.Copy
                                     ).then_inc(sem("xs_ready"), 1)

            act.wait_ge(sem("table_ready"), 1)
            turns = act.value_load(table_i[0:1, MAX_BLOCKS:MAX_BLOCKS + 1].bitcast(I32), min_val=16, max_val=20)
            take_gather(0, 0)
            with act.Fori(0, turns) as i:
                for b in range(2):
                    j = 2 * i + b
                    act.wait_ge(sem("h_mm"), j + 1)
                    nc.scalar.activation(msig, bank(2), ACT.Sigmoid).then_inc(sem("msig_ready"), 1)
                    take_gather(j + 1, 1 - b)
                    act.wait_ge(sem("mgT_mm"), j + 1)
                    nc.scalar.activation(mgT, bank(4).rearrange("p (k t) -> p k t", k=4), ACT.Copy
                                         ).then_inc(sem("mgT_ready"), 1)
            ln_scale(1)

        @block.vector
        def _(dve):
            C = Chain(dve, sem("dve_order"))
            v = nc.vector
            dve.sem_inc(sem("mod_free"), 2)
            dve.sem_inc(sem("proj_free"), 4)
            C.link(v.memset(eps, EPS))
            C.settle()
            dve.wait_ge(sem("const_in"), 96)
            C.link(v.tensor_copy(pos_f, pos_i.bitcast(I32)))
            C.settle()
            ang, r_sin, r_cos = rt

            def reduce_angle(dst, src, tmp, quarter):
                C.link(v.tensor_scalar(tmp, src, 1.0 / TWO_PI, 0.25 * quarter,
                                       ALU.mult, ALU.add))
                C.settle()
                C.link(v.tensor_scalar(tmp, tmp, ROUND, None, ALU.add))
                C.settle()
                C.link(v.tensor_scalar(tmp, tmp, ROUND, None, ALU.subtract))
                C.settle()
                for n, part in enumerate((C1, C2, C3)):
                    C.link(v.scalar_tensor_tensor(out=dst, in0=tmp, scalar=-part, in1=dst if n else src,
                                                  op0=ALU.mult, op1=ALU.add))
                    C.settle()
                if quarter:
                    C.link(v.tensor_scalar(dst, dst, 0.5 * np.pi, None, ALU.add))
                    C.settle()
                C.link(v.tensor_scalar(dst, dst, float(np.float32(-3.1415925)), float(np.float32(3.1415925)),
                                       ALU.max, ALU.min))
                C.settle()

            for i in range(T):
                C.link(v.tensor_scalar(ang[:, i], inv1, pos_f[:, i:i + 1], None, ALU.mult))
            C.settle()
            reduce_angle(r_sin, ang, ang_tmp, 0)
            reduce_angle(r_cos, ang, ang_tmp, 1)
            v.tensor_copy(ang, r_sin).then_inc(sem("angles_ready"), 1)
            dve.wait_ge(sem("x_in"), 16)
            dve.sem_inc(sem("x_ready"), 1)

            def modulation(l, j):
                what, c = (j % 6) // 2, slice(512 * (j % 2), 512 * (j % 2) + 512)
                dve.wait_ge(sem("mod_mm"), MOD_UNITS * l + (j + 1))
                dve.wait_ge(sem(f"aux{j % 2}_in"), aux_total[j % 2] * l + aux_at[j])
                b, g = aux[:, j % 2, 0], aux[:, j % 2, 1]
                if what == 0:
                    m = v.tensor_tensor(shift[:, c], bank(j % 2), b, ALU.add)
                else:
                    dst = scale if what == 1 else (gate_m, gate_f)[j // 6]
                    C.link(v.scalar_tensor_tensor(out=dst[:, c], in0=bank(j % 2), scalar=1.0 if what == 1 else 0.0,
                                                  in1=b, op0=ALU.add, op1=ALU.add))
                    C.settle()
                    m = v.tensor_tensor(dst[:, c], dst[:, c], g, ALU.mult)
                m.then_inc(sem("mod_free"), 1)

            def pre_norm(l, which):
                n = 2 * l + which
                dve.wait_ge(sem("pre_rstd"), n + 1)
                dve.wait_ge(sem("mod_free"), MOD_UNITS * l + (8 + 6 * which))
                for i in range(T):
                    if i >= 2:
                        dve.wait_ge(sem("tr_mm"), 4 * n + (i - 1))
                    C.link(v.scalar_tensor_tensor(out=hrow[:, i % 2], in0=x[:, i], scalar=rstd[:, i:i + 1], in1=scale,
                                                  op0=ALU.mult, op1=ALU.mult))
                    C.settle()
                    v.tensor_tensor(hrow[:, i % 2], hrow[:, i % 2], shift, ALU.add).then_inc(sem("h_row"), 1)

            def post_norm(l, which):
                n = 2 * l + which
                gate = (gate_m, gate_f)[which]
                dve.wait_ge(sem("post_sq"), n + 1)
                v.tensor_tensor(ssq[:, 0:T], ssq[:, 0:T], ssq[:, T:2 * T], ALU.add).then_inc(sem("post_sum"), 1)
                dve.wait_ge(sem("post_rstd"), n + 1)
                for i in range(T):
                    for c in range(2):
                        cs = slice(512 * c, 512 * c + 512)
                        C.link(v.scalar_tensor_tensor(out=tmp_row[:, c], in0=bank(4 * c + i), scalar=rstd[:, i:i + 1],
                                                      in1=gate[:, cs], op0=ALU.mult, op1=ALU.mult))
                    C.settle()
                    m = v.tensor_tensor(x[:, i], x[:, i], tmp_row.rearrange("p a b -> p (a b)"), ALU.add)
                    m.then_inc(sem("x_ready"), 1)
                    dve.wait_ge(sem("x_ready"), 8 * l + (4 * which + i + 2))

            dve.wait_ge(sem("zeros_out"), 16 * (MAX_BLOCKS - EXPERTS))
            with dve.Fori(0, LAYERS) as l:
                C.enter(l, "dve_layer")
                for j in range(6):
                    modulation(l, j)
                pre_norm(l, 0)
                dve.wait_ge(sem("layer_in"), 64 * l + 64)
                for c in range(IN_UNITS):
                    for i in range(T):
                        dve.wait_ge(sem("proj_mm"), 16 * l + (4 * c + i + 1))
                        cs = slice(c * IN_COLS, (c + 1) * IN_COLS)
                        v.tensor_tensor(proj[:, i, cs], psum[:, 2 + i, 0:IN_COLS], b_in[:, cs], ALU.add
                                        ).then_inc(sem("proj_free"), 1)
                dve.wait_ge(sem("proj_free"), 16 * l + 20)
                dve.wait_ge(sem("rope_tables"), 1)
                for i in range(T):
                    qk = proj[:, i, 0:640].rearrange("p (h d) -> p h d", d=HD)
                    t1, t2 = qk[:, :, 0:ROT_HALF], qk[:, :, ROT_HALF:2 * ROT_HALF]
                    cs_, sn_ = (a[:, i:i + 1].to_broadcast([P, 10, ROT_HALF]) for a in (cos1, sin1))
                    r = [rope_tile(a, i) for a in range(4)]
                    C.link(v.tensor_tensor(r[0], t1, cs_, ALU.mult))
                    C.link(v.tensor_tensor(r[1], t2, sn_, ALU.mult))
                    C.link(v.tensor_tensor(r[2], t2, cs_, ALU.mult))
                    C.link(v.tensor_tensor(r[3], t1, sn_, ALU.mult))
                C.settle()
                for i in range(T):
                    qk = proj[:, i, 0:640].rearrange("p (h d) -> p h d", d=HD)
                    t1, t2 = qk[:, :, 0:ROT_HALF], qk[:, :, ROT_HALF:2 * ROT_HALF]
                    r = [rope_tile(a, i) for a in range(4)]
                    C.link(v.tensor_tensor(t1, r[0], r[1], ALU.subtract))
                    C.link(v.tensor_tensor(t2, r[2], r[3], ALU.add))
                C.settle()
                for i in range(T):
                    for b in range(2):
                        k = proj[:, i, 512:640].rearrange("p (g d) -> p g d", g=KVH)
                        m = v.tensor_copy(kdup[:, i, :, b], k)
                        m.then_inc(sem("rope_done"), 1) if i == T - 1 and b else C.link(m)
                for j in range(6, 12):
                    modulation(l, j)
                for g in range(POOL_G):
                    dve.wait_ge(sem("pool_mm"), 4 * l + (g + 1))
                    v.tensor_copy(pooled[:, g % 2], bank(2 + g % 2)).then_inc(sem("pooled_ready"), 1)

                def mask(n):
                    nk = 2 * P if n else P
                    b = n % 2
                    win = window[:, 0:2 * P] if n else window[:, P:2 * P]
                    for j in range(4):
                        dve.wait_ge(sem("score_mm"), 16 * l + (4 * n + j + 1))
                        v.scalar_tensor_tensor(
                            out=probs[:, b, 4 * (j // 2) + j % 2:4 * (j // 2) + 4:2, 0:nk],
                            in0=psum[:, 4 + j, 0:2 * nk].rearrange("p (a k) -> p a k", a=2), scalar=HD ** -0.5,
                            in1=win.rearrange("p (a k) -> p a k", a=1).to_broadcast([P, 2, nk]),
                            op0=ALU.mult, op1=ALU.add).then_inc(sem("score_free"), 1)
                    dve.wait_ge(sem("score_free"), 16 * l + (4 * n + 4))
                    C.link(v.tensor_reduce(mx[:, b], probs[:, b, :, 0:nk], AXX, ALU.max))
                    C.settle()
                    C.link(v.tensor_tensor(mx[:, b], mx[:, b], sink, ALU.max))
                    C.settle()
                    C.link(v.tensor_tensor(den[:, b], sink, mx[:, b], ALU.subtract))
                    v.tensor_scalar(negm[:, b], mx[:, b], -1.0, None, ALU.mult).then_inc(sem("max_ready"), 1)

                def normalise(n):
                    nk = 2 * P if n else P
                    b = n % 2
                    dve.wait_ge(sem("exp_done"), 4 * l + (n + 1))
                    C.link(v.tensor_tensor(den[:, b], rsum[:, b], esink[:, b], ALU.add))
                    C.settle()
                    C.link(v.reciprocal(den[:, b], den[:, b]))
                    C.settle()
                    d3 = den[:, b].rearrange("p (h a) -> p h a", a=1).to_broadcast([P, HEADS, nk])
                    v.tensor_tensor(probs[:, b, :, 0:nk], probs[:, b, :, 0:nk], d3, ALU.mult
                                    ).then_inc(sem("probs_ready"), 1)

                mask(0)
                for n in range(T):
                    if n + 1 < T:
                        mask(n + 1)
                    normalise(n)
                post_norm(l, 0)
                pre_norm(l, 1)
                for u in range(GU_UNITS):
                    b = 4 * (u % 2)
                    dve.wait_ge(sem("sig_ready"), GU_UNITS * l + (u + 1))
                    C.link(v.tensor_tensor(sig[:, u % 2], sig[:, u % 2], psum[:, b:b + 2], ALU.mult))
                    C.settle()
                    v.tensor_tensor(actT[:, 2 * u:2 * u + 2], sig[:, u % 2], psum[:, b + 2:b + 4], ALU.mult
                                    ).then_inc(sem("actT_ready"), 1)
                post_norm(l, 1)
                C.leave(LAYERS)

            dve.wait_ge(sem("const2_in"), 128)
            v.memset(ones, 1.0).then_inc(sem("ones_ready"), 1)
            C.settle()
            C.link(v.tensor_tensor(mx[:, 0], lb, one_lb, ALU.max))
            C.settle()
            C.link(v.tensor_tensor(lb, lb, mx[:, 0], ALU.subtract))
            v.tensor_tensor(one_lb, one_lb, mx[:, 0], ALU.subtract).then_inc(sem("lb_shifted"), 1)
            C.link(v.tensor_copy(pos2_f, pos2_i.bitcast(I32)))
            C.settle()
            C.link(v.tensor_scalar(ang2, pos2_f, inv2, None, ALU.mult))
            C.settle()
            reduce_angle(sin_arg, ang2, ang2_tmp, 0)
            reduce_angle(cos_arg, ang2, ang2_tmp, 1)
            v.tensor_copy(ang2_tmp, cos_arg).then_inc(sem("angles2_ready"), 1)
            dve.wait_ge(sem("lb_exp"), 1)
            C.link(v.tensor_tensor(mx[:, 0], lb, one_lb, ALU.add))
            C.settle()
            C.link(v.reciprocal(mx[:, 0], mx[:, 0]))
            C.settle()
            C.link(v.tensor_tensor(lb, one_lb, mx[:, 0], ALU.mult))
            C.settle()
            C.link(v.tensor_scalar(one_lb, lb, -1.0, 1.0, ALU.mult, ALU.add))
            C.settle()
            C.link(v.tensor_scalar(lb, lb, 2.0 ** -60, None, ALU.max))
            dve.wait_ge(sem("rope2_tables"), 1)
            dve.sem_inc(sem("hg_out"), 1)
            dve.sem_inc(sem("sum_taken"), 1)
            C.settle()

            cross_f, cross_kf, cross_kb, cross_qb = (sigs[:, a] for a in range(4))

            def col(a, h):
                return a[:, bass.ds(h, 1)] if not isinstance(h, int) else a[:, h:h + 1]

            def hg_gates(h, b):
                dve.wait_ge(sem("hg_sig"), 4 * h + 1)
                v.tensor_tensor(q_h, sigs[:, 0], bank(0), ALU.mult).then_inc(sem("hgp_taken"), 1)
                dve.wait_ge(sem("hg_sig"), 4 * h + 3)
                v.tensor_scalar(sigs[:, 1:3], sigs[:, 1:3], col(one_lb, h), col(lb, h), ALU.mult, ALU.add
                                ).then_inc(sem("f_ready"), 1)
                dve.wait_ge(sem("hg_sig"), 4 * h + 4)
                v.tensor_tensor(gate_h[:, b], sigs[:, 3], bank(3), ALU.mult).then_inc(sem("hgp_taken"), 1)
                dve.wait_ge(sem("f_ready"), h + 1)
                C.link(v.tensor_scalar(k_h, sigs[:, 1:3], -1.0, 1.0, ALU.mult, ALU.add))
                dve.wait_ge(sem("lf_ready"), h + 1)
                C.link(v.tensor_tensor_scan(cum_f, restart, lf[:, 0], 0.0, ALU.mult, ALU.add))
                C.link(v.tensor_tensor_scan(cum_b, restart, lf[:, 1], 0.0, ALU.mult, ALU.add))
                C.settle()
                C.link(v.tensor_tensor(cumx_b, cum_b, lf[:, 1], ALU.subtract))
                C.settle()

            def halves(a, l):
                return a.rearrange("p (n h b) -> p n h b", h=2, b=2 ** (l - 1))

            def level_sub(h, l):
                n, hb = S >> l, 2 ** (l - 1)
                if l <= LEVELS - 2:
                    dve.wait_ge(sem("kq_ready"), 8 * h + (LEVELS - 1 - l))
                cf, cx = halves(cum_f, l), halves(cumx_b, l)
                eq, ek = halves(lev_e[:, l % 2, 0], l), halves(lev_e[:, l % 2, 1], l)
                ref_f = cf[:, :, 0, hb - 1:hb].to_broadcast([P, n, hb])
                ref_b = cx[:, :, 1, 0:1].to_broadcast([P, n, hb])
                C.link(v.tensor_tensor(eq[:, :, 1], cf[:, :, 1], ref_f, ALU.subtract))
                C.link(v.tensor_tensor(eq[:, :, 0], ref_b, cx[:, :, 0], ALU.subtract))
                C.link(v.tensor_tensor(ek[:, :, 0], ref_f, cf[:, :, 0], ALU.subtract))
                v.tensor_tensor(ek[:, :, 1], cx[:, :, 1], ref_b, ALU.subtract).then_inc(sem("sub_ready"), 1)

            def level_mult(h, l):
                dve.wait_ge(sem("exp_ready"), 7 * h + (LEVELS - l + 1))
                if l == 5:
                    dve.wait_ge(sem("hgs_mm"), 12 * h + 4)
                elif l < 5:
                    dve.wait_ge(sem("hgs_mm"), 12 * h + (9 - l))
                e, o = lev_e[:, l % 2], lev_qk[:, l % 2]
                C.link(v.tensor_tensor(o[:, 0], q_h, e[:, 0], ALU.mult))
                C.link(v.tensor_tensor(halves(o[:, 1], l)[:, :, 0], halves(k_h[:, 0], l)[:, :, 0],
                                       halves(e[:, 1], l)[:, :, 0], ALU.mult))
                m = v.tensor_tensor(halves(o[:, 1], l)[:, :, 1], halves(k_h[:, 1], l)[:, :, 1],
                                    halves(e[:, 1], l)[:, :, 1], ALU.mult)
                C.link(m) if l == LEVELS else m.then_inc(sem("kq_ready"), 1)

            def tiles(a):
                return a.rearrange("p (i t) -> p i t", i=T)

            def cross_mult(h):
                dve.wait_ge(sem("cross_ready"), h + 1)
                q, kf, kb = tiles(q_h), tiles(k_h[:, 0]), tiles(k_h[:, 1])
                ef, ekf, ekb, eqb = tiles(cross_f), tiles(cross_kf), tiles(cross_kb), tiles(cross_qb)
                C.link(v.tensor_tensor(xf_q[:, 0:3:2], q[:, 1:3], ef[:, 1:3], ALU.mult))
                C.link(v.tensor_tensor(xf_q[:, 1], q[:, 3], ef[:, 3], ALU.mult))
                C.link(v.tensor_tensor(xf_k[:, 0:2], kf[:, 0:3:2], ekf[:, 0:3:2], ALU.mult))
                C.link(v.tensor_tensor(xf_k[:, 3], kf[:, 1], ekf[:, 1], ALU.mult))
                C.link(v.tensor_tensor(xb_q[:, 0:2], q[:, 0:3:2], eqb[:, 0:3:2], ALU.mult))
                C.link(v.tensor_tensor(xb_q[:, 3], q[:, 1], eqb[:, 1], ALU.mult))
                C.link(v.tensor_tensor(xb_k[:, 0:2], kb[:, 1:4:2], ekb[:, 1:4:2], ALU.mult))
                C.link(v.tensor_tensor(xb_k[:, 2], kb[:, 2], ekb[:, 2], ALU.mult))
                C.settle()
                C.link(v.tensor_scalar(xf_q[:, 3], xf_q[:, 1], ef[:, 2, P - 1:P], None, ALU.mult))
                C.link(v.tensor_scalar(xf_k[:, 2], xf_k[:, 0], ef[:, 1, P - 1:P], None, ALU.mult))
                C.link(v.tensor_scalar(xb_q[:, 2], xb_q[:, 0], et_b[:, 1:2], None, ALU.mult))
                v.tensor_scalar(xb_k[:, 3], xb_k[:, 1], et_b[:, 2:3], None, ALU.mult).then_inc(sem("kq_ready"), 1)

            def level_take(h, l):
                dve.wait_ge(sem("hgs_mm"), 12 * h + (11 - l))
                dve.wait_ge(sem("row_ready"), 4 * h + 4)
                if l < LEVELS - 1:
                    dve.wait_ge(sem("level_taken"), 7 * h + (LEVELS - 1 - l))
                m = masks[:, l:l + 1].bitcast(I32).to_broadcast([P, T, P])
                dve.sem_inc(sem("take_order"), 1)
                v.copy_predicated(diag, m, tiles(psum[:, 5 + (LEVELS - 1 - l) % 2])).then_inc(sem("level_taken"), 1)

            def hg_out(h, b):
                dve.wait_ge(sem("sum_taken"), h + 2)
                C.link(v.tensor_tensor(rs_h, rs_h, bank(7), ALU.mult))
                C.settle()
                dst = o_hgT[:, bass.ds(h, 1)] if not isinstance(h, int) else o_hgT[:, h:h + 1]
                v.scalar_tensor_tensor(out=dst.rearrange("p a s -> p (a s)"), in0=rs_h, scalar=col(hg_g, h),
                                       in1=gate_h[:, b], op0=ALU.mult, op1=ALU.mult).then_inc(sem("hg_out"), 1)

            def hg_head(h, b, last=False):
                level_sub(h, 7)
                level_sub(h, 6)
                level_mult(h, 7)
                cross_mult(h)
                level_sub(h, 5)
                level_mult(h, 6)
                for l in range(5, 0, -1):
                    if l > 1:
                        level_sub(h, l - 1)
                    level_mult(h, l)
                    level_take(h, l + 1)
                dve.wait_ge(sem("hgs_mm"), 12 * h + 9)
                v.tensor_tensor(lev_qk[:, 0, 1], k_h[:, 0], k_h[:, 1], ALU.add).then_inc(sem("kq_ready"), 1)
                level_take(h, 1)
                level_take(h, 0)
                if not last:
                    hg_gates(h + 1, 1 - b)
                hg_out(h, b)

            hg_gates(0, 0)
            hg_head(0, 0)
            with dve.Fori(0, HG // 2 - 1) as i:
                C.enter(i, "dve_hg")
                hg_head(2 * i + 1, 1)
                hg_head(2 * i + 2, 0)
                C.leave(HG // 2 - 1)
            hg_head(HG - 1, 1, last=True)

            both = lambda a: a.rearrange("p (a s) -> p a s", a=1).to_broadcast([P, 2, S])

            def ret_rope(r):
                dve.wait_ge(sem("hg_out"), HG + 1)
                if r:
                    dve.wait_ge(sem("rs_mm"), 4 * r)
                for a, dst in ((0, rq), (1, rk)):
                    dve.wait_ge(sem("retp_mm"), 8 * r + 2 * a + 2)
                    eo = psum[:, 2 * a:2 * a + 2]
                    C.link(v.tensor_tensor(rope_a, eo, both(cos2), ALU.mult))
                    C.link(v.tensor_tensor(rope_b, eo, both(sin2), ALU.mult))
                    C.settle()
                    C.link(v.tensor_tensor(dst[:, 0], rope_a[:, 0], rope_b[:, 1], ALU.subtract))
                    v.tensor_tensor(dst[:, 1], rope_b[:, 0], rope_a[:, 1], ALU.add).then_inc(sem("rope2_done"), 1)
                    dve.wait_ge(sem("rope2_done"), 2 * r + a + 1)

            def ret_gate(r):
                for a in range(2):
                    dve.wait_ge(sem("rsig_ready"), 2 * r + a + 1)
                    m = v.tensor_tensor(rgate[:, r % 2, a], rsig[:, a], bank(6 + a), ALU.mult)
                    m.then_inc(sem("rgate_ready"), 1) if a else C.link(m)

            def ret_decay(r):
                dve.wait_ge(sem(f"strip{r % 2}_in"), 16 * (r // 2 + 1))
                for s in range(T):
                    dve.wait_ge(sem("rs_mm"), 4 * r + s + 1)
                    c = (3 - s) * P
                    v.tensor_tensor(rscT[:, s], bank(s), strip[:, r % 2, c:c + S], ALU.mult
                                    ).then_inc(sem("rsc_ready"), 1)

            def ret_out(r):
                dve.wait_ge(sem("rsum_taken"), r + 1)
                C.link(v.tensor_tensor(o_c, o_c, both(rrs), ALU.mult))
                C.settle()
                for a in range(2):
                    m = v.scalar_tensor_tensor(out=o_retT[:, 2 * r + a], in0=o_c[:, a],
                                               scalar=ret_g[:, 2 * r + a:2 * r + a + 1], in1=rgate[:, r % 2, a],
                                               op0=ALU.mult, op1=ALU.mult)
                    m.then_inc(sem("ret_out"), 1) if a else C.link(m)

            ret_rope(0)
            ret_gate(0)
            for r in range(RH):
                ret_decay(r)
                if r + 1 < RH:
                    ret_rope(r + 1)
                    ret_gate(r + 1)
                ret_out(r)

            dve.wait_ge(sem("ret_out"), RH)
            for s in range(16):
                dve.wait_ge(sem("gsig_ready"), s + 1)
                dst = mergedT[:, 4 * (s // 8) + s % 4]
                if (s // 4) % 2 == 0:
                    v.tensor_tensor(dst, gsig[:, s % 2], bank(2 * (s % 4) + 1), ALU.mult).then_inc(sem("merge_taken"), 1)
                else:
                    dve.wait_ge(sem("merge_taken"), s)
                    C.link(v.tensor_tensor(ytmp[:, s % 2], gsig[:, s % 2], bank(2 * (s % 4) + 1), ALU.mult))
                    C.settle()
                    v.tensor_tensor(dst, dst, ytmp[:, s % 2], ALU.add).then_inc(sem("merge_taken"), 1)

            def layer_norm(n, done, out_sem):
                for i in range(T):
                    for c in range(2):
                        C.link(v.bn_stats(bn[:, i, c], x[:, i, 512 * c:512 * c + 512]))
                C.settle()
                for i in range(T):
                    m = v.bn_aggr(mv[:, i], bn[:, i])
                    m.then_inc(sem("ln_stats"), 1) if i == T - 1 else C.link(m)
                dve.wait_ge(sem("ln_rstd"), n + 1)
                dve.wait_ge(sem(f"ln{n}_in"), 32)
                for i in range(T):
                    C.link(v.tensor_scalar(x[:, i], x[:, i], mv[:, i, 0:1], rstd[:, i:i + 1], ALU.subtract, ALU.mult))
                C.settle()
                for i in range(T):
                    C.link(v.tensor_tensor(x[:, i], x[:, i], ln_g[:, n], ALU.mult))
                C.settle()
                for i in range(T):
                    v.tensor_tensor(x[:, i], x[:, i], ln_b[:, n], ALU.add).then_inc(out_sem, 1)

            C.link(v.memset(ln_eps, LN_EPS))
            dve.wait_ge(sem("mix2_mm"), 16)
            for i in range(T):
                C.link(v.scalar_tensor_tensor(out=x[:, i], in0=x[:, i], scalar=ALPHA,
                                              in1=psum[:, 2 * i:2 * i + 2].rearrange("p a b -> p (a b)"),
                                              op0=ALU.mult, op1=ALU.add))
            C.settle()
            layer_norm(0, None, sem("x1_ready"))

            def bc(a, *shape):
                return a.to_broadcast([P, *shape])

            def last(a, n):
                return a.rearrange("p (t a) -> p t a", a=1).to_broadcast([P, T, n])

            def over_tiles(a, n):
                return a.rearrange("p (a n) -> p a n", a=1).to_broadcast([P, T, n])

            def first_max(onehot, vals, vmax, n, tmp, least):
                C.link(v.tensor_reduce(vmax, vals, AXX, ALU.max))
                C.settle()
                C.link(v.tensor_tensor(onehot, vals, last(vmax, n), ALU.is_equal))
                C.settle()
                C.link(v.scalar_tensor_tensor(out=tmp, in0=onehot, scalar=-64.0, in1=over_tiles(iota[:, 0:n], n),
                                              op0=ALU.mult, op1=ALU.add))
                C.settle()
                C.link(v.tensor_reduce(least, tmp, AXX, ALU.min))
                C.settle()
                C.link(v.tensor_tensor(onehot, tmp, last(least, n), ALU.is_equal))
                C.settle()

            dve.wait_ge(sem("route_in"), 96)
            dve.wait_ge(sem("logits_mm"), 1)
            C.link(v.tensor_tensor(logits, psum[:, 0, 0:T * NL].rearrange("p (t n) -> p t n", t=T), over_tiles(bias_r, NL), ALU.add))
            C.settle()
            lgr, ler = logits[:, :, 0:GROUPS], logits[:, :, GROUPS:NL].rearrange("p t (g e) -> p t g e", g=GROUPS)
            gmax, least, e_diff, e_exp, e1, e2 = r4
            first_max(oh_g, lgr, gmax, GROUPS, gexp, least)
            v.tensor_tensor(gexp, lgr, last(gmax, GROUPS), ALU.subtract).then_inc(sem("gshift_ready"), 1)
            for i in range(T):
                og = oh_g[:, i].rearrange("p (g a) -> p g a", a=1).to_broadcast([P, GROUPS, PER_GROUP])
                C.link(v.tensor_tensor(picked[:, i], ler[:, i], og, ALU.mult))
            C.settle()
            for i in range(T):
                C.link(v.tensor_reduce(es[:, i], picked[:, i].rearrange("p g e -> p e g"), AXX, ALU.add))
            C.settle()
            first_max(oh_e[:, 0], es, e1, PER_GROUP, t8, least)
            C.link(v.scalar_tensor_tensor(out=es, in0=oh_e[:, 0], scalar=NEG, in1=es, op0=ALU.mult, op1=ALU.add))
            C.settle()
            first_max(oh_e[:, 1], es, e2, PER_GROUP, t8, least)
            v.tensor_tensor(e_diff, e2, e1, ALU.subtract).then_inc(sem("eshift_ready"), 1)
            for k in range(2):
                for i in range(T):
                    og = oh_g[:, i].rearrange("p (g a) -> p g a", a=1).to_broadcast([P, GROUPS, PER_GROUP])
                    oe = oh_e[:, k, i].rearrange("p (a e) -> p a e", a=1).to_broadcast([P, GROUPS, PER_GROUP])
                    C.link(v.tensor_tensor(m_k[:, k, i].rearrange("p (g e) -> p g e", g=GROUPS), og, oe, ALU.mult))
            C.settle()
            v.tensor_tensor(m_sum, m_k[:, 0], m_k[:, 1], ALU.add).then_inc(sem("onehots_ready"), 1)
            dve.wait_ge(sem("gexp_ready"), 1)
            C.link(v.tensor_reduce(gmax, gexp, AXX, ALU.add))
            dve.wait_ge(sem("eexp_ready"), 1)
            C.link(v.tensor_scalar(e1, e_exp, 1.0, None, ALU.add))
            C.settle()
            C.link(v.tensor_tensor(e1, e1, gmax, ALU.mult))
            C.settle()
            C.link(v.reciprocal(wts[:, 0], e1))
            C.settle()
            C.link(v.tensor_tensor(wts[:, 1], wts[:, 0], e_exp, ALU.mult))
            C.link(v.tensor_scalar(base_e, iota[:, 0:EXPERTS], float(P), None, ALU.mult))
            dve.wait_ge(sem("ranks_mm"), 1)
            C.link(v.tensor_copy(rank, psum[:, 1, 0:T * EXPERTS].rearrange("p (t e) -> p t e", t=T)))
            C.link(v.tensor_copy(cnt, psum[:, 1, T * EXPERTS:(T + 1) * EXPERTS]))
            C.settle()
            C.link(v.tensor_scalar(extra, cnt, float(P), None, ALU.is_gt))
            for m in (2, 3):
                C.settle()
                C.link(v.scalar_tensor_tensor(out=extra, in0=cnt, scalar=float(m * P), in1=extra,
                                              op0=ALU.is_gt, op1=ALU.add))
            C.settle()
            C.link(v.tensor_tensor_scan(ends, ones[:, 0:EXPERTS], extra, 0.0, ALU.mult, ALU.add))
            C.settle()
            C.link(v.tensor_tensor(over_d, ends, extra, ALU.subtract))
            C.settle()
            C.link(v.tensor_scalar(over_d, over_d, float(EXPERTS - 1), float(P), ALU.add, ALU.mult))
            C.settle()
            C.link(v.tensor_tensor(over_d, over_d, base_e, ALU.subtract))
            C.link(v.tensor_scalar(ge, rank, float(P), None, ALU.is_ge))
            C.settle()
            C.link(v.tensor_tensor(ge, ge, over_tiles(over_d, EXPERTS), ALU.mult))
            C.link(v.tensor_tensor(rank, rank, over_tiles(base_e, EXPERTS), ALU.add))
            C.settle()
            C.link(v.tensor_tensor(rank, rank, ge, ALU.add))
            C.settle()
            for k in range(2):
                C.link(v.tensor_tensor(m_k[:, k], m_k[:, k], rank, ALU.mult))
            C.settle()
            for k in range(2):
                C.link(v.tensor_reduce(slot_f[:, k], m_k[:, k], AXX, ALU.add))
            C.settle()
            C.link(v.tensor_copy(slot_i.bitcast(I32), slot_f))
            C.link(v.tensor_copy(table_f[:, 0:EXPERTS], iota[:, 0:EXPERTS]))
            C.link(v.tensor_tensor(cmp8, bc(ends.rearrange("p (a e) -> p a e", a=1), 8, EXPERTS),
                                   bc(iota[:, 0:8].rearrange("p (b a) -> p b a", a=1), 8, EXPERTS), ALU.is_le))
            C.settle()
            C.link(v.tensor_reduce(table_f[:, EXPERTS:MAX_BLOCKS], cmp8, AXX, ALU.add))
            C.link(v.tensor_scalar(table_f[:, MAX_BLOCKS:], ends[:, EXPERTS - 1:EXPERTS], 0.0, float(EXPERTS // 2),
                                   ALU.is_gt, ALU.add))
            for m in (2, 4, 6):
                C.settle()
                C.link(v.scalar_tensor_tensor(out=table_f[:, MAX_BLOCKS:], in0=ends[:, EXPERTS - 1:EXPERTS], scalar=float(m),
                                              in1=table_f[:, MAX_BLOCKS:], op0=ALU.is_gt, op1=ALU.add))
            C.settle()
            C.link(v.tensor_scalar(table_f[:, 0:MAX_BLOCKS], table_f[:, 0:MAX_BLOCKS], float(EXPERTS - 1), None, ALU.min))
            C.settle()
            v.tensor_copy(table_i.bitcast(I32), table_f).then_inc(sem("table_ready"), 1)

            def select(j, b):
                for i in range(T):
                    M.link(v.tensor_scalar(sel[:, b, i], iota_b, slot_f[:, 0, i:i + 1], None, ALU.is_equal))
                M.settle()
                for i in range(T):
                    m = v.scalar_tensor_tensor(out=sel[:, b, i], in0=iota_b, scalar=slot_f[:, 1, i:i + 1],
                                               in1=sel[:, b, i], op0=ALU.is_equal, op1=ALU.add)
                    m.then_inc(sem("sel_ready"), 1) if i == T - 1 else M.link(m)
                dve.wait_ge(sem("sel_ready"), j + 1)
                M.link(v.tensor_scalar(iota_b, iota_b, float(P), None, ALU.add))
                M.settle()

            M = Chain(dve, sem("moe_order"))
            C.link(v.tensor_copy(iota_b, iota))
            C.settle()
            dve.wait_ge(sem("table_ready"), 1)
            turns = dve.value_load(table_i[0:1, MAX_BLOCKS:MAX_BLOCKS + 1].bitcast(I32), min_val=16, max_val=20)
            dve.sem_inc(sem("y_free"), 1)
            select(0, 0)
            with dve.Fori(0, turns) as i:
                M.enter(i, "dve_moe")
                for b in range(2):
                    j = 2 * i + b
                    select(j + 1, 1 - b)
                    dve.wait_ge(sem("msig_ready"), j + 1)
                    M.link(v.tensor_tensor(mg, msig, bank(2), ALU.mult))
                    M.settle()
                    v.tensor_tensor(mg, mg, bank(3), ALU.mult).then_inc(sem("mg_ready"), 1)
                    dve.wait_ge(sem("y_mm"), j + 1)
                    dve.wait_ge(sem("ysb_free"), j + 1)
                    v.tensor_copy(ysb[:, b].rearrange("p (a n) -> p a n", a=2), psum[:, 5:7]
                                  ).then_inc(sem("y_taken"), 1)
                    dve.wait_ge(sem("y_taken"), j + 1)
                    dve.sem_inc(sem("y_free"), 1)
                M.leave(0)
            for i in range(T):
                dve.wait_ge(sem(f"rows{i}_in"), 32)
                C.link(v.tensor_scalar(yg[0][i], yg[0][i], wts[:, 0, i:i + 1], None, ALU.mult))
                C.settle()
                C.link(v.scalar_tensor_tensor(out=yg[0][i], in0=yg[1][i], scalar=wts[:, 1, i:i + 1], in1=yg[0][i],
                                              op0=ALU.mult, op1=ALU.add))
                C.settle()
                C.link(v.scalar_tensor_tensor(out=x[:, i], in0=x[:, i], scalar=ALPHA, in1=yg[0][i],
                                              op0=ALU.mult, op1=ALU.add))
            C.settle()
            layer_norm(1, None, sem("x2_ready"))


def kernel(**inputs):
    import concourse.bacc as _bacc
    from concourse.bass_utils import run_bass_kernel_spmd as _run

    nc = _bacc.Bacc("TRN2", target_bir_lowering=False, num_devices=1)
    arrays, A, K = {}, {}, {}
    for name, a in inputs.items():
        a = np.ascontiguousarray(a)
        arrays["in_" + name] = a
        A[name] = nc.dram_tensor("in_" + name, a.shape, mybir.dt.from_np(a.dtype), kind="ExternalInput").ap()
    for name, a in shape_constants().items():
        arrays["const_" + name] = a
        K[name] = nc.dram_tensor("const_" + name, a.shape, F32, kind="ExternalInput").ap()
    out = nc.dram_tensor("out", (1, S, D), F32, kind="ExternalOutput").ap()
    build(nc, A, K, out)
    r = _run(nc, [arrays], core_ids=[0])
    return r.results[0]["out"]
```

```python
from contextlib import ExitStack

import concourse.bass as bass
import concourse.mybir as mybir
import numpy as np
from concourse.alu_op_type import AluOpType as ALU

F32 = mybir.dt.float32
I32 = mybir.dt.int32
F32R = mybir.dt.float32r
ACT = mybir.ActivationFunctionType
AXX = mybir.AxisListType.X

P = 128
D = 1024
KD = D // P
S = 512
T = S // P
LAYERS = 2
HEADS, HD, KVH, GROUP = 8, 64, 2, 4
QKV = HEADS * HD + 2 * KVH * HD
POOL_G = 4
IN_W = QKV + 512
FF = 2816
KF = FF // P
ROT_HALF = 8
EPS = 1e-6
NEG = -1e30
POOL_WINDOWS = (2, 4, 8, 16)

RING = 4
SLOT = 4096
MOD_UNITS = 12
IN_UNITS = 4
IN_COLS = IN_W // IN_UNITS
OUT_UNITS = 2
GU_UNITS = 11
DOWN_UNITS = ((0, 3), (3, 3), (6, 3), (9, 3), (12, 3), (15, 3), (18, 4))
GU_PIECES = 4 * GU_UNITS
MLP_PIECES = GU_PIECES + KF
LAYER_UNITS = MOD_UNITS + IN_UNITS + OUT_UNITS + GU_UNITS + len(DOWN_UNITS)
U_MOD_M, U_IN = 0, 6
U_MOD_F = U_IN + IN_UNITS
U_OUT = U_MOD_F + 6
U_GU = U_OUT + OUT_UNITS
U_DOWN = U_GU + GU_UNITS

HG = 8
RH, RDK = 4, 256
LEVELS = 7
ALPHA = 2.0 ** 0.25
RMS_EPS, LN_EPS = 1e-6, 1e-5
COL_Q, COL_F, COL_FB, COL_V, COL_G = 0, 1024, 2048, 3072, 4096
COL_RQ, COL_RK, COL_RV, COL_RG, COL_GA, COL_GB = 5120, 6144, 7168, 8192, 9216, 10240
GROUPS, PER_GROUP, EXPERTS, DE = 4, 8, 32, 512
NL = GROUPS + EXPERTS
TOKENS_PER_BLOCK = P
MAX_BLOCKS = 40
XT_TURN = 2 * LAYERS

TURN = {"dve_layer": 91, "act_layer": 68, "dve_hg": 104, "act_hg": 18, "dve_moe": 16}

TWO_PI = 2.0 * np.pi
C1 = 6.28125
C2 = float(np.float32(np.round((TWO_PI - C1) * 2.0**20) / 2.0**20))
C3 = float(np.float32(TWO_PI - C1 - C2))
ROUND = 1.5 * 2.0**23


DOWN_CREDIT, POST_CREDIT = len(DOWN_UNITS) - 1, 16


def unit_done(u):
    if u < 0:
        name, per_layer, count = unit_done(u + LAYER_UNITS)
        return name, per_layer, count - per_layer
    if U_MOD_M <= u < U_IN:
        return "mod_mm", MOD_UNITS, u + 1
    if U_IN <= u < U_MOD_F:
        return "proj_mm", 16, 4 * (u - U_IN + 1)
    if U_MOD_F <= u < U_OUT:
        return "mod_mm", MOD_UNITS, 6 + u - U_MOD_F + 1
    if U_OUT <= u < U_GU:
        return "post_mm", 16, POST_CREDIT + 4 * (u - U_OUT + 1)
    if U_GU <= u < U_DOWN:
        return "gu_mm", GU_UNITS, u - U_GU + 1
    if u < LAYER_UNITS - 1:
        return "down_mm", len(DOWN_UNITS) - 1, DOWN_CREDIT + u - U_DOWN + 1
    return "post_mm", 16, POST_CREDIT + 16


PIECES = 4
PIECE = 1024


class Chain:

    def __init__(self, eng, sem):
        self.eng, self.sem, self.base, self.n, self.turn = eng, sem, 0, 0, 0

    def link(self, ins):
        ins.then_inc(self.sem, 1)
        self.n += 1
        return ins

    def settle(self):
        self.eng.wait_ge(self.sem, self.turn + (self.base + self.n))

    def enter(self, i, name):
        self.base += self.n
        self.n, self.turn, self.name = 0, i * TURN[name], name

    def leave(self, turns):
        assert self.n == TURN[self.name], f"TURN[{self.name!r}] is {self.n}"
        self.base += turns * self.n
        self.n, self.turn = 0, 0


def shape_constants():
    c = {}
    c["ident"] = np.eye(P, dtype=np.float32)
    q, k = np.arange(P)[:, None], np.arange(P)[None, :]
    prev = np.where(k > q, 0.0, NEG)
    cur = np.where(k <= q, 0.0, NEG)
    c["window"] = np.concatenate([prev, cur], 1).astype(np.float32)
    pool = np.zeros((P, POOL_G, 3, P), np.float32)
    s, t = np.arange(P)[:, None], np.arange(P)[None, :]
    for g, w in enumerate(POOL_WINDOWS):
        here = (s <= t) & (s > t - w)
        pool[:, g, 0] = here / np.float32(w) - (s == t)
        pool[:, g, 1] = (s - P > t - w) / np.float32(w)
        pool[:, g, 2] = here / np.minimum(t + 1.0, w).astype(np.float32) - (s == t)
    c["pool"] = pool.reshape(P, -1)
    inv = (np.float32(500000.0) ** (-np.arange(0, 16, 2, dtype=np.float32) / 16)).astype(np.float32)
    c["inv1"] = np.broadcast_to(inv, (P, ROT_HALF)).copy()
    a, b = np.arange(P)[:, None], np.arange(P)[None, :]
    masks = [a == b] + [(a >> l == b >> l) & (a >> (l - 1) != b >> (l - 1)) for l in range(1, LEVELS)]
    c["masks"] = np.stack(masks, 1).astype(np.float32).reshape(P, -1)
    c["restart"] = np.tile((np.arange(S) % P != 0).astype(np.float32), (P, 1))
    half = RDK // 2
    inv = 1.0 / (np.float32(10000.0) ** np.linspace(0.0, 1.0, half, dtype=np.float32))
    c["inv2"] = inv.astype(np.float32).reshape(P, 1)
    gamma = 1.0 - 2.0 ** (-5.0 - np.arange(RH, dtype=np.float64))
    dist = np.abs(np.arange(S + 3 * P)[None, :] - 3 * P - np.arange(P)[:, None])
    strip = gamma[:, None, None] ** dist[None] * np.where(dist == 0, 2.0, 1.0) * RDK ** -0.5
    c["iota"] = np.tile(np.arange(P, dtype=np.float32), (P, 1))
    c["before"] = (np.arange(P)[:, None] < np.arange(P)[None, :]).astype(np.float32)
    c["decay"] = strip.astype(np.float32)
    return c


def build(nc, A, K, out, stop=None):
    with ExitStack() as ctx:
        sems = {}

        def sem(name):
            if name not in sems:
                sems[name] = ctx.enter_context(nc.semaphore(name))
            return sems[name]

        arena_size = 53200
        arena_at = (nc.sbuf_base + 31) // 32 * 32
        arena = ctx.enter_context(nc.sbuf_tensor("arena", [P, arena_size], F32))
        top = [0]

        def view(memory, at, shape):
            names = "abcd"[:len(shape)]
            return memory[:, at:at + int(np.prod(shape))].rearrange(
                f"p ({' '.join(names)}) -> p {' '.join(names)}", **dict(zip(names[1:], shape[1:])))

        def view_r(at, shape):
            n = int(np.prod(shape))
            part = nc.alloc_sbuf_tensor_at(f"split_{at}_{n}", [P, n], F32R, offset=arena_at + 4 * at)
            return view(part, 0, shape)

        def take(*shape):
            at = top[0]
            top[0] += int(np.prod(shape))
            assert top[0] <= arena_size, top[0]
            return view(arena, at, shape)

        def align():
            top[0] = (top[0] + 7) // 8 * 8
            return top[0]

        def take_split(*shape):
            at = align()
            take(2, *shape)
            return view_r(at, (2, *shape))

        psum = ctx.enter_context(nc.psum_tensor("psum", [P, 8, 512], F32))

        def bank(b):
            return psum[:, b, :]

        ring = [take(SLOT) for _ in range(RING)]
        x = take(T, D)
        hT_at = align()
        hT = take(KD, S)
        mixT = hT
        ident = take(P)
        eps = take(1)
        ln_eps = take(1)
        lnv, rstd = take(T), take(T)
        mx = take(2, HEADS)
        small_top = align()
        shift_at = top[0]
        shift, scale, gate_m, gate_f = take(D), take(D), take(D), take(D)
        region = top[0]
        proj = take(T, IN_W)
        qkT = take(6, S)
        kdup = take(T, 2, 2, HD)
        probs = take(2, HEADS, 2 * P)
        probsT = take(HEADS, 2, P)
        pooled = take(2, S)
        mixer_top = top[0]
        top[0] = region
        actT = take(KF, S)
        sig = take(2, 2, 512)
        hrow_at = align()
        hrow = take(2, D)
        tmp_row = take(2, 512)
        sq_junk = hrow[:, 0]
        top[0] = mixer_top
        window = take(2 * P)
        poolm = take(POOL_G, 3, P)
        inv1 = take(ROT_HALF)
        pos_i = take(T)
        pos_f = take(T)
        cos1, sin1 = take(T, ROT_HALF), take(T, ROT_HALF)
        rt = [take(T, ROT_HALF) for _ in range(3)]
        rope_flat = probs.rearrange("p a b c -> p (a b c)")

        def rope_tile(a, i):
            n = 10 * ROT_HALF
            return rope_flat[:, (T * a + i) * n:(T * a + i + 1) * n].rearrange("p (h d) -> p h d", h=10)

        ang_tmp = take(T, ROT_HALF)
        aux = take(2, 2, 512)
        b_in_at = align()
        b_in = take(IN_W)
        poolw = take(POOL_G, P)
        top[0] = b_in_at + 4 * S
        sink = take(HEADS)
        pscale = take(POOL_G)
        crep = take(KD, P)
        ccol = take(KD)
        csil = take(KD)
        ssq = take(8)
        negm, den, esink, rsum = (take(2, HEADS) for _ in range(4))

        hT_hi = view_r(hT_at, (KD, S))
        hT_lo = [view_r(shift_at + 2 * D, (2, S)), view_r(hrow_at + 2 * D, (2, S)), view_r(b_in_at, (4, S))]
        hT_lo_k = ((0, 2), (2, 2), (4, 4))
        mlp_pieces = [view_r(at, (2, PIECE)) for at in (shift_at, hrow_at)]
        act_pieces = [view_r(hT_at + 2 * S * b, (2, S)) for b in range(2)]

        def hT_part(a, k):
            return hT_hi[:, k] if a == 0 else [lo[:, c] for lo, (_, n) in zip(hT_lo, hT_lo_k) for c in range(n)][k]

        top[0] = small_top
        o_hgT = take(HG, S)
        masks = take(LEVELS, P)
        restart = take(S)
        ones = take(P)
        inv2 = take(1)
        lb, one_lb = take(HG), take(HG)
        hg_g, ret_g = take(HG), take(2 * RH)
        cos2, sin2 = take(S), take(S)
        heads_top = align()
        sigs = take(4, S)
        q_h = take(S)
        k_h = take(2, S)
        lf = take(2, S)
        cum_f, cum_b, cumx_b = take(S), take(S), take(S)
        gate_h = take(2, S)
        v_h = take(T, P)
        lev_e = take(2, 2, S)
        lev_qk = take(2, 2, S)
        xf_q, xf_k, xb_q, xb_k = (take(4, P) for _ in range(4))
        et_b = take(T)
        scoresT = take(T, S)
        osq, rs_h = take(S), take(S)
        diag = bass.AP(scoresT.tensor, scoresT.offset, [[arena_size, P], [S + P, T], [1, P]])
        hg_top = top[0]
        top[0] = heads_top
        o_retT = take(2 * RH, S)
        rq, rk = take(2, S), take(2, S)
        rv = take(T, RDK)
        rgate = take(2, 2, S)
        rsig = take(2, S)
        rope_a, rope_b = take(2, S), take(2, S)
        rscT = take(T, S)
        o_c, o_sq = take(2, S), take(2, S)
        rrs = take(S)
        strip = take(2, S + 3 * P)
        ret_top = top[0]
        top[0] = heads_top + 8 * S
        mergedT = take(KD, S)
        gsig = take(2, S)
        ytmp = take(2, S)
        ln_g, ln_b = take(2, D), take(2, D)
        bn = take(T, 2, 6)
        mv = take(T, 2)
        x_of_top = top[0]
        wr = take(KD, NL)
        bias_r = take(NL)
        logits = take(T, NL)
        iota = take(P)
        iota_b = take(P)
        sel_tmp = take(T, P)
        before = take(P)
        oh_g, gexp = take(T, GROUPS), take(T, GROUPS)
        picked = take(T, GROUPS, PER_GROUP)
        es, t8 = take(T, PER_GROUP), take(T, PER_GROUP)
        oh_e = take(2, T, PER_GROUP)
        m_k = take(2, T, EXPERTS)
        m_sum = take(T, EXPERTS)
        rank = take(T, EXPERTS)
        ge = take(T, EXPERTS)
        cnt, extra, ends, base_e, over_d = (take(EXPERTS) for _ in range(5))
        r4 = [take(T) for _ in range(6)]
        wts = take(2, T)
        slot_f, slot_i = take(2, T), take(2, T)
        cmp8 = take(8, EXPERTS)
        table_f, table_i = take(MAX_BLOCKS + 1), take(MAX_BLOCKS + 1)
        assert top[0] <= arena_size
        xs_at = top[0]
        xsT = take_split(KD, P)
        top[0] = heads_top + 8 * S
        gated, mg = take(S), take(S)
        mgT = take_split(T, P)
        ysb = take(2, D)
        sel = view_r(align(), (T, P))
        take(T, P)
        xrow = take(D)
        assert top[0] <= heads_top + 8 * S + 12 * S
        x_hl = [[view_r(at + i * D, (D,)) for i in range(T)] for at in (hT_at, heads_top)]
        moe_slots = ring[0:3]
        piece_at = [3 * SLOT, 3 * SLOT + 2 * PIECE, small_top, small_top + 2 * PIECE]
        pieces = [view_r(at, (2, PIECE)) for at in piece_at]
        yg = [[ring[k][:, i * D:(i + 1) * D] for i in range(T)] for k in range(2)]
        y_dram = nc.dram_tensor("y_blocks", (MAX_BLOCKS * P, D), F32).ap()
        ang2, sin_arg, cos_arg, ang2_tmp, pos2_f, pos2_i = (o_hgT[:, a] for a in range(6))

        wslot = lambda u: ring[u % RING]
        ready = [sem(f"slot{i}_loaded") for i in range(RING)]

        def x_of(l):
            return 1 + 8 * l

        aux_total = [0, 0]
        aux_at = []
        for j in range(MOD_UNITS):
            aux_total[j % 2] += 16 if (j % 6) < 2 else 32
            aux_at.append(aux_total[j % 2])

        block = ctx.enter_context(nc.Block())

        @block.sync
        def _(sp):
            sp.dma_start(x, A["x"].rearrange("b (t p) d -> p (b t) d", p=P)).then_inc(sem("x_in"), 16)

            sp.sem_inc(sem("down_mm"), DOWN_CREDIT)
            sp.sem_inc(sem("post_mm"), POST_CREDIT)

            def wait_slot(l, u):
                name, per_layer, count = unit_done(u - RING)
                sp.wait_ge(sem(name), l * per_layer + count)

            def unit(l, u, dst, src):
                wait_slot(l, u)
                sp.dma_start(dst, src).then_inc(ready[u % RING], 16)

            with sp.Fori(0, LAYERS) as l:
                def cols(name, u, c0, n):
                    w = A[name][l].rearrange("(k p) n -> p k n", p=P)
                    unit(l, u, wslot(u)[:, 0:KD * n].rearrange("p (k n) -> p k n", k=KD), w[:, :, c0:c0 + n])

                for j in range(6):
                    cols("ada_w", U_MOD_M + j, 512 * j, 512)
                for j in range(IN_UNITS):
                    cols("w_in", U_IN + j, IN_COLS * j, IN_COLS)
                for j in range(6):
                    cols("ada_w", U_MOD_F + j, 512 * (6 + j), 512)
                for j in range(OUT_UNITS):
                    cols("w_out", U_OUT + j, 512 * j, 512)
                wg = A["w_gate"][l].rearrange("(k p) n -> p k n", p=P)
                wu = A["w_up"][l].rearrange("(k p) n -> p k n", p=P)
                for j in range(GU_UNITS):
                    u = U_GU + j
                    dst = wslot(u).rearrange("p (h k n) -> p h k n", h=2, k=KD)
                    wait_slot(l, u)
                    sp.dma_start(dst[:, 0], wg[:, :, 256 * j:256 * j + 256]).then_inc(ready[u % RING], 16)
                    sp.dma_start(dst[:, 1], wu[:, :, 256 * j:256 * j + 256]).then_inc(ready[u % RING], 16)
                wd = A["w_down"][l].rearrange("(k p) n -> p k n", p=P)
                for j, (k0, n) in enumerate(DOWN_UNITS):
                    unit(l, U_DOWN + j, wslot(U_DOWN + j)[:, 0:n * D].rearrange("p (k n) -> p k n", k=n),
                         wd[:, k0:k0 + n, :])

            w2 = A["w_in_2"][0].rearrange("(k p) n -> p k n", p=P)

            def pieces(n, width, srcs, wait):
                sp.wait_ge(*wait)
                dst = ring[n % RING][:, 0:KD * width * len(srcs)].rearrange("p (s k n) -> p s k n", k=KD, n=width)
                for a, src in enumerate(srcs):
                    sp.dma_start(dst[:, a], src).then_inc(ready[n % RING], 16)

            def hg_units(h, b, waits):
                def src(col):
                    return w2[:, :, bass.ds(h * P + col, P)]
                pieces(2 * b, P, [src(COL_Q), src(COL_F), src(COL_FB)], waits[0])
                pieces(2 * b + 1, P, [src(COL_G), src(COL_V)], waits[1])

            def layer_end(u):
                name, per_layer, count = unit_done(u)
                return sem(name), (LAYERS - 1) * per_layer + count

            hg_units(0, 0, (layer_end(LAYER_UNITS - 4), layer_end(LAYER_UNITS - 3)))
            hg_units(1, 1, (layer_end(LAYER_UNITS - 2), layer_end(LAYER_UNITS - 1)))

            with sp.Fori(0, HG // 2 - 1) as i:
                for b in range(2):
                    h = i * 2 + (2 + b)
                    hg_units(h, b, ((sem("hgp_mm"), i * 10 + (3 + 5 * b)), (sem("hgp_mm"), i * 10 + (5 + 5 * b))))

            def ret_units(r):
                b, c = r % 2, r * RDK
                if r < 2:
                    f = 5 * (HG - 2 + r)
                    waits = (sem("hgp_mm"), f + 3), (sem("hgp_mm"), f + 5)
                else:
                    waits = (sem("retp_mm"), 8 * (r - 2) + 4), (sem("retp_mm"), 8 * (r - 2) + 8)
                pieces(2 * b, RDK, [w2[:, :, COL_RQ + c:COL_RQ + c + RDK], w2[:, :, COL_RK + c:COL_RK + c + RDK]], waits[0])
                pieces(2 * b + 1, RDK, [w2[:, :, COL_RG + c:COL_RG + c + RDK], w2[:, :, COL_RV + c:COL_RV + c + RDK]], waits[1])

            for r in range(RH):
                ret_units(r)
            wh = A["w_branch_hg_2"][0].rearrange("(k p) n -> p k n", p=P)
            wr = A["w_branch_ret_2"][0].rearrange("(k p) n -> p k n", p=P)
            wo = A["w_out_2"][0].rearrange("(k p) n -> p k n", p=P)
            merge_srcs = []
            for c in range(2):
                for g, w in ((COL_GA, wh), (COL_GB, wr)):
                    merge_srcs += [w2[:, :, g + 512 * c:g + 512 * c + 512], w[:, :, 512 * c:512 * c + 512]]
            for n, src in enumerate(merge_srcs):
                if n < 4:
                    wait = sem("retp_mm"), 8 * (2 + n // 2) + (4, 8)[n % 2]
                else:
                    wait = sem("merge_mm"), 4 * ((n - 4) // 2 + 1)
                pieces(n, 512, [src], wait)
            for n in range(4):
                pieces(n, 256, [wo[:, :, 256 * n:256 * n + 256]], (sem("merge_mm"), 4 * (n // 2 + 3)))
            def expert_units(e, waits):
                for a, name in enumerate(("w1_2", "w3_2", "w2_2")):
                    dst = moe_slots[a]
                    src = A[name][0, e].rearrange("(k p) n -> p k n", p=P)
                    for w_ in waits[a]:
                        sp.wait_ge(*w_)
                    sp.dma_start(dst.rearrange("p (k n) -> p k n", n=src.shape[2]), src
                                 ).then_inc(sem(f"expert_w{a}"), 16)

            def slot_free(unit):
                return [(sem("lo_ready"), 4 * unit + 4)]

            mixed = lambda n: [(sem("mix2_mm"), 4 * (n + 1))]
            expert_units(0, (mixed(0), mixed(1), mixed(2)))
            expert_units(1, (slot_free(0), slot_free(1), slot_free(2)))
            sp.wait_ge(sem("table_ready"), 1)
            turns = sp.value_load(table_i[0:1, MAX_BLOCKS:MAX_BLOCKS + 1].bitcast(I32), min_val=16, max_val=20)
            with sp.Fori(1, turns) as i:
                for b in range(2):
                    e = sp.value_load(table_i[0:1, bass.ds(2 * i + b, 1)].bitcast(I32), min_val=0, max_val=EXPERTS - 1)
                    expert_units(e, [slot_free((2 * i + (b - 1)) * 3 + a) for a in range(3)])
            sp.wait_ge(sem("x2_ready"), 4)
            sp.dma_start(out.rearrange("b (t p) d -> p (b t) d", p=P), x).then_inc(sem("out_done"), 16)
            sp.wait_ge(sem("out_done"), 16)

        arrivals = [0] * RING
        arrive_at = []
        for u in range(LAYER_UNITS):
            arrivals[u % RING] += 32 if U_GU <= u < U_DOWN else 16
            arrive_at.append(arrivals[u % RING])

        def mlp_raw(p):
            if p < GU_PIECES:
                u, n = U_GU + p // 4, p % 4
            else:
                j = max(j for j, (k0, _) in enumerate(DOWN_UNITS) if k0 <= p - GU_PIECES)
                u, n = U_DOWN + j, p - GU_PIECES - DOWN_UNITS[j][0]
            return u, wslot(u)[:, n * PIECE:(n + 1) * PIECE]

        @block.gpsimd
        def _(pool):
            with nc.allow_non_contiguous_dma("small load, once"):
                pool.dma_start(ccol, A["c"].rearrange("b (k p) -> p (b k)", p=P)).then_inc(sem("c_in"), 16)
            for dst, src in ((ident, K["ident"]), (window, K["window"]),
                             (poolm.rearrange("p a b c -> p (a b c)"), K["pool"]), (inv1, K["inv1"]),
                             (pos_i.bitcast(I32), A["positions"].rearrange("b (t p) -> p (b t)", p=P))):
                with nc.allow_non_contiguous_dma("small loads, once"):
                    pool.dma_start(dst, src).then_inc(sem("const_in"), 16)
            nc.gpsimd.memset(pooled, 0.0).then_inc(sem("zeros_ready"), 1)
            pool.wait_ge(sem("zeros_ready"), 1)
            for b in range(EXPERTS, MAX_BLOCKS):
                pool.dma_start(y_dram[b * P:(b + 1) * P, :], pooled.rearrange("p a n -> p (a n)")
                               ).then_inc(sem("zeros_out"), 16)
            with pool.Fori(0, LAYERS) as l:
                pool.wait_ge(sem("x_ready"), x_of(l))
                with nc.allow_non_contiguous_dma("small loads"):
                    pool.dma_start(b_in, A["b_in"][l].partition_broadcast(P)).then_inc(sem("layer_in"), 16)
                    pool.dma_start(sink, A["sinks"][l].partition_broadcast(P)).then_inc(sem("layer_in"), 16)
                    pool.dma_start(pscale, A["pool_scale"][l].rearrange("(g p) -> p g", p=P)
                                   ).then_inc(sem("layer_in"), 16)
                    pool.dma_start(poolw, A["pool_w"][l].rearrange("g c d -> c g d")).then_inc(sem("layer_in"), 16)
                for j in range(MOD_UNITS):
                    what, c = (j % 6) // 2, 512 * (j % 2)
                    pool.wait_ge(sem("mod_free"), l * MOD_UNITS + (j + 1))
                    pool.dma_start(aux[:, j % 2, 0], A["ada_b"][l, 512 * j:512 * j + 512].partition_broadcast(P)
                                   ).then_inc(sem(f"aux{j % 2}_in"), 16)
                    if what:
                        g = A[(("g_pre_mix", "g_post_mix"), ("g_pre_ffn", "g_post_ffn"))[j // 6][what - 1]]
                        pool.dma_start(aux[:, j % 2, 1], g[l, c:c + 512].partition_broadcast(P)
                                       ).then_inc(sem(f"aux{j % 2}_in"), 16)

            pool.wait_ge(sem("x_ready"), x_of(LAYERS))
            with nc.allow_non_contiguous_dma("small loads"):
                for dst, src in (
                        (pos2_i.bitcast(I32), A["positions_2"][0].partition_broadcast(P)),
                        (inv2, K["inv2"]), (restart, K["restart"]),
                        (masks.rearrange("p a b -> p (a b)"), K["masks"]),
                        (lb, A["hg_lb_logits_2"][0].rearrange("(h p) -> p h", p=P)),
                        (one_lb, A["hg_lb_logits_2"][1].rearrange("(h p) -> p h", p=P)),
                        (hg_g, A["hg_norm_g_2"][0].rearrange("(h p) -> p h", p=P)),
                        (ret_g, A["ret_norm_g_2"][0].rearrange("(h p) -> p h", p=P))):
                    pool.dma_start(dst, src).then_inc(sem("const2_in"), 16)
            pool.wait_ge(sem("hg_out"), HG + 1)
            for r in range(RH):
                if r >= 2:
                    pool.wait_ge(sem("rsc_ready"), 4 * (r - 1))
                pool.dma_start(strip[:, r % 2], K["decay"][r]).then_inc(sem(f"strip{r % 2}_in"), 16)
            pool.wait_ge(sem("ret_out"), RH)
            for dst, name in ((ln_g[:, 0], "ln1_g_2"), (ln_b[:, 0], "ln1_b_2")):
                pool.dma_start(dst, A[name][0].partition_broadcast(P)).then_inc(sem("ln0_in"), 16)

            for dst, src in ((wr[:, :, 0:GROUPS], A["w_group_2"][0].rearrange("(k p) n -> p k n", p=P)),
                             (wr[:, :, GROUPS:NL], A["w_router_2"][0].rearrange("(k p) n -> p k n", p=P)),
                             (bias_r[:, 0:GROUPS], A["b_group_2"][0].partition_broadcast(P)),
                             (bias_r[:, GROUPS:NL], A["b_router_2"][0].partition_broadcast(P)),
                             (iota, K["iota"]), (before, K["before"])):
                with nc.allow_non_contiguous_dma("small loads"):
                    pool.dma_start(dst, src).then_inc(sem("route_in"), 16)
            for dst, name in ((ln_g[:, 1], "ln2_g_2"), (ln_b[:, 1], "ln2_b_2")):
                pool.dma_start(dst, A[name][0].partition_broadcast(P)).then_inc(sem("ln1_in"), 16)
            pool.wait_ge(sem("table_ready"), 1)
            pool.sem_inc(sem("ysb_free"), 2)
            turns = pool.value_load(table_i[0:1, MAX_BLOCKS:MAX_BLOCKS + 1].bitcast(I32), min_val=16, max_val=20)
            with pool.Fori(0, turns) as i:
                for b in range(2):
                    pool.wait_ge(sem("y_taken"), 2 * i + (b + 2))
                    pool.sem_inc(sem("store_order"), 1)
                    pool.dma_start(y_dram[bass.ds((2 * i + b) * P, P), :], ysb[:, b]).then_inc(sem("y_stored"), 16)
                    pool.wait_ge(sem("y_stored"), 32 * i + (16 * b + 16))
                    pool.sem_inc(sem("ysb_free"), 1)
            pool.wait_ge(sem("zeros_out"), 16 * (MAX_BLOCKS - EXPERTS))
            for i in range(T):
                for k in range(2):
                    pool.indirect_dma_start(
                        out=yg[k][i], out_offset=None, in_=y_dram,
                        in_offset=bass.IndirectOffsetOnAxis(ap=slot_i[:, k, i:i + 1].bitcast(I32), axis=0),
                        bounds_check=MAX_BLOCKS * P - 1, oob_is_err=False).then_inc(sem(f"rows{i}_in"), 16)

        @block.tensor
        def _(pe):

            def need(l, u):
                pe.wait_ge(ready[u % RING], l * arrivals[u % RING] + arrive_at[u])
                return wslot(u)

            def product(out, stationary, moving, start, stop):
                for n, (a, b) in enumerate(((0, 0), (0, 1), (1, 0))):
                    m = nc.tensor.matmul(out, stationary(a), moving(b), start=start and n == 0, stop=stop and n == 2)
                    yield m

            def modulation(l, j, u):
                w = need(l, u).rearrange("p (k n) -> p k n", k=KD)
                pe.wait_ge(sem("mod_free"), l * MOD_UNITS + (j + 1))
                for k in range(KD):
                    m = nc.tensor.matmul(bank(j % 2), crep[:, k], w[:, k], start=k == 0, stop=k == KD - 1)
                m.then_inc(sem("mod_mm"), 1)

            def to_features(n):
                for i in range(T):
                    pe.wait_ge(sem("h_row"), 4 * n + (i + 1))
                    if i >= 2:
                        pe.wait_ge(sem("hT_ready"), 4 * n + (i - 1))
                    for k in range(KD):
                        m = nc.tensor.transpose(psum[:, 2 + 2 * (i % 2) + k // 4, (k % 4) * P:(k % 4 + 1) * P],
                                                hrow[:, i % 2, k * P:(k + 1) * P], ident)
                    m.then_inc(sem("tr_mm"), 1)
                pe.wait_ge(sem("hT_ready"), 4 * n + 4)

            pe.wait_ge(sem("crep_ready"), 1)
            with pe.Fori(0, LAYERS) as l:
                pe.wait_ge(sem("x_ready"), x_of(l))
                for j in range(6):
                    modulation(l, j, U_MOD_M + j)
                to_features(2 * l)
                for c in range(IN_UNITS):
                    w = need(l, U_IN + c)[:, 0:KD * IN_COLS].rearrange("p (k n) -> p k n", k=KD)
                    for i in range(T):
                        pe.wait_ge(sem("proj_free"), 16 * l + (4 * c + i + 1))
                        for k in range(KD):
                            m = nc.tensor.matmul(psum[:, 2 + i, 0:IN_COLS], hT[:, k, i * P:(i + 1) * P], w[:, k],
                                                 start=k == 0, stop=k == KD - 1)
                        m.then_inc(sem("proj_mm"), 1)
                for j in range(6, 12):
                    modulation(l, j, U_MOD_F + j - 6)
                pe.wait_ge(sem("proj_free"), 16 * l + 20)
                pe.wait_ge(sem("layer_in"), 64 * l + 64)

                def pool_window(g):
                    for i in range(T):
                        u_i = [proj[:, j, QKV + g * P:QKV + (g + 1) * P] for j in (i, max(i - 1, 0))]
                        o = psum[:, 2 + g % 2, i * P:(i + 1) * P]
                        m = nc.tensor.matmul(o, u_i[0], poolm[:, g, 0 if i else 2], start=True, stop=i == 0)
                        if i:
                            m = nc.tensor.matmul(o, u_i[1], poolm[:, g, 1], start=False, stop=True)
                    m.then_inc(sem("pool_mm"), 1)

                def pool_weights(g):
                    pe.wait_ge(sem("pooled_ready"), 4 * l + (g + 1))
                    if g >= 2:
                        pe.wait_ge(sem("poolT_ready"), 4 * l + (g - 1))
                    nc.tensor.matmul(bank(6 + g % 2), poolw[:, g], pooled[:, g % 2], start=True, stop=True
                                     ).then_inc(sem("poolw_mm"), 1)

                pool_window(0)
                pool_window(1)
                for g in range(POOL_G):
                    pool_weights(g)
                    if g + 2 < POOL_G:
                        pool_window(g + 2)
                pe.wait_ge(sem("rope_done"), l + 1)
                for c in range(6):
                    if c >= 4:
                        pe.wait_ge(sem("qkT_ready"), 6 * l + (c - 3))
                    for i in range(T):
                        src = proj[:, i, c * P:(c + 1) * P] if c < 4 else \
                            kdup[:, i, c - 4].rearrange("p a d -> p (a d)")
                        m = nc.tensor.transpose(psum[:, 2 + c % 4, i * P:(i + 1) * P], src, ident)
                    m.then_inc(sem("qkT_mm"), 1)
                pe.wait_ge(sem("qkT_ready"), 6 * l + 6)
                pe.wait_ge(sem("poolT_ready"), 4 * l + 4)

                def scores(n):
                    k0, nk = (n - 1, 2 * P) if n else (0, P)
                    for jj in range(KVH):
                        if n:
                            pe.wait_ge(sem("score_free"), 16 * l + (4 * (n - 1) + 2 * jj + 2))
                        for j in (2 * jj, 2 * jj + 1):
                            for a in range(2):
                                half = slice(64 * a, 64 * a + 64)
                                m = nc.tensor.matmul(psum[:, 4 + 2 * jj + a, (j % 2) * nk:(j % 2 + 1) * nk],
                                                     qkT[half, j, n * P:(n + 1) * P],
                                                     qkT[half, 4 + jj, k0 * P:k0 * P + nk], start=True, stop=True)
                                if j % 2:
                                    m.then_inc(sem("score_mm"), 1)

                def attend(n):
                    nk = 2 if n else 1
                    pe.wait_ge(sem("probs_ready"), 4 * l + (n + 1))
                    for g in range(4):
                        if 4 * n + g >= 2:
                            pe.wait_ge(sem("probsT_ready"), 16 * l + (4 * n + g - 1))
                        for a in range(2):
                            for b in range(nk):
                                m = nc.tensor.transpose(psum[:, 2 + g % 2, (a * nk + b) * P:(a * nk + b + 1) * P],
                                                        probs[:, n % 2, 2 * g + a, b * P:(b + 1) * P], ident)
                        m.then_inc(sem("probsT_mm"), 1)
                    pe.wait_ge(sem("probsT_ready"), 16 * l + (4 * n + 4))
                    if n >= 2:
                        pe.wait_ge(sem("attnT_ready"), 4 * l + (n - 1))
                    else:
                        pe.wait_ge(sem("mod_free"), l * MOD_UNITS + 14)
                    for h in range(HEADS):
                        v0 = HEADS * HD + KVH * HD + (h // GROUP) * HD
                        o = psum[64 * (h % 2):64 * (h % 2) + 64, n % 2, (h // 2) * P:(h // 2 + 1) * P]
                        for b in range(nk):
                            m = nc.tensor.matmul(o, proj[:, n - nk + 1 + b, v0:v0 + HD], probsT[:, h, b],
                                                 start=b == 0, stop=b == nk - 1)
                    m.then_inc(sem("attn_mm"), 1)

                scores(0)
                for n in range(T):
                    if n + 1 < T:
                        scores(n + 1)
                    attend(n)
                pe.wait_ge(sem("attnT_ready"), 4 * l + 4)
                for c in range(OUT_UNITS):
                    w = need(l, U_OUT + c).rearrange("p (k n) -> p k n", k=KD)
                    for i in range(T):
                        for k in range(KD):
                            m = nc.tensor.matmul(bank(4 * c + i), mixT[:, k, i * P:(i + 1) * P], w[:, k],
                                                 start=k == 0, stop=k == KD - 1)
                        m.then_inc(sem("post_mm"), 1)
                to_features(2 * l + 1)
                for u in range(GU_UNITS):
                    if u >= 2:
                        pe.wait_ge(sem("actT_ready"), GU_UNITS * l + (u - 1))
                    for a in range(2):
                        for half in range(2):
                            p = 4 * u + 2 * a + half
                            pe.wait_ge(sem("mlp_lo"), MLP_PIECES * l + (p + 1))
                            w = mlp_pieces[p % 2].rearrange("p h (k n) -> p h k n", k=4)
                            for c in range(2):
                                for k in range(4):
                                    kk = 4 * half + k
                                    for n, m in enumerate(product(bank(4 * (u % 2) + 2 * a + c),
                                                                  lambda h: w[:, h, k, c * P:(c + 1) * P],
                                                                  lambda h: hT_part(h, kk), kk == 0, kk == KD - 1)):
                                        if c == k == n == 0:
                                            m.then_inc(sem("mlp_started"), 1)
                    m.then_inc(sem("gu_mm"), 1)
                pe.wait_ge(sem("actT_ready"), GU_UNITS * l + GU_UNITS)
                for j, (k0, nk) in enumerate(DOWN_UNITS):
                    for k in range(k0, k0 + nk):
                        p = GU_PIECES + k
                        pe.wait_ge(sem("mlp_lo"), MLP_PIECES * l + (p + 1))
                        pe.wait_ge(sem("acts_lo"), KF * l + (k + 1))
                        w, a_k = mlp_pieces[p % 2], act_pieces[k % 2]
                        for i in range(T):
                            for c in range(2):
                                for n, m in enumerate(product(bank(4 * c + i), lambda h: a_k[:, h, i * P:(i + 1) * P],
                                                              lambda h: w[:, h, c * 512:(c + 1) * 512],
                                                              k == 0, k == KF - 1)):
                                    if i == c == n == 0:
                                        m.then_inc(sem("mlp_started"), 1)
                                if k == KF - 1:
                                    m.then_inc(sem("post_mm"), 1)
                    if k < KF - 1:
                        m.then_inc(sem("down_mm"), 1)


            def x_to_features(n, sem_name):
                for i in range(T):
                    pe.wait_ge(sem(sem_name), {"x_ready": 1 + 4 * XT_TURN - 3 + i, "x1_ready": i + 1}[sem_name])
                    if i >= 2:
                        pe.wait_ge(sem("hT_ready"), 4 * n + i - 1)
                    for k in range(KD):
                        m = nc.tensor.transpose(psum[:, 2 + 2 * (i % 2) + k // 4, (k % 4) * P:(k % 4 + 1) * P],
                                                x[:, i, k * P:(k + 1) * P], ident)
                    m.then_inc(sem("tr_mm"), 1)
                pe.wait_ge(sem("hT_ready"), 4 * n + 4)

            pe.wait_ge(sem("x_ready"), x_of(LAYERS))
            x_to_features(XT_TURN, "x_ready")
            xT = hT
            seen = [LAYERS * a for a in arrivals]

            def hg_chunk(h, b, what):
                if what in (0, 3):
                    slot = 2 * b + what // 3
                    n = 48 if what == 0 else 32
                    pe.wait_ge(ready[slot], (h - b) * (n // 2) + (seen[slot] + n))
                w = ring[2 * b + what // 3][:, 0:KD * P * (3 if what < 3 else 2)].rearrange(
                    "p (s k n) -> p s k n", k=KD, n=P)[:, what % 3]
                if what < 4:
                    for k in range(KD):
                        m = nc.tensor.matmul(bank(what), w[:, k], xT[:, k], start=k == 0, stop=k == KD - 1)
                else:
                    for i in range(T):
                        for k in range(KD):
                            m = nc.tensor.matmul(psum[:, 4, i * P:(i + 1) * P], xT[:, k, i * P:(i + 1) * P], w[:, k],
                                                 start=k == 0, stop=k == KD - 1)
                m.then_inc(sem("hgp_mm"), 1)

            def hg_free(h, what):
                if what == 0:
                    pe.wait_ge(sem("hgp_taken"), 2 * h - 1)
                elif what in (1, 2):
                    pe.wait_ge(sem("hg_sig"), 4 * h - 2 + (what - 1))
                elif what == 3:
                    pe.wait_ge(sem("hgp_taken"), 2 * h)
                else:
                    pe.wait_ge(sem("v_ready"), h)

            def next_chunk(h, b, what, last):
                if last:
                    if what < 4:
                        ret_qk(0, what)
                    return
                hg_free(h + 1, what)
                hg_chunk(h + 1, 1 - b, what)

            def ret_w(r, side, width=RDK):
                return ring[2 * (r % 2) + side][:, 0:2 * KD * width].rearrange("p (s k n) -> p s k n", k=KD, n=width)

            def ret_qk(r, what):
                if what == 0:
                    pe.wait_ge(ready[2 * (r % 2)], seen[2 * (r % 2)] + 48 * (HG // 2) + 32 * (r // 2 + 1))
                if r == 0:
                    hg_free(HG, what)
                else:
                    pe.wait_ge(sem("rsc_ready"), 4 * (r - 1) + what + 1)
                w = ret_w(r, 0)[:, what // 2]
                for k in range(KD):
                    m = nc.tensor.matmul(bank(what), w[:, k, what % 2:RDK:2], xT[:, k], start=k == 0, stop=k == KD - 1)
                m.then_inc(sem("retp_mm"), 1)

            def hg_norm_sum(h):
                pe.wait_ge(sem("osq_ready"), h + 1)
                nc.tensor.matmul(bank(6), ones, osq, start=True, stop=True).then_inc(sem("hgs_mm"), 1)

            def hg_level(h, l):
                pe.wait_ge(sem("kq_ready"), 8 * h + (LEVELS - l + 1))
                if l >= LEVELS - 2:
                    pe.wait_ge(sem("row_ready"), 4 * h + (LEVELS - 1 - l + 3))
                else:
                    pe.wait_ge(sem("level_taken"), 7 * h + (LEVELS - 2 - l))
                for i in range(T):
                    ts = slice(i * P, (i + 1) * P)
                    rhs = lev_qk[:, l % 2, 0, ts] if l else q_h[:, ts]
                    m = nc.tensor.matmul(psum[:, 5 + (LEVELS - 1 - l) % 2, ts], lev_qk[:, l % 2, 1, ts], rhs,
                                         start=True, stop=True)
                m.then_inc(sem("hgs_mm"), 1)

            def hg_rows(h):
                pe.wait_ge(sem("kq_ready"), 8 * h + 1)
                for s in range(T):
                    if s == 1:
                        pe.wait_ge(sem("sum_taken"), h + 1)
                    elif s >= 2:
                        pe.wait_ge(sem("row_ready"), 4 * h + (s - 1))
                    far_f, far_b = xf_q[:, 2:4].rearrange("p a t -> p (a t)"), xb_q[:, 2:4].rearrange("p a t -> p (a t)")
                    own = (s, 1, lev_qk[:, 1, 1, s * P:(s + 1) * P], lev_qk[:, 1, 0, s * P:(s + 1) * P])
                    products = {
                        0: [own, (1, 1, xf_k[:, 0], xf_q[:, 0]), (2, 2, xf_k[:, 2], far_f)],
                        1: [(0, 1, xb_k[:, 0], xb_q[:, 0]), own, (2, 2, xf_k[:, 3], far_f)],
                        2: [(0, 2, xb_k[:, 2], far_b), own, (3, 1, xf_k[:, 1], xf_q[:, 1])],
                        3: [(0, 2, xb_k[:, 3], far_b), (2, 1, xb_k[:, 1], xb_q[:, 1]), own],
                    }[s]
                    for t, n, lhs, rhs in products:
                        m = nc.tensor.matmul(psum[:, 5 + s % 2, t * P:(t + n) * P], lhs, rhs, start=True, stop=True)
                    m.then_inc(sem("hgs_mm"), 1)

            def hg_out(h):
                pe.wait_ge(sem("level_taken"), 7 * h + 7)
                pe.wait_ge(sem("v_ready"), h + 1)
                pe.wait_ge(sem("hg_out"), h + 1)
                for i in range(T):
                    m = nc.tensor.matmul(bank(7), v_h[:, i], scoresT[:, i], start=i == 0, stop=i == T - 1)
                m.then_inc(sem("o_mm"), 1)

            def hg_head(h, b, first=False, last=False):
                next_chunk(h, b, 0, last)
                if not first:
                    hg_norm_sum(h - 1)
                hg_rows(h)
                for what, pair in ((1, (6, 5)), (2, (4, 3)), (3, (2, 1)), (4, (0,))):
                    next_chunk(h, b, what, last)
                    for l in pair:
                        hg_level(h, l)
                hg_out(h)

            pe.wait_ge(sem("ones_ready"), 1)
            for what in range(5):
                hg_chunk(0, 0, what)
            hg_head(0, 0, first=True)
            with pe.Fori(0, HG // 2 - 1) as i:
                hg_head(2 * i + 1, 1)
                hg_head(2 * i + 2, 0)
            hg_head(HG - 1, 1, last=True)
            hg_norm_sum(HG - 1)

            def ret_gate(r):
                pe.wait_ge(ready[2 * (r % 2) + 1], seen[2 * (r % 2) + 1] + 32 * (HG // 2) + 32 * (r // 2 + 1))
                if r == 0:
                    pe.wait_ge(sem("hg_out"), HG + 1)
                else:
                    pe.wait_ge(sem("rgate_ready"), r)
                if r >= 2:
                    pe.wait_ge(sem("rsum_taken"), r - 1)
                w = ret_w(r, 1)[:, 0]
                for a in range(2):
                    for k in range(KD):
                        m = nc.tensor.matmul(bank(6 + a), w[:, k, a * P:(a + 1) * P], xT[:, k],
                                             start=k == 0, stop=k == KD - 1)
                    m.then_inc(sem("retp_mm"), 1)

            def ret_v(r):
                w = ret_w(r, 1)[:, 1]
                if r:
                    pe.wait_ge(sem("o_copied"), 2 * r)
                for i in range(T):
                    for k in range(KD):
                        m = nc.tensor.matmul(psum[:, 4 + i // 2, (i % 2) * RDK:(i % 2 + 1) * RDK],
                                             xT[:, k, i * P:(i + 1) * P], w[:, k], start=k == 0, stop=k == KD - 1)
                    if i % 2:
                        m.then_inc(sem("retp_mm"), 1)

            def ret_scores(r):
                pe.wait_ge(sem("rope2_done"), 2 * r + 2)
                for s in range(T):
                    for a in range(2):
                        m = nc.tensor.matmul(bank(s), rk[:, a, s * P:(s + 1) * P], rq[:, a],
                                             start=a == 0, stop=a == 1)
                    m.then_inc(sem("rs_mm"), 1)

            def ret_out(r):
                pe.wait_ge(sem("rsc_ready"), 4 * r + 4)
                pe.wait_ge(sem("rv_ready"), 2 * r + 2)
                for a in range(2):
                    for s in range(T):
                        m = nc.tensor.matmul(bank(4 + a), rv[:, s, a * P:(a + 1) * P], rscT[:, s],
                                             start=s == 0, stop=s == T - 1)
                    m.then_inc(sem("ro_mm"), 1)

            def ret_norm_sum(r):
                pe.wait_ge(sem("rosq_ready"), r + 1)
                pe.wait_ge(sem("rgate_ready"), min(r + 2, RH))
                for a in range(2):
                    m = nc.tensor.matmul(bank(6), ones, o_sq[:, a], start=a == 0, stop=a == 1)
                m.then_inc(sem("rsum_mm"), 1)

            ret_gate(0)
            pe.wait_ge(sem("v_ready"), HG)
            ret_v(0)
            for r in range(RH):
                ret_scores(r)
                if r + 1 < RH:
                    for what in range(4):
                        ret_qk(r + 1, what)
                ret_out(r)
                if r + 1 < RH:
                    ret_gate(r + 1)
                    ret_v(r + 1)
                ret_norm_sum(r)

            base = [seen[n] + (48, 32, 48, 32)[n] * (HG // 2) + 32 * (RH // 2) for n in range(RING)]
            pe.wait_ge(sem("ret_out"), RH)
            for n in range(0, 8, 2):
                src = o_hgT if n % 4 == 0 else o_retT
                for a in range(2):
                    pe.wait_ge(ready[(n + a) % RING], base[(n + a) % RING] + 16 * ((n + a) // RING + 1))
                wg_, wb = (ring[(n + a) % RING].rearrange("p (k n) -> p k n", k=KD) for a in range(2))
                for j in range(4):
                    s = 2 * n + j
                    if s >= 4:
                        pe.wait_ge(sem("merge_taken"), s - 3)
                    b = 2 * (s % 4)
                    for k in range(KD):
                        m = nc.tensor.matmul(bank(b), wg_[:, k, j * P:(j + 1) * P], xT[:, k],
                                             start=k == 0, stop=k == KD - 1)
                    for k in range(KD):
                        m = nc.tensor.matmul(bank(b + 1), wb[:, k, j * P:(j + 1) * P], src[:, k],
                                             start=k == 0, stop=k == KD - 1)
                    m.then_inc(sem("merge_mm"), 1)
            pe.wait_ge(sem("merge_taken"), 16)
            for n in range(4):
                pe.wait_ge(ready[n], base[n] + 16 * 3)
                w = ring[n][:, 0:KD * 256].rearrange("p (k n) -> p k n", k=KD)
                for i in range(T):
                    for k in range(KD):
                        m = nc.tensor.matmul(psum[:, 2 * i + n // 2, (n % 2) * 256:(n % 2 + 1) * 256],
                                             mergedT[:, k, i * P:(i + 1) * P], w[:, k],
                                             start=k == 0, stop=k == KD - 1)
                    m.then_inc(sem("mix2_mm"), 1)


            x_to_features(XT_TURN + 1, "x1_ready")
            pe.wait_ge(sem("route_in"), 96)
            for i in range(T):
                for k in range(KD):
                    m = nc.tensor.matmul(psum[:, 0, i * NL:(i + 1) * NL], hT[:, k, i * P:(i + 1) * P], wr[:, k],
                                         start=k == 0, stop=k == KD - 1)
            m.then_inc(sem("logits_mm"), 1)
            pe.wait_ge(sem("onehots_ready"), 1)
            for i in range(T + 1):
                o = psum[:, 1, i * EXPERTS:(i + 1) * EXPERTS]
                for j in range(i):
                    m = nc.tensor.matmul(o, ones, m_sum[:, j], start=j == 0, stop=j == T - 1)
                if i < T:
                    m = nc.tensor.matmul(o, before, m_sum[:, i], start=i == 0, stop=True)
            m.then_inc(sem("ranks_mm"), 1)

            def gather(j, half):
                pe.wait_ge(sem("sel_ready"), j + 1)
                for i in range(T):
                    for a in range(2):
                        m = nc.tensor.matmul(bank(half), sel[:, i], x_hl[a][i][:, 512 * half:512 * half + 512],
                                             start=i == 0 and a == 0, stop=i == T - 1 and a == 1)
                m.then_inc(sem("gather_mm"), 1)

            def gathered_to_features(j):
                pe.wait_ge(sem("xrow_ready"), 2 * j + 2)
                for k in range(KD):
                    m = nc.tensor.transpose(psum[:, k // 4, (k % 4) * P:(k % 4 + 1) * P], xrow[:, k * P:(k + 1) * P], ident)
                    if k % 4 == 3:
                        m.then_inc(sem("gathered_tr"), 1)

            def expert(i, b):
                j = 2 * i + b

                def piece(q):
                    pe.wait_ge(sem("lo_ready"), 12 * j + (q + 1))
                    return pieces[q % PIECES]

                for q in range(8):
                    if q in (0, 2):
                        pe.wait_ge(sem("xs_ready"), 2 * j + (q // 2 + 1))
                    w = piece(q).rearrange("p h (k n) -> p h k n", k=2)
                    for c in range(2):
                        k = 2 * (q % 4) + c
                        for n, m in enumerate(product(bank(2 + q // 4), lambda a: xsT[:, a, k], lambda a: w[:, a, c],
                                                      k == 0, k == KD - 1)):
                            if c == 0 and n == 0:
                                m.then_inc(sem("piece_started"), 1)
                    if q % 4 == 3:
                        m.then_inc(sem("h_mm"), 1)
                gather(j + 1, 0)
                pe.wait_ge(sem("mg_ready"), j + 1)
                for k in range(DE // P):
                    m = nc.tensor.transpose(psum[:, 4, k * P:(k + 1) * P], mg[:, k * P:(k + 1) * P], ident)
                m.then_inc(sem("mgT_mm"), 1)
                gather(j + 1, 1)
                pe.wait_ge(sem("mgT_ready"), j + 1)
                pe.wait_ge(sem("y_taken"), j + 1)
                for k in range(DE // P):
                    w = piece(8 + k).rearrange("p h (c n) -> p h c n", c=2)
                    for c in range(2):
                        for n, m in enumerate(product(bank(5 + c), lambda a: mgT[:, a, k], lambda a: w[:, a, c],
                                                      k == 0, k == DE // P - 1)):
                            if c == 0 and n == 0:
                                m.then_inc(sem("piece_started"), 1)
                    if k == 0:
                        gathered_to_features(j + 1)
                m.then_inc(sem("y_mm"), 1)

            pe.wait_ge(sem("table_ready"), 1)
            turns = pe.value_load(table_i[0:1, MAX_BLOCKS:MAX_BLOCKS + 1].bitcast(I32), min_val=16, max_val=20)
            pe.sem_inc(sem("piece_started"), PIECES)
            pe.wait_ge(sem("x_split"), T)
            gather(0, 0)
            gather(0, 1)
            gathered_to_features(0)
            with pe.Fori(0, turns) as i:
                for b in range(2):
                    expert(i, b)

        @block.scalar
        def _(act):
            C = Chain(act, sem("act_order"))

            def rsqrt_mean(src, dst, n):
                C.settle()
                C.link(nc.scalar.activation(lnv[:, 0:n], src, ACT.Ln, bias=eps, scale=1.0 / D))
                C.settle()
                return nc.scalar.activation(dst, lnv[:, 0:n], ACT.Exp, scale=-0.5)

            act.wait_ge(sem("c_in"), 16)
            C.link(nc.scalar.activation(csil, ccol, ACT.Silu))
            C.settle()
            for k in range(KD):
                m = nc.scalar.activation(crep[:, k], csil[:, k:k + 1].to_broadcast([P, P]), ACT.Copy)
                m.then_inc(sem("crep_ready"), 1) if k == KD - 1 else C.link(m)
            act.wait_ge(sem("angles_ready"), 1)
            C.link(nc.scalar.activation(sin1, rt[1], ACT.Sin))
            nc.scalar.activation(cos1, rt[2], ACT.Sin).then_inc(sem("rope_tables"), 1)

            def pre_norm(l, which):
                n = 2 * l + which
                if not which:
                    act.wait_ge(sem("x_ready"), x_of(l))
                for i in range(T):
                    if which:
                        act.wait_ge(sem("x_ready"), x_of(l) + (i + 1))
                    C.link(nc.scalar.activation(sq_junk, x[:, i], ACT.Square, accum_out=ssq[:, i:i + 1]))
                    C.settle()
                rsqrt_mean(ssq[:, 0:T], rstd, T).then_inc(sem("pre_rstd"), 1)
                for i in range(T):
                    act.wait_ge(sem("tr_mm"), 4 * n + (i + 1))
                    dst = hT_hi if which else hT
                    for q in range(2):
                        m = nc.scalar.activation(dst[:, 4 * q:4 * q + 4, i * P:(i + 1) * P],
                                                 bank(2 + 2 * (i % 2) + q).rearrange("p (k t) -> p k t", k=4), ACT.Copy)
                        m.then_inc(sem("hT_hi" if which else "hT_ready"), 1) if q else C.link(m)

            def mlp_hi(l, p):
                u, raw = mlp_raw(p)
                act.wait_ge(ready[u % RING], l * arrivals[u % RING] + arrive_at[u])
                if p >= 2:
                    act.wait_ge(sem("mlp_started"), MLP_PIECES * l + p)
                nc.scalar.activation(mlp_pieces[p % 2][:, 0], raw, ACT.Copy).then_inc(sem("mlp_hi"), 1)

            def post_norm(l, which):
                n = 2 * l + which
                junk = sig[:, 0, 0] if which else sq_junk[:, 0:512]
                for i in range(T):
                    act.wait_ge(sem("post_mm"), 8 * n + (POST_CREDIT + (2 * i + 2 if which else i + 5)))
                    for c in range(2):
                        C.link(nc.scalar.activation(junk, bank(4 * c + i), ACT.Square,
                                                    accum_out=ssq[:, 4 * c + i:4 * c + i + 1]))
                        C.settle()
                m = nc.scalar.activation(lnv, ssq[:, 0:T], ACT.Identity, bias=0.0)
                m.then_inc(sem("post_sq"), 1)
                act.wait_ge(sem("post_sum"), n + 1)
                rsqrt_mean(ssq[:, 0:T], rstd, T).then_inc(sem("post_rstd"), 1)

            with act.Fori(0, LAYERS) as l:
                C.enter(l, "act_layer")
                pre_norm(l, 0)
                act.wait_ge(sem("layer_in"), 64 * l + 64)
                for g in range(POOL_G):
                    act.wait_ge(sem("poolw_mm"), 4 * l + (g + 1))
                    nc.scalar.activation(mixT[:, 4 + g], bank(6 + g % 2), ACT.Copy, scale=pscale[:, g:g + 1]
                                         ).then_inc(sem("poolT_ready"), 1)
                for c in range(6):
                    act.wait_ge(sem("qkT_mm"), 6 * l + (c + 1))
                    nc.scalar.activation(qkT[:, c], bank(2 + c % 4), ACT.Copy).then_inc(sem("qkT_ready"), 1)

                def soft(n):
                    nk = 2 * P if n else P
                    b = n % 2
                    act.wait_ge(sem("max_ready"), 4 * l + (n + 1))
                    for h in range(HEADS):
                        C.link(nc.scalar.activation(probs[:, b, h, 0:nk], probs[:, b, h, 0:nk], ACT.Exp,
                                                    bias=negm[:, b, h:h + 1], accum_out=rsum[:, b, h:h + 1]))
                    nc.scalar.activation(esink[:, b], den[:, b], ACT.Exp).then_inc(sem("exp_done"), 1)

                def take_probsT(n):
                    nk = 2 if n else 1
                    for g in range(4):
                        act.wait_ge(sem("probsT_mm"), 16 * l + (4 * n + g + 1))
                        nc.scalar.activation(probsT[:, 2 * g:2 * g + 2, 0:nk],
                                             bank(2 + g % 2)[:, 0:2 * nk * P].rearrange("p (h b t) -> p h b t", h=2, b=nk),
                                             ACT.Copy).then_inc(sem("probsT_ready"), 1)
                    act.wait_ge(sem("attn_mm"), 4 * l + (n + 1))
                    nc.scalar.activation(mixT[:, 0:4, n * P:(n + 1) * P],
                                         bank(n % 2).rearrange("p (k t) -> p k t", k=4), ACT.Copy
                                         ).then_inc(sem("attnT_ready"), 1)

                soft(0)
                for n in range(T):
                    if n + 1 < T:
                        soft(n + 1)
                    take_probsT(n)
                post_norm(l, 0)
                pre_norm(l, 1)
                mlp_hi(l, 0)
                mlp_hi(l, 1)
                for u in range(GU_UNITS):
                    for p in range(4 * u + 2, min(4 * u + 6, GU_PIECES + 1)):
                        mlp_hi(l, p)
                    act.wait_ge(sem("gu_mm"), GU_UNITS * l + (u + 1))
                    if u >= 2:
                        act.wait_ge(sem("actT_ready"), GU_UNITS * l + (u - 1))
                    b = 4 * (u % 2)
                    nc.scalar.activation(sig[:, u % 2], psum[:, b:b + 2], ACT.Silu).then_inc(sem("sig_ready"), 1)
                for k in range(KF):
                    if k:
                        mlp_hi(l, GU_PIECES + k)
                    act.wait_ge(sem("actT_ready"), GU_UNITS * l + (k // 2 + 1))
                    nc.scalar.activation(act_pieces[k % 2][:, 0], actT[:, k], ACT.Copy).then_inc(sem("acts_hi"), 1)
                post_norm(l, 1)
                C.leave(LAYERS)


            n = XT_TURN
            for i in range(T):
                act.wait_ge(sem("tr_mm"), 4 * n + i + 1)
                for q in range(2):
                    m = nc.scalar.activation(hT[:, 4 * q:4 * q + 4, i * P:(i + 1) * P],
                                             bank(2 + 2 * (i % 2) + q).rearrange("p (k t) -> p k t", k=4), ACT.Copy)
                    m.then_inc(sem("hT_ready"), 1) if q else C.link(m)
            act.wait_ge(sem("lb_shifted"), 1)
            C.link(nc.scalar.activation(lb, lb, ACT.Exp))
            nc.scalar.activation(one_lb, one_lb, ACT.Exp).then_inc(sem("lb_exp"), 1)
            act.wait_ge(sem("angles2_ready"), 1)
            C.link(nc.scalar.activation(sin2, sin_arg, ACT.Sin))
            nc.scalar.activation(cos2, cos_arg, ACT.Sin).then_inc(sem("rope2_tables"), 1)

            cross_f, cross_kf, cross_kb, cross_qb = (sigs[:, a] for a in range(4))

            def hg_gates(h, b):
                act.wait_ge(sem("kq_ready"), 8 * h - 7) if not isinstance(h, int) or h else None
                for a in range(4):
                    act.wait_ge(sem("hgp_mm"), 5 * h + (a + 1))
                    nc.scalar.activation(sigs[:, a], bank(a), ACT.Sigmoid).then_inc(sem("hg_sig"), 1)
                act.wait_ge(sem("f_ready"), h + 1)
                nc.scalar.activation(lf, sigs[:, 1:3], ACT.Ln).then_inc(sem("lf_ready"), 1)

            def hg_v(h):
                act.wait_ge(sem("hgp_mm"), 5 * h + 5)
                nc.scalar.activation(v_h, bank(4).rearrange("p (i d) -> p i d", i=T), ACT.Copy
                                     ).then_inc(sem("v_ready"), 1)

            def level_exp(h, l):
                act.wait_ge(sem("sub_ready"), 7 * h + (LEVELS - l + 1))
                nc.scalar.activation(lev_e[:, l % 2], lev_e[:, l % 2], ACT.Exp).then_inc(sem("exp_ready"), 1)

            def cross_exp(h):
                C.link(nc.scalar.activation(cross_f, cum_f, ACT.Exp))
                C.link(nc.scalar.activation(cross_kb, cumx_b, ACT.Exp))
                for i in range(T - 1):
                    ts = slice(i * P, (i + 1) * P)
                    edge = slice((i + 1) * P - 1, (i + 1) * P)
                    C.link(nc.scalar.activation(cross_kf[:, ts], cum_f[:, ts], ACT.Exp, scale=-1.0, bias=cum_f[:, edge]))
                    C.link(nc.scalar.activation(cross_qb[:, ts], cumx_b[:, ts], ACT.Exp, scale=-1.0, bias=cum_b[:, edge]))
                nc.scalar.activation(et_b, cum_b[:, P - 1:S:P], ACT.Exp).then_inc(sem("cross_ready"), 1)

            def hg_norm(h):
                act.wait_ge(sem("hgs_mm"), 12 * h + 12)
                C.link(nc.scalar.activation(rs_h, bank(6), ACT.Ln, bias=eps, scale=1.0 / P))
                C.settle()
                nc.scalar.activation(rs_h, rs_h, ACT.Exp, scale=-0.5).then_inc(sem("sum_taken"), 1)

            def hg_head(h, b, last=False):
                level_exp(h, 7)
                cross_exp(h)
                level_exp(h, 6)
                for s in range(T):
                    act.wait_ge(sem("hgs_mm"), 12 * h + (s + 1))
                    nc.scalar.activation(scoresT[:, s], bank(5 + s % 2), ACT.Copy).then_inc(sem("row_ready"), 1)
                for l in range(5, 0, -1):
                    level_exp(h, l)
                if not last:
                    hg_gates(h + 1, 1 - b)
                act.wait_ge(sem("o_mm"), h + 1)
                nc.scalar.activation(osq, bank(7), ACT.Square).then_inc(sem("osq_ready"), 1)
                if not last:
                    hg_v(h + 1)
                hg_norm(h)

            hg_gates(0, 0)
            hg_v(0)
            hg_head(0, 0)
            with act.Fori(0, HG // 2 - 1) as i:
                C.enter(i, "act_hg")
                hg_head(2 * i + 1, 1)
                hg_head(2 * i + 2, 0)
                C.leave(HG // 2 - 1)
            hg_head(HG - 1, 1, last=True)

            def ret_gates(r):
                for a in range(2):
                    act.wait_ge(sem("retp_mm"), 8 * r + 5 + a)
                    m = nc.scalar.activation(rsig[:, a], bank(6 + a), ACT.Sigmoid)
                    m.then_inc(sem("rsig_ready"), 1)

            def ret_v(r):
                for a in range(2):
                    act.wait_ge(sem("retp_mm"), 8 * r + 7 + a)
                    nc.scalar.activation(rv[:, 2 * a:2 * a + 2], bank(4 + a).rearrange("p (i d) -> p i d", i=2), ACT.Copy
                                         ).then_inc(sem("rv_ready"), 1)

            def ret_o(r):
                for a in range(2):
                    act.wait_ge(sem("ro_mm"), 2 * r + a + 1)
                    nc.scalar.activation(o_c[:, a], bank(4 + a), ACT.Copy).then_inc(sem("o_copied"), 1)
                act.wait_ge(sem("o_copied"), 2 * r + 2)
                nc.scalar.activation(o_sq, o_c, ACT.Square).then_inc(sem("rosq_ready"), 1)

            def ret_norm(r):
                act.wait_ge(sem("rsum_mm"), r + 1)
                C.link(nc.scalar.activation(rrs, bank(6), ACT.Ln, bias=eps, scale=1.0 / RDK))
                C.settle()
                nc.scalar.activation(rrs, rrs, ACT.Exp, scale=-0.5).then_inc(sem("rsum_taken"), 1)

            act.wait_ge(sem("hg_out"), HG + 1)
            ret_gates(0)
            ret_v(0)
            for r in range(RH):
                if r:
                    act.wait_ge(sem("ret_out"), r)
                ret_o(r)
                if r + 1 < RH:
                    act.wait_ge(sem("rgate_ready"), r + 1)
                    ret_gates(r + 1)
                    ret_v(r + 1)
                ret_norm(r)

            act.wait_ge(sem("ret_out"), RH)
            for s in range(16):
                act.wait_ge(sem("merge_mm"), s + 1)
                if s >= 2:
                    act.wait_ge(sem("merge_taken"), s - 1)
                nc.scalar.activation(gsig[:, s % 2], bank(2 * (s % 4)), ACT.Sigmoid).then_inc(sem("gsig_ready"), 1)

            def ln_scale(n):
                act.wait_ge(sem("ln_stats"), n + 1)
                C.link(nc.scalar.activation(lnv, mv[:, :, 1], ACT.Ln, bias=ln_eps))
                C.settle()
                nc.scalar.activation(rstd, lnv, ACT.Exp, scale=-0.5).then_inc(sem("ln_rstd"), 1)

            ln_scale(0)

            n = XT_TURN + 1
            for i in range(T):
                act.wait_ge(sem("tr_mm"), 4 * n + i + 1)
                for q in range(2):
                    m = nc.scalar.activation(hT[:, 4 * q:4 * q + 4, i * P:(i + 1) * P],
                                             bank(2 + 2 * (i % 2) + q).rearrange("p (k t) -> p k t", k=4), ACT.Copy)
                    m.then_inc(sem("hT_ready"), 1) if q else C.link(m)
            act.wait_ge(sem("gshift_ready"), 1)
            nc.scalar.activation(gexp, gexp, ACT.Exp).then_inc(sem("gexp_ready"), 1)
            act.wait_ge(sem("eshift_ready"), 1)
            nc.scalar.activation(r4[3], r4[2], ACT.Exp).then_inc(sem("eexp_ready"), 1)

            def hi(j, q):
                if q % 4 == 0:
                    act.wait_ge(sem(f"expert_w{q // 4}"), 16 * j + 16)
                act.wait_ge(sem("piece_started"), 12 * j + (q + 2))
                nc.scalar.activation(pieces[q % PIECES][:, 0], moe_slots[q // 4][:, (q % 4) * PIECE:(q % 4 + 1) * PIECE],
                                     ACT.Copy).then_inc(sem("hi_ready"), 1)

            def take_rows(j, half):
                act.wait_ge(sem("gather_mm"), 2 * j + (half + 1))
                nc.scalar.activation(xrow[:, 512 * half:512 * half + 512], bank(half), ACT.Copy
                                     ).then_inc(sem("xrow_ready"), 1)

            def take_gather(j, half):
                act.wait_ge(sem("gathered_tr"), 2 * j + (half + 1))
                nc.scalar.activation(xsT[:, 0, 4 * half:4 * half + 4], bank(half).rearrange("p (k t) -> p k t", k=4),
                                     ACT.Copy).then_inc(sem("xs_hi"), 1)

            act.wait_ge(sem("logits_mm"), 1)
            for i in range(T):
                nc.scalar.activation(x_hl[0][i], x[:, i], ACT.Copy).then_inc(sem("x_hi"), 1)
            act.wait_ge(sem("table_ready"), 1)
            turns = act.value_load(table_i[0:1, MAX_BLOCKS:MAX_BLOCKS + 1].bitcast(I32), min_val=16, max_val=20)
            act.sem_inc(sem("y_taken"), 1)
            for q in range(3):
                hi(0, q)
            take_rows(0, 0)
            take_rows(0, 1)
            take_gather(0, 0)
            take_gather(0, 1)
            with act.Fori(0, turns) as i:
                for b in range(2):
                    j = 2 * i + b
                    for q in range(3, 8):
                        hi(j, q)
                    act.wait_ge(sem("h_mm"), 2 * j + 1)
                    nc.scalar.activation(gated, bank(2), ACT.Silu).then_inc(sem("gate_silu_ready"), 1)
                    for q in range(8, 11):
                        hi(j, q)
                    act.wait_ge(sem("h_mm"), 2 * j + 2)
                    take_rows(j + 1, 0)
                    act.wait_ge(sem("mgT_mm"), j + 1)
                    nc.scalar.activation(mgT[:, 0], bank(4).rearrange("p (k t) -> p k t", k=4), ACT.Copy
                                         ).then_inc(sem("mgT_hi"), 1)
                    take_rows(j + 1, 1)
                    hi(j, 11)
                    take_gather(j + 1, 0)
                    take_gather(j + 1, 1)
                    for q in range(3):
                        hi(j + 1, q)
                    act.wait_ge(sem("y_mm"), j + 1)
                    act.wait_ge(sem("ysb_free"), j + 1)
                    nc.scalar.activation(ysb[:, b].rearrange("p (a n) -> p a n", a=2), psum[:, 5:7], ACT.Copy
                                         ).then_inc(sem("y_taken"), 1)
            ln_scale(1)

        @block.vector
        def _(dve):
            C = Chain(dve, sem("dve_order"))
            v = nc.vector
            dve.sem_inc(sem("mod_free"), 2)
            dve.sem_inc(sem("proj_free"), 4)
            C.link(v.memset(eps, EPS))
            C.settle()
            dve.wait_ge(sem("x_in"), 16)
            dve.sem_inc(sem("x_ready"), 1)
            dve.wait_ge(sem("const_in"), 80)
            C.link(v.tensor_copy(pos_f, pos_i.bitcast(I32)))
            C.settle()
            ang, r_sin, r_cos = rt

            def reduce_angle(dst, src, tmp, quarter):
                C.link(v.tensor_scalar(tmp, src, 1.0 / TWO_PI, 0.25 * quarter,
                                       ALU.mult, ALU.add))
                C.settle()
                C.link(v.tensor_scalar(tmp, tmp, ROUND, None, ALU.add))
                C.settle()
                C.link(v.tensor_scalar(tmp, tmp, ROUND, None, ALU.subtract))
                C.settle()
                for n, part in enumerate((C1, C2, C3)):
                    C.link(v.scalar_tensor_tensor(out=dst, in0=tmp, scalar=-part, in1=dst if n else src,
                                                  op0=ALU.mult, op1=ALU.add))
                    C.settle()
                if quarter:
                    C.link(v.tensor_scalar(dst, dst, 0.5 * np.pi, None, ALU.add))
                    C.settle()
                C.link(v.tensor_scalar(dst, dst, float(np.float32(-3.1415925)), float(np.float32(3.1415925)),
                                       ALU.max, ALU.min))
                C.settle()

            for i in range(T):
                C.link(v.tensor_scalar(ang[:, i], inv1, pos_f[:, i:i + 1], None, ALU.mult))
            C.settle()
            reduce_angle(r_sin, ang, ang_tmp, 0)
            reduce_angle(r_cos, ang, ang_tmp, 1)
            v.tensor_copy(ang, r_sin).then_inc(sem("angles_ready"), 1)

            def modulation(l, j):
                what, c = (j % 6) // 2, slice(512 * (j % 2), 512 * (j % 2) + 512)
                dve.wait_ge(sem("mod_mm"), MOD_UNITS * l + (j + 1))
                dve.wait_ge(sem(f"aux{j % 2}_in"), aux_total[j % 2] * l + aux_at[j])
                b, g = aux[:, j % 2, 0], aux[:, j % 2, 1]
                if what == 0:
                    m = v.tensor_tensor(shift[:, c], bank(j % 2), b, ALU.add)
                else:
                    dst = scale if what == 1 else (gate_m, gate_f)[j // 6]
                    C.link(v.scalar_tensor_tensor(out=dst[:, c], in0=bank(j % 2), scalar=1.0 if what == 1 else 0.0,
                                                  in1=b, op0=ALU.add, op1=ALU.add))
                    C.settle()
                    m = v.tensor_tensor(dst[:, c], dst[:, c], g, ALU.mult)
                m.then_inc(sem("mod_free"), 1)

            def pre_norm(l, which):
                n = 2 * l + which
                dve.wait_ge(sem("pre_rstd"), n + 1)
                dve.wait_ge(sem("mod_free"), MOD_UNITS * l + (8 + 6 * which))
                for i in range(T):
                    if i >= 2:
                        dve.wait_ge(sem("tr_mm"), 4 * n + (i - 1))
                    C.link(v.scalar_tensor_tensor(out=hrow[:, i % 2], in0=x[:, i], scalar=rstd[:, i:i + 1], in1=scale,
                                                  op0=ALU.mult, op1=ALU.mult))
                    C.settle()
                    v.tensor_tensor(hrow[:, i % 2], hrow[:, i % 2], shift, ALU.add).then_inc(sem("h_row"), 1)
                    if which and i:
                        low_h(l, i - 1)
                if which:
                    low_h(l, T - 1)

            def low_h(l, i):
                dve.wait_ge(sem("hT_hi"), T * l + (i + 1))
                cols = slice(i * P, (i + 1) * P)
                for low, (k0, n) in zip(hT_lo, hT_lo_k):
                    src = psum[:, 2 + 2 * (i % 2) + k0 // 4, (k0 % 4) * P:(k0 % 4 + n) * P]
                    m = v.tensor_tensor(low[:, :, cols], src.rearrange("p (k t) -> p k t", k=n),
                                        hT_hi[:, k0:k0 + n, cols].bitcast(F32), ALU.subtract)
                    m.then_inc(sem("hT_ready"), 1) if k0 == 4 else C.link(m)

            def mlp_lo(l, p):
                dve.wait_ge(sem("mlp_hi"), MLP_PIECES * l + (p + 1))
                v.tensor_tensor(mlp_pieces[p % 2][:, 1], mlp_raw(p)[1], mlp_pieces[p % 2][:, 0].bitcast(F32),
                                ALU.subtract).then_inc(sem("mlp_lo"), 1)

            def post_norm(l, which):
                n = 2 * l + which
                gate = (gate_m, gate_f)[which]
                dve.wait_ge(sem("post_sq"), n + 1)
                v.tensor_tensor(ssq[:, 0:T], ssq[:, 0:T], ssq[:, T:2 * T], ALU.add).then_inc(sem("post_sum"), 1)
                dve.wait_ge(sem("post_rstd"), n + 1)
                for i in range(T):
                    for c in range(2):
                        cs = slice(512 * c, 512 * c + 512)
                        C.link(v.scalar_tensor_tensor(out=tmp_row[:, c], in0=bank(4 * c + i), scalar=rstd[:, i:i + 1],
                                                      in1=gate[:, cs], op0=ALU.mult, op1=ALU.mult))
                    C.settle()
                    m = v.tensor_tensor(x[:, i], x[:, i], tmp_row.rearrange("p a b -> p (a b)"), ALU.add)
                    m.then_inc(sem("x_ready"), 1)
                    dve.wait_ge(sem("x_ready"), 8 * l + (4 * which + i + 2))

            dve.wait_ge(sem("zeros_out"), 16 * (MAX_BLOCKS - EXPERTS))
            with dve.Fori(0, LAYERS) as l:
                C.enter(l, "dve_layer")
                for j in range(6):
                    modulation(l, j)
                pre_norm(l, 0)
                dve.wait_ge(sem("layer_in"), 64 * l + 64)
                for c in range(IN_UNITS):
                    for i in range(T):
                        dve.wait_ge(sem("proj_mm"), 16 * l + (4 * c + i + 1))
                        cs = slice(c * IN_COLS, (c + 1) * IN_COLS)
                        v.tensor_tensor(proj[:, i, cs], psum[:, 2 + i, 0:IN_COLS], b_in[:, cs], ALU.add
                                        ).then_inc(sem("proj_free"), 1)
                dve.wait_ge(sem("proj_free"), 16 * l + 20)
                dve.wait_ge(sem("rope_tables"), 1)
                for i in range(T):
                    qk = proj[:, i, 0:640].rearrange("p (h d) -> p h d", d=HD)
                    t1, t2 = qk[:, :, 0:ROT_HALF], qk[:, :, ROT_HALF:2 * ROT_HALF]
                    cs_, sn_ = (a[:, i:i + 1].to_broadcast([P, 10, ROT_HALF]) for a in (cos1, sin1))
                    r = [rope_tile(a, i) for a in range(4)]
                    C.link(v.tensor_tensor(r[0], t1, cs_, ALU.mult))
                    C.link(v.tensor_tensor(r[1], t2, sn_, ALU.mult))
                    C.link(v.tensor_tensor(r[2], t2, cs_, ALU.mult))
                    C.link(v.tensor_tensor(r[3], t1, sn_, ALU.mult))
                C.settle()
                for i in range(T):
                    qk = proj[:, i, 0:640].rearrange("p (h d) -> p h d", d=HD)
                    t1, t2 = qk[:, :, 0:ROT_HALF], qk[:, :, ROT_HALF:2 * ROT_HALF]
                    r = [rope_tile(a, i) for a in range(4)]
                    C.link(v.tensor_tensor(t1, r[0], r[1], ALU.subtract))
                    C.link(v.tensor_tensor(t2, r[2], r[3], ALU.add))
                C.settle()
                for i in range(T):
                    for b in range(2):
                        k = proj[:, i, 512:640].rearrange("p (g d) -> p g d", g=KVH)
                        m = v.tensor_copy(kdup[:, i, :, b], k)
                        m.then_inc(sem("rope_done"), 1) if i == T - 1 and b else C.link(m)
                for j in range(6, 12):
                    modulation(l, j)
                for g in range(POOL_G):
                    dve.wait_ge(sem("pool_mm"), 4 * l + (g + 1))
                    v.tensor_copy(pooled[:, g % 2], bank(2 + g % 2)).then_inc(sem("pooled_ready"), 1)

                def mask(n):
                    nk = 2 * P if n else P
                    b = n % 2
                    win = window[:, 0:2 * P] if n else window[:, P:2 * P]
                    for j in range(4):
                        dve.wait_ge(sem("score_mm"), 16 * l + (4 * n + j + 1))
                        v.scalar_tensor_tensor(
                            out=probs[:, b, 4 * (j // 2) + j % 2:4 * (j // 2) + 4:2, 0:nk],
                            in0=psum[:, 4 + j, 0:2 * nk].rearrange("p (a k) -> p a k", a=2), scalar=HD ** -0.5,
                            in1=win.rearrange("p (a k) -> p a k", a=1).to_broadcast([P, 2, nk]),
                            op0=ALU.mult, op1=ALU.add).then_inc(sem("score_free"), 1)
                    dve.wait_ge(sem("score_free"), 16 * l + (4 * n + 4))
                    C.link(v.tensor_reduce(mx[:, b], probs[:, b, :, 0:nk], AXX, ALU.max))
                    C.settle()
                    C.link(v.tensor_tensor(mx[:, b], mx[:, b], sink, ALU.max))
                    C.settle()
                    C.link(v.tensor_tensor(den[:, b], sink, mx[:, b], ALU.subtract))
                    v.tensor_scalar(negm[:, b], mx[:, b], -1.0, None, ALU.mult).then_inc(sem("max_ready"), 1)

                def normalise(n):
                    nk = 2 * P if n else P
                    b = n % 2
                    dve.wait_ge(sem("exp_done"), 4 * l + (n + 1))
                    C.link(v.tensor_tensor(den[:, b], rsum[:, b], esink[:, b], ALU.add))
                    C.settle()
                    C.link(v.reciprocal(den[:, b], den[:, b]))
                    C.settle()
                    d3 = den[:, b].rearrange("p (h a) -> p h a", a=1).to_broadcast([P, HEADS, nk])
                    v.tensor_tensor(probs[:, b, :, 0:nk], probs[:, b, :, 0:nk], d3, ALU.mult
                                    ).then_inc(sem("probs_ready"), 1)

                mask(0)
                for n in range(T):
                    if n + 1 < T:
                        mask(n + 1)
                    normalise(n)
                post_norm(l, 0)
                pre_norm(l, 1)
                mlp_lo(l, 0)
                mlp_lo(l, 1)
                for u in range(GU_UNITS):
                    for p in range(4 * u + 2, min(4 * u + 6, GU_PIECES + 1)):
                        mlp_lo(l, p)
                    b = 4 * (u % 2)
                    dve.wait_ge(sem("sig_ready"), GU_UNITS * l + (u + 1))
                    v.tensor_tensor(actT[:, 2 * u:2 * u + 2], sig[:, u % 2], psum[:, b + 2:b + 4], ALU.mult
                                    ).then_inc(sem("actT_ready"), 1)
                for k in range(KF):
                    if k:
                        mlp_lo(l, GU_PIECES + k)
                    dve.wait_ge(sem("acts_hi"), KF * l + (k + 1))
                    v.tensor_tensor(act_pieces[k % 2][:, 1], actT[:, k], act_pieces[k % 2][:, 0].bitcast(F32),
                                    ALU.subtract).then_inc(sem("acts_lo"), 1)
                post_norm(l, 1)
                C.leave(LAYERS)

            dve.wait_ge(sem("const2_in"), 128)
            v.memset(ones, 1.0).then_inc(sem("ones_ready"), 1)
            C.settle()
            C.link(v.tensor_tensor(mx[:, 0], lb, one_lb, ALU.max))
            C.settle()
            C.link(v.tensor_tensor(lb, lb, mx[:, 0], ALU.subtract))
            v.tensor_tensor(one_lb, one_lb, mx[:, 0], ALU.subtract).then_inc(sem("lb_shifted"), 1)
            C.link(v.tensor_copy(pos2_f, pos2_i.bitcast(I32)))
            C.settle()
            C.link(v.tensor_scalar(ang2, pos2_f, inv2, None, ALU.mult))
            C.settle()
            reduce_angle(sin_arg, ang2, ang2_tmp, 0)
            reduce_angle(cos_arg, ang2, ang2_tmp, 1)
            v.tensor_copy(ang2_tmp, cos_arg).then_inc(sem("angles2_ready"), 1)
            dve.wait_ge(sem("lb_exp"), 1)
            C.link(v.tensor_tensor(mx[:, 0], lb, one_lb, ALU.add))
            C.settle()
            C.link(v.reciprocal(mx[:, 0], mx[:, 0]))
            C.settle()
            C.link(v.tensor_tensor(lb, one_lb, mx[:, 0], ALU.mult))
            C.settle()
            C.link(v.tensor_scalar(one_lb, lb, -1.0, 1.0, ALU.mult, ALU.add))
            C.settle()
            C.link(v.tensor_scalar(lb, lb, 2.0 ** -60, None, ALU.max))
            dve.wait_ge(sem("rope2_tables"), 1)
            dve.sem_inc(sem("hg_out"), 1)
            dve.sem_inc(sem("sum_taken"), 1)
            C.settle()

            cross_f, cross_kf, cross_kb, cross_qb = (sigs[:, a] for a in range(4))

            def col(a, h):
                return a[:, bass.ds(h, 1)] if not isinstance(h, int) else a[:, h:h + 1]

            def hg_gates(h, b):
                dve.wait_ge(sem("hg_sig"), 4 * h + 1)
                v.tensor_tensor(q_h, sigs[:, 0], bank(0), ALU.mult).then_inc(sem("hgp_taken"), 1)
                dve.wait_ge(sem("hg_sig"), 4 * h + 3)
                v.tensor_scalar(sigs[:, 1:3], sigs[:, 1:3], col(one_lb, h), col(lb, h), ALU.mult, ALU.add
                                ).then_inc(sem("f_ready"), 1)
                dve.wait_ge(sem("hg_sig"), 4 * h + 4)
                v.tensor_tensor(gate_h[:, b], sigs[:, 3], bank(3), ALU.mult).then_inc(sem("hgp_taken"), 1)
                dve.wait_ge(sem("f_ready"), h + 1)
                C.link(v.tensor_scalar(k_h, sigs[:, 1:3], -1.0, 1.0, ALU.mult, ALU.add))
                dve.wait_ge(sem("lf_ready"), h + 1)
                C.link(v.tensor_tensor_scan(cum_f, restart, lf[:, 0], 0.0, ALU.mult, ALU.add))
                C.link(v.tensor_tensor_scan(cum_b, restart, lf[:, 1], 0.0, ALU.mult, ALU.add))
                C.settle()
                C.link(v.tensor_tensor(cumx_b, cum_b, lf[:, 1], ALU.subtract))
                C.settle()

            def halves(a, l):
                return a.rearrange("p (n h b) -> p n h b", h=2, b=2 ** (l - 1))

            def level_sub(h, l):
                n, hb = S >> l, 2 ** (l - 1)
                if l <= LEVELS - 2:
                    dve.wait_ge(sem("kq_ready"), 8 * h + (LEVELS - 1 - l))
                cf, cx = halves(cum_f, l), halves(cumx_b, l)
                eq, ek = halves(lev_e[:, l % 2, 0], l), halves(lev_e[:, l % 2, 1], l)
                ref_f = cf[:, :, 0, hb - 1:hb].to_broadcast([P, n, hb])
                ref_b = cx[:, :, 1, 0:1].to_broadcast([P, n, hb])
                C.link(v.tensor_tensor(eq[:, :, 1], cf[:, :, 1], ref_f, ALU.subtract))
                C.link(v.tensor_tensor(eq[:, :, 0], ref_b, cx[:, :, 0], ALU.subtract))
                C.link(v.tensor_tensor(ek[:, :, 0], ref_f, cf[:, :, 0], ALU.subtract))
                v.tensor_tensor(ek[:, :, 1], cx[:, :, 1], ref_b, ALU.subtract).then_inc(sem("sub_ready"), 1)

            def level_mult(h, l):
                dve.wait_ge(sem("exp_ready"), 7 * h + (LEVELS - l + 1))
                if l == 5:
                    dve.wait_ge(sem("hgs_mm"), 12 * h + 4)
                elif l < 5:
                    dve.wait_ge(sem("hgs_mm"), 12 * h + (9 - l))
                e, o = lev_e[:, l % 2], lev_qk[:, l % 2]
                C.link(v.tensor_tensor(o[:, 0], q_h, e[:, 0], ALU.mult))
                C.link(v.tensor_tensor(halves(o[:, 1], l)[:, :, 0], halves(k_h[:, 0], l)[:, :, 0],
                                       halves(e[:, 1], l)[:, :, 0], ALU.mult))
                m = v.tensor_tensor(halves(o[:, 1], l)[:, :, 1], halves(k_h[:, 1], l)[:, :, 1],
                                    halves(e[:, 1], l)[:, :, 1], ALU.mult)
                C.link(m) if l == LEVELS else m.then_inc(sem("kq_ready"), 1)

            def tiles(a):
                return a.rearrange("p (i t) -> p i t", i=T)

            def cross_mult(h):
                dve.wait_ge(sem("cross_ready"), h + 1)
                q, kf, kb = tiles(q_h), tiles(k_h[:, 0]), tiles(k_h[:, 1])
                ef, ekf, ekb, eqb = tiles(cross_f), tiles(cross_kf), tiles(cross_kb), tiles(cross_qb)
                C.link(v.tensor_tensor(xf_q[:, 0:3:2], q[:, 1:3], ef[:, 1:3], ALU.mult))
                C.link(v.tensor_tensor(xf_q[:, 1], q[:, 3], ef[:, 3], ALU.mult))
                C.link(v.tensor_tensor(xf_k[:, 0:2], kf[:, 0:3:2], ekf[:, 0:3:2], ALU.mult))
                C.link(v.tensor_tensor(xf_k[:, 3], kf[:, 1], ekf[:, 1], ALU.mult))
                C.link(v.tensor_tensor(xb_q[:, 0:2], q[:, 0:3:2], eqb[:, 0:3:2], ALU.mult))
                C.link(v.tensor_tensor(xb_q[:, 3], q[:, 1], eqb[:, 1], ALU.mult))
                C.link(v.tensor_tensor(xb_k[:, 0:2], kb[:, 1:4:2], ekb[:, 1:4:2], ALU.mult))
                C.link(v.tensor_tensor(xb_k[:, 2], kb[:, 2], ekb[:, 2], ALU.mult))
                C.settle()
                C.link(v.tensor_scalar(xf_q[:, 3], xf_q[:, 1], ef[:, 2, P - 1:P], None, ALU.mult))
                C.link(v.tensor_scalar(xf_k[:, 2], xf_k[:, 0], ef[:, 1, P - 1:P], None, ALU.mult))
                C.link(v.tensor_scalar(xb_q[:, 2], xb_q[:, 0], et_b[:, 1:2], None, ALU.mult))
                v.tensor_scalar(xb_k[:, 3], xb_k[:, 1], et_b[:, 2:3], None, ALU.mult).then_inc(sem("kq_ready"), 1)

            def level_take(h, l):
                dve.wait_ge(sem("hgs_mm"), 12 * h + (11 - l))
                dve.wait_ge(sem("row_ready"), 4 * h + 4)
                if l < LEVELS - 1:
                    dve.wait_ge(sem("level_taken"), 7 * h + (LEVELS - 1 - l))
                m = masks[:, l:l + 1].bitcast(I32).to_broadcast([P, T, P])
                dve.sem_inc(sem("take_order"), 1)
                v.copy_predicated(diag, m, tiles(psum[:, 5 + (LEVELS - 1 - l) % 2])).then_inc(sem("level_taken"), 1)

            def hg_out(h, b):
                dve.wait_ge(sem("sum_taken"), h + 2)
                C.link(v.tensor_tensor(rs_h, rs_h, bank(7), ALU.mult))
                C.settle()
                dst = o_hgT[:, bass.ds(h, 1)] if not isinstance(h, int) else o_hgT[:, h:h + 1]
                v.scalar_tensor_tensor(out=dst.rearrange("p a s -> p (a s)"), in0=rs_h, scalar=col(hg_g, h),
                                       in1=gate_h[:, b], op0=ALU.mult, op1=ALU.mult).then_inc(sem("hg_out"), 1)

            def hg_head(h, b, last=False):
                level_sub(h, 7)
                level_sub(h, 6)
                level_mult(h, 7)
                cross_mult(h)
                level_sub(h, 5)
                level_mult(h, 6)
                for l in range(5, 0, -1):
                    if l > 1:
                        level_sub(h, l - 1)
                    level_mult(h, l)
                    level_take(h, l + 1)
                dve.wait_ge(sem("hgs_mm"), 12 * h + 9)
                v.tensor_tensor(lev_qk[:, 0, 1], k_h[:, 0], k_h[:, 1], ALU.add).then_inc(sem("kq_ready"), 1)
                level_take(h, 1)
                level_take(h, 0)
                if not last:
                    hg_gates(h + 1, 1 - b)
                hg_out(h, b)

            hg_gates(0, 0)
            hg_head(0, 0)
            with dve.Fori(0, HG // 2 - 1) as i:
                C.enter(i, "dve_hg")
                hg_head(2 * i + 1, 1)
                hg_head(2 * i + 2, 0)
                C.leave(HG // 2 - 1)
            hg_head(HG - 1, 1, last=True)

            both = lambda a: a.rearrange("p (a s) -> p a s", a=1).to_broadcast([P, 2, S])

            def ret_rope(r):
                dve.wait_ge(sem("hg_out"), HG + 1)
                if r:
                    dve.wait_ge(sem("rs_mm"), 4 * r)
                for a, dst in ((0, rq), (1, rk)):
                    dve.wait_ge(sem("retp_mm"), 8 * r + 2 * a + 2)
                    eo = psum[:, 2 * a:2 * a + 2]
                    C.link(v.tensor_tensor(rope_a, eo, both(cos2), ALU.mult))
                    C.link(v.tensor_tensor(rope_b, eo, both(sin2), ALU.mult))
                    C.settle()
                    C.link(v.tensor_tensor(dst[:, 0], rope_a[:, 0], rope_b[:, 1], ALU.subtract))
                    v.tensor_tensor(dst[:, 1], rope_b[:, 0], rope_a[:, 1], ALU.add).then_inc(sem("rope2_done"), 1)
                    dve.wait_ge(sem("rope2_done"), 2 * r + a + 1)

            def ret_gate(r):
                for a in range(2):
                    dve.wait_ge(sem("rsig_ready"), 2 * r + a + 1)
                    m = v.tensor_tensor(rgate[:, r % 2, a], rsig[:, a], bank(6 + a), ALU.mult)
                    m.then_inc(sem("rgate_ready"), 1) if a else C.link(m)

            def ret_decay(r):
                dve.wait_ge(sem(f"strip{r % 2}_in"), 16 * (r // 2 + 1))
                for s in range(T):
                    dve.wait_ge(sem("rs_mm"), 4 * r + s + 1)
                    c = (3 - s) * P
                    v.tensor_tensor(rscT[:, s], bank(s), strip[:, r % 2, c:c + S], ALU.mult
                                    ).then_inc(sem("rsc_ready"), 1)

            def ret_out(r):
                dve.wait_ge(sem("rsum_taken"), r + 1)
                C.link(v.tensor_tensor(o_c, o_c, both(rrs), ALU.mult))
                C.settle()
                for a in range(2):
                    m = v.scalar_tensor_tensor(out=o_retT[:, 2 * r + a], in0=o_c[:, a],
                                               scalar=ret_g[:, 2 * r + a:2 * r + a + 1], in1=rgate[:, r % 2, a],
                                               op0=ALU.mult, op1=ALU.mult)
                    m.then_inc(sem("ret_out"), 1) if a else C.link(m)

            ret_rope(0)
            ret_gate(0)
            for r in range(RH):
                ret_decay(r)
                if r + 1 < RH:
                    ret_rope(r + 1)
                    ret_gate(r + 1)
                ret_out(r)

            dve.wait_ge(sem("ret_out"), RH)
            for s in range(16):
                dve.wait_ge(sem("gsig_ready"), s + 1)
                dst = mergedT[:, 4 * (s // 8) + s % 4]
                if (s // 4) % 2 == 0:
                    v.tensor_tensor(dst, gsig[:, s % 2], bank(2 * (s % 4) + 1), ALU.mult).then_inc(sem("merge_taken"), 1)
                else:
                    dve.wait_ge(sem("merge_taken"), s)
                    C.link(v.tensor_tensor(ytmp[:, s % 2], gsig[:, s % 2], bank(2 * (s % 4) + 1), ALU.mult))
                    C.settle()
                    v.tensor_tensor(dst, dst, ytmp[:, s % 2], ALU.add).then_inc(sem("merge_taken"), 1)

            def layer_norm(n, done, out_sem):
                for i in range(T):
                    for c in range(2):
                        C.link(v.bn_stats(bn[:, i, c], x[:, i, 512 * c:512 * c + 512]))
                C.settle()
                for i in range(T):
                    m = v.bn_aggr(mv[:, i], bn[:, i])
                    m.then_inc(sem("ln_stats"), 1) if i == T - 1 else C.link(m)
                dve.wait_ge(sem("ln_rstd"), n + 1)
                dve.wait_ge(sem(f"ln{n}_in"), 32)
                for i in range(T):
                    C.link(v.tensor_scalar(x[:, i], x[:, i], mv[:, i, 0:1], rstd[:, i:i + 1], ALU.subtract, ALU.mult))
                C.settle()
                for i in range(T):
                    C.link(v.tensor_tensor(x[:, i], x[:, i], ln_g[:, n], ALU.mult))
                C.settle()
                for i in range(T):
                    v.tensor_tensor(x[:, i], x[:, i], ln_b[:, n], ALU.add).then_inc(out_sem, 1)

            C.link(v.memset(ln_eps, LN_EPS))
            dve.wait_ge(sem("mix2_mm"), 16)
            for i in range(T):
                C.link(v.scalar_tensor_tensor(out=x[:, i], in0=x[:, i], scalar=ALPHA,
                                              in1=psum[:, 2 * i:2 * i + 2].rearrange("p a b -> p (a b)"),
                                              op0=ALU.mult, op1=ALU.add))
            C.settle()
            layer_norm(0, None, sem("x1_ready"))

            def bc(a, *shape):
                return a.to_broadcast([P, *shape])

            def last(a, n):
                return a.rearrange("p (t a) -> p t a", a=1).to_broadcast([P, T, n])

            def over_tiles(a, n):
                return a.rearrange("p (a n) -> p a n", a=1).to_broadcast([P, T, n])

            def first_max(onehot, vals, vmax, n, tmp, least):
                C.link(v.tensor_reduce(vmax, vals, AXX, ALU.max))
                C.settle()
                C.link(v.tensor_tensor(onehot, vals, last(vmax, n), ALU.is_equal))
                C.settle()
                C.link(v.scalar_tensor_tensor(out=tmp, in0=onehot, scalar=-64.0, in1=over_tiles(iota[:, 0:n], n),
                                              op0=ALU.mult, op1=ALU.add))
                C.settle()
                C.link(v.tensor_reduce(least, tmp, AXX, ALU.min))
                C.settle()
                C.link(v.tensor_tensor(onehot, tmp, last(least, n), ALU.is_equal))
                C.settle()

            dve.wait_ge(sem("route_in"), 96)
            dve.wait_ge(sem("logits_mm"), 1)
            C.link(v.tensor_tensor(logits, psum[:, 0, 0:T * NL].rearrange("p (t n) -> p t n", t=T), over_tiles(bias_r, NL), ALU.add))
            C.settle()
            lgr, ler = logits[:, :, 0:GROUPS], logits[:, :, GROUPS:NL].rearrange("p t (g e) -> p t g e", g=GROUPS)
            gmax, least, e_diff, e_exp, e1, e2 = r4
            first_max(oh_g, lgr, gmax, GROUPS, gexp, least)
            v.tensor_tensor(gexp, lgr, last(gmax, GROUPS), ALU.subtract).then_inc(sem("gshift_ready"), 1)
            for i in range(T):
                og = oh_g[:, i].rearrange("p (g a) -> p g a", a=1).to_broadcast([P, GROUPS, PER_GROUP])
                C.link(v.tensor_tensor(picked[:, i], ler[:, i], og, ALU.mult))
            C.settle()
            for i in range(T):
                C.link(v.tensor_reduce(es[:, i], picked[:, i].rearrange("p g e -> p e g"), AXX, ALU.add))
            C.settle()
            first_max(oh_e[:, 0], es, e1, PER_GROUP, t8, least)
            C.link(v.scalar_tensor_tensor(out=es, in0=oh_e[:, 0], scalar=NEG, in1=es, op0=ALU.mult, op1=ALU.add))
            C.settle()
            first_max(oh_e[:, 1], es, e2, PER_GROUP, t8, least)
            v.tensor_tensor(e_diff, e2, e1, ALU.subtract).then_inc(sem("eshift_ready"), 1)
            for k in range(2):
                for i in range(T):
                    og = oh_g[:, i].rearrange("p (g a) -> p g a", a=1).to_broadcast([P, GROUPS, PER_GROUP])
                    oe = oh_e[:, k, i].rearrange("p (a e) -> p a e", a=1).to_broadcast([P, GROUPS, PER_GROUP])
                    C.link(v.tensor_tensor(m_k[:, k, i].rearrange("p (g e) -> p g e", g=GROUPS), og, oe, ALU.mult))
            C.settle()
            v.tensor_tensor(m_sum, m_k[:, 0], m_k[:, 1], ALU.add).then_inc(sem("onehots_ready"), 1)
            dve.wait_ge(sem("gexp_ready"), 1)
            C.link(v.tensor_reduce(gmax, gexp, AXX, ALU.add))
            dve.wait_ge(sem("eexp_ready"), 1)
            C.link(v.tensor_scalar(e1, e_exp, 1.0, None, ALU.add))
            C.settle()
            C.link(v.tensor_tensor(e1, e1, gmax, ALU.mult))
            C.settle()
            C.link(v.reciprocal(wts[:, 0], e1))
            C.settle()
            C.link(v.tensor_tensor(wts[:, 1], wts[:, 0], e_exp, ALU.mult))
            C.link(v.tensor_scalar(base_e, iota[:, 0:EXPERTS], float(P), None, ALU.mult))
            dve.wait_ge(sem("ranks_mm"), 1)
            C.link(v.tensor_copy(rank, psum[:, 1, 0:T * EXPERTS].rearrange("p (t e) -> p t e", t=T)))
            C.link(v.tensor_copy(cnt, psum[:, 1, T * EXPERTS:(T + 1) * EXPERTS]))
            C.settle()
            C.link(v.tensor_scalar(extra, cnt, float(P), None, ALU.is_gt))
            for m in (2, 3):
                C.settle()
                C.link(v.scalar_tensor_tensor(out=extra, in0=cnt, scalar=float(m * P), in1=extra,
                                              op0=ALU.is_gt, op1=ALU.add))
            C.settle()
            C.link(v.tensor_tensor_scan(ends, ones[:, 0:EXPERTS], extra, 0.0, ALU.mult, ALU.add))
            C.settle()
            C.link(v.tensor_tensor(over_d, ends, extra, ALU.subtract))
            C.settle()
            C.link(v.tensor_scalar(over_d, over_d, float(EXPERTS - 1), float(P), ALU.add, ALU.mult))
            C.settle()
            C.link(v.tensor_tensor(over_d, over_d, base_e, ALU.subtract))
            C.link(v.tensor_scalar(ge, rank, float(P), None, ALU.is_ge))
            C.settle()
            C.link(v.tensor_tensor(ge, ge, over_tiles(over_d, EXPERTS), ALU.mult))
            C.link(v.tensor_tensor(rank, rank, over_tiles(base_e, EXPERTS), ALU.add))
            C.settle()
            C.link(v.tensor_tensor(rank, rank, ge, ALU.add))
            C.settle()
            for k in range(2):
                C.link(v.tensor_tensor(m_k[:, k], m_k[:, k], rank, ALU.mult))
            C.settle()
            for k in range(2):
                C.link(v.tensor_reduce(slot_f[:, k], m_k[:, k], AXX, ALU.add))
            C.settle()
            C.link(v.tensor_copy(slot_i.bitcast(I32), slot_f))
            C.link(v.tensor_copy(table_f[:, 0:EXPERTS], iota[:, 0:EXPERTS]))
            C.link(v.tensor_tensor(cmp8, bc(ends.rearrange("p (a e) -> p a e", a=1), 8, EXPERTS),
                                   bc(iota[:, 0:8].rearrange("p (b a) -> p b a", a=1), 8, EXPERTS), ALU.is_le))
            C.settle()
            C.link(v.tensor_reduce(table_f[:, EXPERTS:MAX_BLOCKS], cmp8, AXX, ALU.add))
            C.link(v.tensor_scalar(table_f[:, MAX_BLOCKS:], ends[:, EXPERTS - 1:EXPERTS], 0.0, float(EXPERTS // 2),
                                   ALU.is_gt, ALU.add))
            for m in (2, 4, 6):
                C.settle()
                C.link(v.scalar_tensor_tensor(out=table_f[:, MAX_BLOCKS:], in0=ends[:, EXPERTS - 1:EXPERTS], scalar=float(m),
                                              in1=table_f[:, MAX_BLOCKS:], op0=ALU.is_gt, op1=ALU.add))
            C.settle()
            C.link(v.tensor_scalar(table_f[:, 0:MAX_BLOCKS], table_f[:, 0:MAX_BLOCKS], float(EXPERTS - 1), None, ALU.min))
            C.settle()
            v.tensor_copy(table_i.bitcast(I32), table_f).then_inc(sem("table_ready"), 1)

            def select(j):
                for i in range(T):
                    M.link(v.tensor_scalar(sel_tmp[:, i], iota_b, slot_f[:, 0, i:i + 1], None, ALU.is_equal))
                M.settle()
                if not (isinstance(j, int) and j == 0):
                    dve.wait_ge(sem("gather_mm"), 2 * j)
                for i in range(T):
                    m = v.scalar_tensor_tensor(out=sel[:, i], in0=iota_b, scalar=slot_f[:, 1, i:i + 1],
                                               in1=sel_tmp[:, i], op0=ALU.is_equal, op1=ALU.add)
                    m.then_inc(sem("sel_ready"), 1) if i == T - 1 else M.link(m)
                dve.wait_ge(sem("sel_ready"), j + 1)
                M.link(v.tensor_scalar(iota_b, iota_b, float(P), None, ALU.add))
                M.settle()

            def lo(j, q):
                dve.wait_ge(sem("hi_ready"), 12 * j + (q + 1))
                v.tensor_tensor(pieces[q % PIECES][:, 1], moe_slots[q // 4][:, (q % 4) * PIECE:(q % 4 + 1) * PIECE],
                                pieces[q % PIECES][:, 0].bitcast(F32), ALU.subtract).then_inc(sem("lo_ready"), 1)

            def take_gather(j, half):
                dve.wait_ge(sem("xs_hi"), 2 * j + (half + 1))
                part = slice(4 * half, 4 * half + 4)
                v.tensor_tensor(xsT[:, 1, part], bank(half).rearrange("p (k t) -> p k t", k=4),
                                xsT[:, 0, part].bitcast(F32), ALU.subtract).then_inc(sem("xs_ready"), 1)

            M = Chain(dve, sem("moe_order"))
            C.link(v.tensor_copy(iota_b, iota))
            C.settle()
            for i in range(T):
                dve.wait_ge(sem("x_hi"), i + 1)
                v.tensor_tensor(x_hl[1][i], x[:, i], x_hl[0][i].bitcast(F32), ALU.subtract).then_inc(sem("x_split"), 1)
            dve.wait_ge(sem("table_ready"), 1)
            turns = dve.value_load(table_i[0:1, MAX_BLOCKS:MAX_BLOCKS + 1].bitcast(I32), min_val=16, max_val=20)
            select(0)
            take_gather(0, 0)
            take_gather(0, 1)
            select(1)
            with dve.Fori(0, turns) as i:
                M.enter(i, "dve_moe")
                for b in range(2):
                    j = 2 * i + b
                    for q in range(8):
                        lo(j, q)
                    dve.wait_ge(sem("gate_silu_ready"), j + 1)
                    dve.wait_ge(sem("h_mm"), 2 * j + 2)
                    v.tensor_tensor(mg, gated, bank(3), ALU.mult).then_inc(sem("mg_ready"), 1)
                    for q in range(8, 11):
                        lo(j, q)
                    dve.wait_ge(sem("mgT_hi"), j + 1)
                    v.tensor_tensor(mgT[:, 1], bank(4).rearrange("p (k t) -> p k t", k=4), mgT[:, 0].bitcast(F32),
                                    ALU.subtract).then_inc(sem("mgT_ready"), 1)
                    select(j + 2)
                    lo(j, 11)
                    take_gather(j + 1, 0)
                    take_gather(j + 1, 1)
                M.leave(0)
            dve.sem_inc(sem("expert_w0"), 16)
            for i in range(T):
                dve.wait_ge(sem(f"rows{i}_in"), 32)
                C.link(v.tensor_scalar(yg[0][i], yg[0][i], wts[:, 0, i:i + 1], None, ALU.mult))
                C.settle()
                C.link(v.scalar_tensor_tensor(out=yg[0][i], in0=yg[1][i], scalar=wts[:, 1, i:i + 1], in1=yg[0][i],
                                              op0=ALU.mult, op1=ALU.add))
                C.settle()
                C.link(v.scalar_tensor_tensor(out=x[:, i], in0=x[:, i], scalar=ALPHA, in1=yg[0][i],
                                              op0=ALU.mult, op1=ALU.add))
            C.settle()
            layer_norm(1, None, sem("x2_ready"))


def kernel(**inputs):
    import concourse.bacc as _bacc
    from concourse.bass_utils import run_bass_kernel_spmd as _run

    nc = _bacc.Bacc("TRN2", target_bir_lowering=False, num_devices=1)
    arrays, A, K = {}, {}, {}
    for name, a in inputs.items():
        a = np.ascontiguousarray(a)
        arrays["in_" + name] = a
        A[name] = nc.dram_tensor("in_" + name, a.shape, mybir.dt.from_np(a.dtype), kind="ExternalInput").ap()
    for name, a in shape_constants().items():
        arrays["const_" + name] = a
        K[name] = nc.dram_tensor("const_" + name, a.shape, F32, kind="ExternalInput").ap()
    out = nc.dram_tensor("out", (1, S, D), F32, kind="ExternalOutput").ap()
    build(nc, A, K, out)
    r = _run(nc, [arrays], core_ids=[0])
    return r.results[0]["out"]
```
